# Optimizing a Trainium2 kernel written in Bass

```python
import math
import jax, jax.numpy as jnp
from jax import lax
import numpy as np

D_MODEL = 1024
BATCH = 1
SEQ = 256
DEPTH = 2
DEC_BATCH = 8
DEC_SEQ = 8
PAST_LEN = 2048
PAGE_SIZE = 128

D_MIX = 2 * D_MODEL
HG_WIDTH = D_MIX // 2
HG_KDIM = 128
HG_HEADS = HG_WIDTH // HG_KDIM
HG_VDIM = HG_WIDTH // HG_HEADS
HG_CHUNK = 32
LB_FLOOR = 1e-30
M_DINNER = D_MIX - HG_WIDTH
M_HEADDIM = 64
M_HEADS = M_DINNER // M_HEADDIM
M_DSTATE = 128
M_GROUPS = 2
CONV_W = 4
CONV_DIM = M_DINNER + 2 * M_GROUPS * M_DSTATE
M_CHUNK = 64
DT_MIN = 0.001
DT_MAX = 0.1
D_FF = 2816
EPS = 1e-6
PROJ_SIZES = (HG_HEADS * HG_KDIM, HG_HEADS * HG_KDIM, HG_HEADS * HG_VDIM, HG_HEADS * HG_VDIM, M_DINNER, CONV_DIM, M_HEADS)
D_PROJ = sum(PROJ_SIZES)
PROJ_SPLITS = tuple(int(s) for s in np.cumsum(PROJ_SIZES)[:-1])

kernel_name = "hymba_hgrn2_mamba2_macaron_step"

def _rmsnorm(x, w):
    xf = x.astype(jnp.float32)
    y = xf * lax.rsqrt(jnp.mean(xf * xf, axis=-1, keepdims=True) + EPS)
    return (y * w.astype(jnp.float32)).astype(x.dtype)

def _swiglu(x, wg, wu, wd):
    return (jax.nn.silu(x @ wg) * (x @ wu)) @ wd

def _chunk_len(L, c):
    c = min(c, L)
    return c if L % c == 0 else L

def _gla_chunked(q, k, v, g, s0):
    Bsz, L, H, K = q.shape
    V = v.shape[-1]
    c = _chunk_len(L, HG_CHUNK)
    n = L // c

    def to_chunks(a):
        return a.reshape(Bsz, n, c, H, a.shape[-1]).transpose(1, 0, 3, 2, 4)

    tril = jnp.tril(jnp.ones((c, c), dtype=bool))[:, :, None]

    def step(S, inp):
        qc, kc, vc, gc = inp
        b = jnp.cumsum(gc, axis=2)
        o_inter = jnp.einsum('bhtk,bhkv->bhtv', qc * jnp.exp(b), S)
        diff = b[:, :, :, None, :] - b[:, :, None, :, :]
        decay = jnp.where(tril, jnp.exp(jnp.where(tril, diff, 0.0)), 0.0)
        A = jnp.einsum('bhtk,bhsk,bhtsk->bhts', qc, kc, decay)
        o_intra = jnp.einsum('bhts,bhsv->bhtv', A, vc)
        b_last = b[:, :, -1:, :]
        S_new = jnp.exp(b_last[:, :, 0, :])[..., None] * S + jnp.einsum('bhsk,bhsv->bhkv', kc * jnp.exp(b_last - b), vc)
        return S_new, o_inter + o_intra

    s_fin, o = lax.scan(step, s0, (to_chunks(q), to_chunks(k), to_chunks(v), to_chunks(g)))
    o = o.transpose(1, 0, 3, 2, 4).reshape(Bsz, L, H, V)
    return o, s_fin

def _ssd_chunked(x, dt, a, Bh, Ch, s0):
    Bsz, L, H, P = x.shape
    c = _chunk_len(L, M_CHUNK)
    n = L // c

    def to_chunks(t):
        return t.reshape((Bsz, n, c) + t.shape[2:]).swapaxes(0, 1)

    tril = jnp.tril(jnp.ones((c, c), dtype=bool))[:, :, None]

    def step(S, inp):
        xc, dtc, ac, bc, cc = inp
        cum = jnp.cumsum(ac, axis=1)
        seg = cum[:, :, None, :] - cum[:, None, :, :]
        Lm = jnp.where(tril, jnp.exp(jnp.where(tril, seg, 0.0)), 0.0)
        scores = jnp.einsum('bthn,bshn->btsh', cc, bc) * Lm
        y_intra = jnp.einsum('btsh,bshp->bthp', scores, xc * dtc[..., None])
        y_inter = jnp.einsum('bthn,bhpn->bthp', cc * jnp.exp(cum)[..., None], S)
        last = cum[:, -1:, :]
        S_new = jnp.exp(last[:, 0, :])[:, :, None, None] * S + jnp.einsum('bshn,bshp->bhpn', bc * (dtc * jnp.exp(last - cum))[..., None], xc)
        return S_new, y_intra + y_inter

    s_fin, y = lax.scan(step, s0, (to_chunks(x), to_chunks(dt), to_chunks(dt * a), to_chunks(Bh), to_chunks(Ch)))
    y = y.swapaxes(0, 1).reshape(Bsz, L, H, P)
    return y, s_fin

def _causal_conv(u, buf, w, b):
    L = u.shape[1]
    cat = jnp.concatenate([buf.astype(u.dtype), u], axis=1)
    out = b
    for j in range(CONV_W):
        out = out + cat[:, j:j + L] * w[j]
    return out, cat[:, L:]

def _mixer(xn, lb, s_hg, s_ssm, s_conv, w_in, conv_w, conv_b, dt_bias, a_log, d_skip, hg_norm_w, ssm_norm_w, w_out):
    f32 = jnp.float32
    Bsz, L, _ = xn.shape
    u = xn @ w_in
    q, fr, iv, go, z, xbc, dt = jnp.split(u, PROJ_SPLITS, axis=-1)
    q = q.reshape(Bsz, L, HG_HEADS, HG_KDIM).astype(f32) * (HG_KDIM ** -0.5)
    fr = fr.reshape(Bsz, L, HG_HEADS, HG_KDIM).astype(f32)
    lb = lb.reshape(HG_HEADS, HG_KDIM).astype(f32)
    g_log = jnp.logaddexp(jnp.log(jnp.maximum(lb, LB_FLOOR)), jnp.log1p(-lb) + jax.nn.log_sigmoid(fr))
    k = (1.0 - lb) * jax.nn.sigmoid(-fr)
    v = iv.reshape(Bsz, L, HG_HEADS, HG_VDIM).astype(f32)
    o_hg, s_hg_new = _gla_chunked(q, k, v, g_log, s_hg.astype(f32))
    o_hg = _rmsnorm(o_hg, hg_norm_w.reshape(HG_HEADS, HG_VDIM)) * jax.nn.silu(go.reshape(Bsz, L, HG_HEADS, HG_VDIM).astype(f32))
    o_hg = o_hg.reshape(Bsz, L, HG_WIDTH)
    xbc_c, s_conv_new = _causal_conv(xbc, s_conv, conv_w, conv_b)
    xbc_c = jax.nn.silu(xbc_c).astype(f32)
    xs, Bm, Cm = jnp.split(xbc_c, (M_DINNER, M_DINNER + M_GROUPS * M_DSTATE), axis=-1)
    xs = xs.reshape(Bsz, L, M_HEADS, M_HEADDIM)
    rep = M_HEADS // M_GROUPS
    Bh = jnp.repeat(Bm.reshape(Bsz, L, M_GROUPS, M_DSTATE), rep, axis=2)
    Ch = jnp.repeat(Cm.reshape(Bsz, L, M_GROUPS, M_DSTATE), rep, axis=2)
    dt = jax.nn.softplus(dt.astype(f32) + dt_bias.astype(f32))
    A = -jnp.exp(a_log.astype(f32))
    y, s_ssm_new = _ssd_chunked(xs, dt, A, Bh, Ch, s_ssm.astype(f32))
    y = y + d_skip.astype(f32)[:, None] * xs
    y = y.reshape(Bsz, L, M_DINNER) * jax.nn.silu(z.astype(f32))
    y = _rmsnorm(y.reshape(Bsz, L, M_GROUPS, M_DINNER // M_GROUPS), ssm_norm_w.reshape(M_GROUPS, M_DINNER // M_GROUPS))
    y = y.reshape(Bsz, L, M_DINNER)
    o = jnp.concatenate([o_hg, y], axis=-1).astype(xn.dtype) @ w_out
    return o, s_hg_new.astype(s_hg.dtype), s_ssm_new.astype(s_ssm.dtype), s_conv_new.astype(s_conv.dtype)

def _layer(x, s_hg, s_ssm, s_conv, lb, gains, w_in, conv_w, conv_b, dt_bias, a_log, d_skip, hg_norm_w, ssm_norm_w, w_out, f1g, f1u, f1d, f2g, f2u, f2d):
    h = x + 0.5 * _rmsnorm(_swiglu(_rmsnorm(x, gains[0]), f1g, f1u, f1d), gains[1])
    m, s_hg, s_ssm, s_conv = _mixer(_rmsnorm(h, gains[2]), lb, s_hg, s_ssm, s_conv, w_in, conv_w, conv_b, dt_bias, a_log, d_skip, hg_norm_w, ssm_norm_w, w_out)
    h = h + _rmsnorm(m, gains[3])
    h = h + 0.5 * _rmsnorm(_swiglu(_rmsnorm(h, gains[4]), f2g, f2u, f2d), gains[5])
    return h, s_hg, s_ssm, s_conv

def setup_inputs(seed: int = 0) -> dict:
    key = jax.random.key(seed)
    ks = jax.random.split(key, 24)
    f32 = jnp.float32

    def nrm(k, shape, fan):
        return jax.random.normal(k, shape, f32) * (fan ** -0.5)

    def gauss(k, shape, s=1.0):
        return jax.random.normal(k, shape, f32) * s

    dt = jnp.exp(jax.random.uniform(ks[9], (DEPTH, M_HEADS), f32) * (math.log(DT_MAX) - math.log(DT_MIN)) + math.log(DT_MIN))
    return {
        "x_prompt": gauss(ks[0], (BATCH, SEQ, D_MODEL)),
        "x_sample": gauss(ks[1], (DEC_BATCH, DEC_SEQ, D_MODEL)),
        "state_hgrn": gauss(ks[2], (DEPTH, DEC_BATCH, HG_HEADS, HG_KDIM, HG_VDIM), 0.5),
        "state_ssm": gauss(ks[3], (DEPTH, DEC_BATCH, M_HEADS, M_HEADDIM, M_DSTATE), 0.5),
        "state_conv": gauss(ks[4], (DEPTH, DEC_BATCH, CONV_W - 1, CONV_DIM)),
        "w_in": nrm(ks[5], (DEPTH, D_MODEL, D_PROJ), D_MODEL),
        "hg_lb_logits": gauss(ks[6], (DEPTH, HG_HEADS * HG_KDIM)),
        "conv_w": nrm(ks[7], (DEPTH, CONV_W, CONV_DIM), CONV_W),
        "conv_b": gauss(ks[8], (DEPTH, CONV_DIM), 0.02),
        "dt_bias": dt + jnp.log(-jnp.expm1(-dt)),
        "a_log": jnp.log(jax.random.uniform(ks[10], (DEPTH, M_HEADS), f32, minval=1.0, maxval=16.0)),
        "d_skip": 1.0 + gauss(ks[11], (DEPTH, M_HEADS), 0.1),
        "hg_norm_w": 1.0 + gauss(ks[12], (DEPTH, HG_WIDTH), 0.05),
        "ssm_norm_w": 1.0 + gauss(ks[13], (DEPTH, M_DINNER), 0.05),
        "w_out": nrm(ks[14], (DEPTH, D_MIX, D_MODEL), D_MIX),
        "ffn1_w_gate": nrm(ks[15], (DEPTH, D_MODEL, D_FF), D_MODEL),
        "ffn1_w_up": nrm(ks[16], (DEPTH, D_MODEL, D_FF), D_MODEL),
        "ffn1_w_down": nrm(ks[17], (DEPTH, D_FF, D_MODEL), D_FF),
        "ffn2_w_gate": nrm(ks[18], (DEPTH, D_MODEL, D_FF), D_MODEL),
        "ffn2_w_up": nrm(ks[19], (DEPTH, D_MODEL, D_FF), D_MODEL),
        "ffn2_w_down": nrm(ks[20], (DEPTH, D_FF, D_MODEL), D_FF),
        "norm_gain": 1.0 + gauss(ks[21], (DEPTH, 6, D_MODEL), 0.05),
    }

def reference(x_prompt, x_sample, state_hgrn, state_ssm, state_conv, w_in, hg_lb_logits, conv_w, conv_b, dt_bias, a_log, d_skip, hg_norm_w, ssm_norm_w, w_out, ffn1_w_gate, ffn1_w_up, ffn1_w_down, ffn2_w_gate, ffn2_w_up, ffn2_w_down, norm_gain):
    p = jax.nn.softmax(hg_lb_logits.astype(jnp.float32), axis=0)
    lb_all = jnp.cumsum(p, axis=0) - p[0]

    def trunk(x, s_hg, s_ssm, s_conv):
        hg_out, ssm_out, conv_out = [], [], []
        for l in range(DEPTH):
            x, a, b, c = _layer(x, s_hg[l], s_ssm[l], s_conv[l], lb_all[l], norm_gain[l], w_in[l], conv_w[l], conv_b[l], dt_bias[l], a_log[l], d_skip[l], hg_norm_w[l], ssm_norm_w[l], w_out[l], ffn1_w_gate[l], ffn1_w_up[l], ffn1_w_down[l], ffn2_w_gate[l], ffn2_w_up[l], ffn2_w_down[l])
            hg_out.append(a)
            ssm_out.append(b)
            conv_out.append(c)
        return x, jnp.stack(hg_out), jnp.stack(ssm_out), jnp.stack(conv_out)

    bp = x_prompt.shape[0]
    dtp = x_prompt.dtype
    y_prompt, hg_p, ssm_p, conv_p = trunk(
        x_prompt,
        jnp.zeros((DEPTH, bp, HG_HEADS, HG_KDIM, HG_VDIM), dtp),
        jnp.zeros((DEPTH, bp, M_HEADS, M_HEADDIM, M_DSTATE), dtp),
        jnp.zeros((DEPTH, bp, CONV_W - 1, CONV_DIM), dtp))
    y_sample, hg_s, ssm_s, conv_s = trunk(x_sample, state_hgrn, state_ssm, state_conv)
    return (y_prompt, y_sample, hg_p, ssm_p, conv_p, hg_s, ssm_s, conv_s)


_drawn_inputs = setup_inputs


def setup_inputs(seed=0):
    import zlib

    import numpy as np

    out = dict(_drawn_inputs(seed))
    spreads = {}
    factors = {}
    for name, (base, spread) in spreads.items():
        noise = np.random.default_rng([zlib.crc32(name.encode()), seed]).standard_normal(out[name].shape)
        drawn = base * np.exp(spread * noise) if base else spread * noise
        out[name] = __import__('jax').numpy.asarray(drawn.astype(out[name].dtype))
    for name, factor in factors.items():
        out[name] = (out[name] * factor).astype(out[name].dtype)
    return out
```

```python
from contextlib import ExitStack

import concourse.bass as bass
from concourse import mybir

F32 = mybir.dt.float32
F32R = mybir.dt.float32r
I32 = mybir.dt.int32
U8 = mybir.dt.uint8
ACT = mybir.ActivationFunctionType
ALU = mybir.AluOpType
ds = bass.ds

P = 128
LAYERS = 2
D = 1024
DT_ = D // P
SEQ = 256
NB, SL = 8, 8
NS = NB * SL
T = SEQ + NS
FF = 2816
FT = FF // P
KD = 128
HH_ = 8
HG = 4
MH, HD = 16, 64
PAIRS = MH // 2
CT = 12
CW = 4
PADP = CW - 1 + SEQ
PADS = CW - 1 + SL
XBW = PADP + NB * PADS
CVW = XBW - (CW - 1)
D_IN = 6672
COL_Q, COL_F, COL_V, COL_GO, COL_Z, COL_X, COL_DT = 0, 1024, 2048, 3072, 4096, 5120, 6656
EPS = 1e-6
LB_FLOOR = 1e-30
QSCALE = KD ** -0.5

UNIT = 2048
U_UP1 = 0
U_DOWN1 = U_UP1 + FT
U_IN = U_DOWN1 + FT // 2
U_OUT = U_IN + 26
U_UP2 = U_OUT + 8
U_DOWN2 = U_UP2 + FT
UNITS = U_DOWN2 + FT // 2
LEVELS = (1, 2, 4, 8, 16, 32, 64)

C_GAIN, C_HGN, C_SSN, C_CB, C_CW, C_LBF, C_OML, C_DSK, C_DTB, C_A, C_END = (
    0, 48, 56, 64, 76, 124, 132, 140, 148, 164, 180)
NROW_A = 84

TILES = ((0, 128), (128, 128), (256, 64))
TURNS = (0, 2, 1)
ROWS = ((slice(0, 128), slice(0, 2)), (slice(0, 64), slice(2, 3)))


class Signal:

    def __init__(self, ctx, nc, name, per_layer, before=0):
        self.sem = ctx.enter_context(nc.semaphore(name))
        self.per_layer, self.before = per_layer, before

    def after(self, l, n):
        return l * self.per_layer + (n + self.before)


def trunk(nc, a, o):
    with ExitStack() as ctx:
        build(nc, a, o, ctx)


def build(nc, a, o, ctx):
    base = (nc.sbuf_base + 31) // 32 * 32
    top = nc.sbuf_usable_end

    def place(name, shape, dtype, at):
        size = 4 if dtype in (F32, F32R, I32) else 1
        n = size
        for s in shape[1:]:
            n *= s
        assert at + n <= top, (name, at + n, top)
        return nc.alloc_sbuf_tensor_at(name, shape, dtype, offset=at), (at + n + 31) // 32 * 32

    at = base
    X, at = place("X", [P, DT_, T], F32, at)
    at_xh = at
    XH, at = place("XH", [P, DT_, T], F32R, at)
    at_xl = at
    XL, at = place("XL", [P, DT_, T], F32R, at)
    at_hh = at
    HH, at = place("HH", [P, FT, T], F32R, at)
    at_hl = at
    HL, at = place("HL", [P, FT, T], F32R, at)
    RAW, at = place("RAW", [P, 2, UNIT], F32, at)
    WH, at = place("WH", [P, 2, UNIT], F32R, at)
    WL, at = place("WL", [P, 2, UNIT], F32R, at)
    IDENT, at = place("IDENT", [P, P], F32, at)
    ONES, at = place("ONES", [P, P], F32, at)
    TRI, at = place("TRI", [P, P], F32, at)
    USTR, at = place("USTR", [P, P], F32, at)
    TRI8, at = place("TRI8", [NS, NS], F32, at)
    USTR8, at = place("USTR8", [NS, NS], F32, at)
    MASK, at = place("MASK", [P, 8, P], U8, at)
    BLK, at = place("BLK", [NS, NB], F32, at)
    PALL, at = place("PALL", [P, LAYERS, C_END], F32, at)
    PAR, at = place("PAR", [P, C_END], F32, at)
    EPST, at = place("EPST", [P, 1], F32, at)
    FREE, at = place("FREE", [P, 1], F32, at)
    FREEV, at = place("FREEV", [P, 1], F32, at)
    ROOT, at = place("ROOT", [P, T], F32, at)
    RINV, at = place("RINV", [P, T], F32, at)
    WDT, at = place("WDT", [P, DT_, MH], F32, at)
    DTT, at = place("DTT", [P, 3, MH], F32, at)
    DTW, at = place("DTW", [P, 5, 3, MH], F32, at)
    AT, at = place("AT", [P, 3, MH], F32, at)
    REM, at = place("REM", [P, 3, MH], F32, at)
    arena = at

    XROW, e = place("XROW", [P, 3, D], F32, arena)
    PROWA, e = place("PROWA", [NROW_A, LAYERS, P], F32, e)
    PROWB, e = place("PROWB", [48, LAYERS, P], F32, e)
    IT, e = place("IT", [P, P], I32, e)
    IS, e = place("IS", [P, P], I32, e)
    IX, e = place("IX", [P, P], I32, e)
    FIT, e = place("FIT", [P, P], F32, e)
    FIX, e = place("FIX", [P, P], F32, e)
    FGE, e = place("FGE", [P, 8, P], F32, e)
    IBK, e = place("IBK", [NS, NB], I32, e)
    FB, e = place("FB", [NS, 2, NB], F32, e)
    LBW, e = place("LBW", [P, 8, 8], F32, e)
    YROW = XROW

    MS, e = place("MS", [P, DT_, T], F32, arena)
    SQ, e = place("SQ", [P, DT_, T], F32, e)
    SG, e = place("SG", [P, 2, 2, T], F32, e)
    HF, e = place("HF", [P, 2, 2, T], F32, e)
    XN = MS

    PRE, e = place("PRE", [P, HG, T], F32, arena)
    KF, e = place("KF", [P, HG, T], F32, e)
    QF, e = place("QF", [P, HG, T], F32, e)
    GO, e = place("GO", [P, HG, T], F32, e)
    SUF, e = place("SUF", [P, HG, T], F32, e)
    at_w = e
    W, e = place("W", [P, 2, HG, T], F32, e)
    SQO, _ = place("SQO", [P, HG, T], F32, at_w)
    RTO, _ = place("RTO", [P, HG, T], F32, at_w + HG * T * 4)
    VF, e = place("VF", [P, HG, T], F32, e)
    APR, e = place("APR", [P, 2, HG, P], F32, e)
    ASM, e = place("ASM", [NS, HG, NS], F32, e)
    VTOK, e = place("VTOK", [P, 3, HG * KD], F32, e)
    KTOK, e = place("KTOK", [P, 3, HG * KD], F32, e)
    VM, e = place("VM", [NS, NB, KD], F32, e)
    tail = 16 * T * 4
    SIN0, e0 = place("SIN0", [P, NB, KD], F32, at_hh + tail)
    SIN1, e1 = place("SIN1", [P, NB, KD], F32, at_hl + tail)
    S1, e0 = place("S1", [P, HG, KD], F32, e0)
    S2, e1 = place("S2", [P, HG, KD], F32, e1)
    assert e0 <= at_hl and e1 <= at_hl + FT * T * 4
    SIN = (SIN0, SIN1)

    at_xb = arena
    XB, e = place("XB", [P, CT, XBW], F32, arena)
    Z, e = place("Z", [P, PAIRS, T], F32, e)
    XC, e = place("XC", [P, CT, T], F32, e)
    at_acc = e
    ACC, e = place("ACC", [P, 4, XBW], F32, e)
    at_dtx = e
    DTX, e = place("DTX", [P, 3, MH * HD], F32, e)
    BTOK, e = place("BTOK", [P, 3, 2 * P], F32, e)
    GM, em = place("GM", [P, 3, 2, P], F32, at_hh + tail + NB * KD * 4)
    assert em <= at_hl
    CROW, _ = place("CROW", [NB * 3, CT * P], F32, at_dtx)
    CS, e2 = place("CS", [P, CT, 27], F32, at_acc)
    CO, _ = place("CO", [27, CT * P], F32, at_hh + 8 * T * 4)
    WX, e3 = place("WX", [P, 3, MH * HD], F32, at_xb)
    HT1, e3 = place("HT1", [P, MH * HD], F32, e3)
    assert e3 <= at_xb + CT * XBW * 4
    L1, e4 = place("L1", [P, 2, 2, P], F32, at_xh)
    L1S, e4 = place("L1S", [NS, 2, NS], F32, e4)
    ST, e4 = place("ST", [P, 2, 2, P], F32, e4)
    STS, e4 = place("STS", [NS, 2, NS], F32, e4)
    EC, e4 = place("EC", [P, T], F32, e4)
    Y2, e4 = place("Y2", [P, T], F32, e4)
    SP, e4 = place("SP", [P, 2, P], F32, e4)
    assert e4 <= at_xl
    HTS, e5 = place("HTS", [P, NB, P], F32, at_xl)
    BMK, e5 = place("BMK", [NS, NB, P], F32, e5)
    assert e5 <= at_hh
    SQS, _ = place("SQS", [P, PAIRS, T], F32, at_xb)

    PS = ctx.enter_context(nc.psum_tensor("PS", [P, 8, 512], F32))

    def gain(i, k):
        return PAR[:, C_GAIN + 8 * i + k:C_GAIN + 8 * i + k + 1]

    def col(c):
        return PAR[:, c:c + 1]

    def sig(name, per_layer=0, before=0):
        return Signal(ctx, nc, name, per_layer, before)

    consts_done = sig("consts_done")
    iota_done = sig("iota_done")
    params_in = sig("params_in")
    params_turned = sig("params_turned")
    params_done = sig("params_done")
    x_rows_in = sig("x_rows_in")
    x_turned = sig("x_turned")
    lb_step = sig("lb_step")
    lb_exp = sig("lb_exp")
    const_step = sig("const_step")

    raw_landed = (sig("raw_landed0", 16 * UNITS // 2), sig("raw_landed1", 16 * UNITS // 2))
    hi_ready = sig("hi_ready", UNITS)
    lo_ready = sig("lo_ready", UNITS, 2)
    unit_done = sig("unit_done", UNITS, 2)

    par_ready = sig("par_ready", 1)
    presq_ready = sig("presq_ready", 12)
    postsq_ready = sig("postsq_ready", 12)
    ms_ready = sig("ms_ready", 12)
    stat_ready = sig("stat_ready", 6)
    root_ready = sig("root_ready", 6)
    rinv_ready = sig("rinv_ready", 6)
    scaled_ready = sig("scaled_ready", 24)
    xn_ready = sig("xn_ready", 24)
    xh_ready = sig("xh_ready", 12)
    xl_ready = sig("xl_ready", 12)
    x_ready = sig("x_ready", 12, 3)
    sg_ready = sig("sg_ready", FT)
    h_ready = sig("h_ready", FT, 2)
    hh_ready = sig("hh_ready", FT)
    hl_ready = sig("hl_ready", FT)
    fsig_ready = sig("fsig_ready", 2 * 4)
    fk_ready = sig("fk_ready", 2 * 8)
    q_ready = sig("q_ready", 2 * 2)
    v_ready = sig("v_ready", 2 * 2)
    go_ready = sig("go_ready", 2 * 2)
    hgz_ready = sig("hgz_ready", 2 * 3)
    w_ready = sig("w_ready", 2 * 16)
    tree_ready = sig("tree_ready", 2 * 14)
    score_ready = sig("score_ready", 2 * 8)
    picked = sig("picked", 2 * 8)
    vturn_ready = sig("vturn_ready", 2 * 3)
    vtok_ready = sig("vtok_ready", 2 * 3)
    kturn_ready = sig("kturn_ready", 2 * 3)
    ktok_ready = sig("ktok_ready", 2 * 3)
    sp1_ready = sig("sp1_ready", 2)
    s1_ready = sig("s1_ready", 2)
    sp2_ready = sig("sp2_ready", 2)
    s2_ready = sig("s2_ready", 2)
    s2_stored = sig("s2_stored", 2 * 16, 16)
    hs_in = (sig("hs_in0", 4 * 16), sig("hs_in1", 4 * 16))
    hs_stored = (sig("hs_stored0", 4 * 16, 16), sig("hs_stored1", 4 * 16, 16))
    vm_ready = sig("vm_ready", HH_)
    upd_ready = sig("upd_ready", HH_)
    decayed = sig("decayed", HH_)
    snew_ready = sig("snew_ready", HH_)
    o_ready = sig("o_ready", HH_)
    sqo_ready = sig("sqo_ready", HH_)
    ostat_ready = sig("ostat_ready", 2)
    oroot_ready = sig("oroot_ready", 2)
    orinv_ready = sig("orinv_ready", 2)
    gor_ready = sig("gor_ready", 2)
    ohg_ready = sig("ohg_ready", HH_, 1)
    ohh_ready = sig("ohh_ready", 2)
    ohl_ready = sig("ohl_ready", 2, 1)
    wdt_in = sig("wdt_in", 16)
    dtp_ready = sig("dtp_ready", 1)
    dt_step = sig("dt_step", 20)
    dt_exp = sig("dt_exp", 4)
    remp_ready = sig("remp_ready", 1)
    rem_ready = sig("rem_ready", 2)
    crow_in = sig("crow_in", 16)
    cturn_ready = sig("cturn_ready", 1)
    zeros_ready = sig("zeros_ready", 1)
    pads_ready = sig("pads_ready", 1)
    xb_ready = sig("xb_ready", 12, 4)
    z_ready = sig("z_ready", 4, 2)
    acc_ready = sig("acc_ready", CT)
    tap_ready = sig("tap_ready", 3 * CT)
    xc_ready = sig("xc_ready", 6)
    cs_ready = sig("cs_ready", 2)
    csturn_ready = sig("csturn_ready", 1)
    co_ready = sig("co_ready", 1)
    co_stored = sig("co_stored", 32)
    xturn_ready = sig("xturn_ready", 3)
    dtx_ready = sig("dtx_ready", 3)
    btok_ready = sig("btok_ready", 3)
    g_ready = sig("g_ready", 3)
    gm_ready = sig("gm_ready", 3)
    wx_ready = sig("wx_ready", 3)
    bmk_ready = sig("bmk_ready", 2)
    ht1p_ready = sig("ht1p_ready", 1)
    ht1_ready = sig("ht1_ready", 1)
    l1_ready = sig("l1_ready", 2 * PAIRS)
    seg_ready = sig("seg_ready", PAIRS)
    e_ready = sig("e_ready", 3 * PAIRS)
    st_ready = sig("st_ready", 2 * PAIRS)
    ms_in = (sig("ms_in0", 4 * 16), sig("ms_in1", 4 * 16))
    ms_stored = (sig("ms_stored0", 4 * 16, 16), sig("ms_stored1", 4 * 16, 16))
    hts_turned = sig("hts_turned", PAIRS)
    hts_ready = sig("hts_ready", PAIRS)
    y_ready = sig("y_ready", PAIRS)
    y2_ready = sig("y2_ready", PAIRS)
    ydone = sig("ydone", PAIRS)
    ystep = sig("ystep", 2 * PAIRS)
    supd_ready = sig("supd_ready", PAIRS)
    spc_ready = sig("spc_ready", PAIRS)
    spn_ready = sig("spn_ready", PAIRS)
    ssm_new = sig("ssm_new", PAIRS)
    sp_stored = (sig("sp_stored0", 4 * 16, 16), sig("sp_stored1", 4 * 16, 16))
    yz_ready = sig("yz_ready", 2)
    sqs_ready = sig("sqs_ready", 2)
    sstat_ready = sig("sstat_ready", 1)
    sroot_ready = sig("sroot_ready", 1)
    srinv_ready = sig("srinv_ready", 1)
    ysn_ready = sig("ysn_ready", PAIRS)
    yh_ready = sig("yh_ready", 4)
    yl_ready = sig("yl_ready", 4)
    yout_turned = sig("yout_turned")
    yout_ready = sig("yout_ready")
    y_stored = sig("y_stored")

    block = ctx.enter_context(nc.Block())

    def unit(u0, i=None, step=2):
        if i is None:
            return u0 % 2, u0, u0 // 2
        return u0 % 2, i * step + u0, i * (step // 2) + u0 // 2

    @block.sync
    def _(sp):
        sp.dma_start(XROW[:, 0:2, :], a["x_prompt"][0].rearrange("(n p) d -> p n d", p=P)).then_inc(x_rows_in.sem, 16)
        sp.dma_start(XROW[0:NS, 2, :], a["x_sample"].rearrange("b t d -> (b t) d")).then_inc(x_rows_in.sem, 16)
        with nc.allow_non_contiguous_dma("small parameter rows"):
            r = 0
            for name, n in (("norm_gain", 48), ("hg_norm_w", 8), ("ssm_norm_w", 8), ("conv_b", 12),
                            ("hg_lb_logits", 8)):
                src = a[name]
                if name == "norm_gain":
                    src = src.rearrange("l g d -> l (g d)")
                sp.dma_start(PROWA[r:r + n, :, :], src.rearrange("l (r p) -> r l p", p=P)).then_inc(params_in.sem, 16)
                r += n
            sp.dma_start(PROWB[:, :, :], a["conv_w"].rearrange("l j (c p) -> (j c) l p", p=P)).then_inc(params_in.sem, 16)
            for hh in range(2):
                for l in range(LAYERS):
                    src = a["d_skip"].rearrange("l (i h) -> h l i", h=2)[hh:hh + 1, l, :]
                    sp.dma_start(PALL[64 * hh:64 * hh + 64, l, C_DSK:C_DSK + PAIRS],
                                 src.broadcast_to([64, PAIRS])).then_inc(params_in.sem, 16)
            for name, c in (("dt_bias", C_DTB), ("a_log", C_A)):
                src = a[name].rearrange("(o l) h -> o l h", o=1)
                sp.dma_start(PALL[:, :, c:c + MH], src.broadcast_to([P, LAYERS, MH])).then_inc(params_in.sem, 16)

        def fetch_columns(l, w, u, c0):
            slot, n, _ = u
            sp.wait_ge(lo_ready.sem, lo_ready.after(l, n) + (1 - 2))
            src = w[ds(l, 1), :, ds(c0, 256)].rearrange("o (k p) c -> p (o k) c", p=P)
            sp.dma_start(RAW[:, slot, :].rearrange("p (k c) -> p k c", c=256), src).then_inc(raw_landed[slot].sem, 16)

        def fetch_rows(l, w, u, r0):
            slot, n, _ = u
            sp.wait_ge(lo_ready.sem, lo_ready.after(l, n) + (1 - 2))
            src = w[ds(l, 1), ds(r0, 256), :].rearrange("o (k p) c -> p (o k) c", p=P)
            sp.dma_start(RAW[:, slot, :].rearrange("p (k c) -> p k c", c=D), src).then_inc(raw_landed[slot].sem, 16)

        def ffn(l, up, down, g, u_, d):
            with sp.Fori(0, FT // 2) as j:
                fetch_columns(l, a[g], unit(up, j), j * 256)
                fetch_columns(l, a[u_], unit(up + 1, j), j * 256)
            with sp.Fori(0, 5) as j:
                fetch_rows(l, a[d], unit(down, j), j * 512)
                fetch_rows(l, a[d], unit(down + 1, j), j * 512 + 256)
            fetch_rows(l, a[d], unit(down + 10), 10 * 256)

        with sp.Fori(0, LAYERS) as l:
            ffn(l, U_UP1, U_DOWN1, "ffn1_w_gate", "ffn1_w_up", "ffn1_w_down")
            with sp.Fori(0, 2) as g:
                for c, c0 in enumerate((COL_F, COL_Q, COL_V, COL_GO)):
                    for s in range(2):
                        fetch_columns(l, a["w_in"], unit(U_IN + 2 * c + s, g, 8), g * 512 + (c0 + 256 * s))
            for first, n, c0 in ((U_IN + 16, 3, COL_X), (U_IN + 22, 2, COL_Z)):
                with sp.Fori(0, n) as i:
                    for s in range(2):
                        fetch_columns(l, a["w_in"], unit(first + s, i), i * 512 + (c0 + 256 * s))
            with sp.Fori(0, 4) as i:
                fetch_rows(l, a["w_out"], unit(U_OUT, i), i * 512)
                fetch_rows(l, a["w_out"], unit(U_OUT + 1, i), i * 512 + 256)
            ffn(l, U_UP2, U_DOWN2, "ffn2_w_gate", "ffn2_w_up", "ffn2_w_down")
        for n in range(3):
            sp.wait_ge(yout_ready.sem, n + 1)
            dst = (o["y_prompt"][0][n * P:(n + 1) * P, :] if n < 2 else o["y_sample"].rearrange("b t d -> (b t) d"))
            sp.dma_start(dst, YROW[0:TILES[n][1], n, :]).then_inc(y_stored.sem, 16)
        sp.wait_ge(y_stored.sem, 48)

    @block.gpsimd
    def _(pool):
        nc.gpsimd.iota(IT[:], pattern=[[1, P]], base=0, channel_multiplier=0).then_inc(iota_done.sem, 1)
        nc.gpsimd.iota(IS[:], pattern=[[0, P]], base=0, channel_multiplier=1).then_inc(iota_done.sem, 1)
        nc.gpsimd.iota(IBK[:], pattern=[[-SL, NB]], base=0, channel_multiplier=1).then_inc(iota_done.sem, 1)

        def blocked(src, n):
            return (src.rearrange("p (o v) -> p o v", o=1).broadcast_to([NS, NB, n]),
                    BLK[:].rearrange("p (b o) -> p b o", o=1).broadcast_to([NS, NB, n]))

        def hgrn(l, g):
            pool.wait_ge(unit_done.sem, unit_done.after(l, g * 8 + (U_IN + 1)))
            pool.wait_ge(ohl_ready.sem, ohl_ready.after(l, g))
            one = ONES[:, 0:1].rearrange("p (a b) -> p a b", a=1).broadcast_to([P, HG, T])
            nc.gpsimd.tensor_tensor(SUF[:], one, one, ALU.mult).then_inc(hgz_ready.sem, 1)
            nc.gpsimd.memset(APR[:], 0.0).then_inc(hgz_ready.sem, 1)
            nc.gpsimd.memset(ASM[:], 0.0).then_inc(hgz_ready.sem, 1)
            for h in range(HG):
                pool.wait_ge(vtok_ready.sem, vtok_ready.after(l, g * 3 + 2))
                if h:
                    pool.wait_ge(upd_ready.sem, upd_ready.after(l, g * 4 + h))
                nc.gpsimd.tensor_tensor(VM[:], *blocked(VTOK[0:NS, 2, h * KD:(h + 1) * KD], KD),
                                        ALU.mult).then_inc(vm_ready.sem, 1)
                pool.wait_ge(o_ready.sem, o_ready.after(l, g * 4 + h + 1))
                s = SIN[h % 2]
                nc.gpsimd.tensor_tensor(
                    s[:], s[:],
                    PRE[:, h, SEQ + SL - 1:T:SL].rearrange("p (b o) -> p b o", o=1).broadcast_to([P, NB, KD]),
                    ALU.mult).then_inc(decayed.sem, 1)

        def mamba(l):
            pool.wait_ge(ohl_ready.sem, ohl_ready.after(l, 2))

            def one(*shape):
                return ONES[:, 0:1].rearrange("p (a b) -> p a b", a=1).broadcast_to([P, *shape])

            nc.gpsimd.tensor_tensor(XB[:, :, 0:CW - 1], one(CT, CW - 1), one(CT, CW - 1), ALU.subtract).then_inc(zeros_ready.sem, 1)
            pool.wait_ge(xc_ready.sem, xc_ready.after(l, 6))
            nc.gpsimd.tensor_tensor(CS[:, :, 0:3], XB[:, :, SEQ:PADP], one(CT, 3), ALU.mult).then_inc(cs_ready.sem, 1)
            nc.gpsimd.tensor_copy(
                CS[:, :, 3:27].rearrange("p c (b j) -> p c b j", j=3),
                XB[:, :, PADP:].rearrange("p c (b j) -> p c b j", j=PADS)[:, :, :, SL:]).then_inc(cs_ready.sem, 1)
            pool.wait_ge(rem_ready.sem, rem_ready.after(l, 2))
            pool.wait_ge(cs_ready.sem, cs_ready.after(l, 2))
            for j, n in enumerate(TURNS):
                tn = TILES[n][1]
                pool.wait_ge(dtx_ready.sem, dtx_ready.after(l, j + 1))
                nc.gpsimd.tensor_tensor(
                    WX[0:tn, n, :].rearrange("p (h d) -> p h d", d=HD),
                    DTX[0:tn, n, :].rearrange("p (h d) -> p h d", d=HD),
                    REM[0:tn, n, :].rearrange("p (h o) -> p h o", o=1).broadcast_to([tn, MH, HD]),
                    ALU.mult).then_inc(wx_ready.sem, 1)
            for g in range(2):
                pool.wait_ge(btok_ready.sem, btok_ready.after(l, 3))
                if g:
                    pool.wait_ge(supd_ready.sem, supd_ready.after(l, 4))
                nc.gpsimd.tensor_tensor(BMK[:], *blocked(BTOK[0:NS, 2, g * P:(g + 1) * P], P),
                                        ALU.mult).then_inc(bmk_ready.sem, 1)

        with pool.Fori(0, LAYERS) as l:
            with pool.Fori(0, 2) as g:
                hgrn(l, g)
            mamba(l)

    @block.scalar
    def _(act):
        def copy(out, in_, scale=1.0):
            return nc.scalar.activation(out, in_, ACT.Copy, scale=scale)

        def split_hi(l, u):
            slot, n, k = u
            act.wait_ge(raw_landed[slot].sem, raw_landed[slot].after(l, k * 16 + 16))
            act.wait_ge(unit_done.sem, unit_done.after(l, n) + (1 - 2))
            copy(WH[:, slot, :], RAW[:, slot, :]).then_inc(hi_ready.sem, 1)

        def ahead(u):
            return u[0], u[1] + 2, u[2] + 1

        act.wait_ge(consts_done.sem, 1)
        for n, (t0, tn) in enumerate(TILES):
            act.wait_ge(x_turned.sem, n + 1)
            copy(X[:, :, t0:t0 + tn],
                 PS[:, 2 * n:2 * n + 2, :].rearrange("p b (k t) -> p (b k) t", t=P)[:, :, 0:tn]).then_inc(x_ready.sem, 1)
        act.wait_ge(lb_step.sem, 3)
        nc.scalar.activation(LBW[:, 3:5], LBW[:, 3:5], ACT.Exp).then_inc(lb_exp.sem, 1)
        nc.scalar.activation(PALL[:, :, C_A:C_A + MH], PALL[:, :, C_A:C_A + MH], ACT.Exp).then_inc(lb_exp.sem, 1)
        for s in (s2_stored, *hs_stored, *ms_stored, *sp_stored):
            copy(FREE[:], EPST[:]).then_inc(s.sem, 16)
            act.wait_ge(s.sem, 16)

        def pre_norm(l, i):
            for c in range(4):
                act.wait_ge(x_ready.sem, x_ready.after(l, 4 * i + c - 3 if i else 0))
                nc.scalar.activation(SQ[:, 2 * c:2 * c + 2], X[:, 2 * c:2 * c + 2], ACT.Square).then_inc(presq_ready.sem, 1)
            act.wait_ge(stat_ready.sem, stat_ready.after(l, 2 * i + 1))
            nc.scalar.activation(ROOT[:], PS[:, 0, 0:T], ACT.Sqrt, bias=EPST[:], scale=1.0 / D).then_inc(root_ready.sem, 1)
            for c in range(4):
                act.wait_ge(xn_ready.sem, xn_ready.after(l, 8 * i + 2 * c + 2))
                copy(XH[:, 2 * c:2 * c + 2], XN[:, 2 * c:2 * c + 2]).then_inc(xh_ready.sem, 1)

        def post_norm(l, i, last_unit):
            act.wait_ge(unit_done.sem, unit_done.after(l, last_unit + 1))
            for c in range(4):
                copy(MS[:, 2 * c:2 * c + 2], PS[:, 2 * c:2 * c + 2, 0:T]).then_inc(ms_ready.sem, 1)
            act.wait_ge(stat_ready.sem, stat_ready.after(l, 2 * i + 2))
            nc.scalar.activation(ROOT[:], PS[:, 0, 0:T], ACT.Sqrt, bias=EPST[:], scale=1.0 / D).then_inc(root_ready.sem, 1)

        def ffn(l, f, up, down):
            def pair(j, par, gate, up_):
                act.wait_ge(unit_done.sem, unit_done.after(l, gate[1]) + 1)
                split_hi(l, ahead(gate))
                nc.scalar.activation(SG[:, par], PS[:, 4 * par:4 * par + 2, 0:T], ACT.Silu).then_inc(sg_ready.sem, 1)
                split_hi(l, ahead(up_))
                act.wait_ge(h_ready.sem, h_ready.after(l, j) + 1)
                copy(HH[:, ds(j * 2 - 22 * f, 2), :], HF[:, par]).then_inc(hh_ready.sem, 1)

            with act.Fori(0, 5) as i:
                for s in range(2):
                    pair(i * 2 + (11 * f + s), s, unit(up + 2 * s, i, 4), unit(up + 2 * s + 1, i, 4))
            act.wait_ge(unit_done.sem, unit_done.after(l, up + 20) + 1)
            split_hi(l, unit(up + 22))
            nc.scalar.activation(SG[:, 0], PS[:, 0:2, 0:T], ACT.Silu).then_inc(sg_ready.sem, 1)
            split_hi(l, unit(up + 23))
            act.wait_ge(h_ready.sem, h_ready.after(l, 11 * f + 11))
            copy(HH[:, 20:22, :], HF[:, 0]).then_inc(hh_ready.sem, 1)
            with act.Fori(0, 4) as i:
                split_hi(l, unit(down + 2, i))
                split_hi(l, unit(down + 3, i))
            split_hi(l, unit(down + 10))
            if f == 0:
                split_hi(l, unit(down + 11))
                split_hi(l, unit(down + 12))

        def hgrn_state_in(l, g, h):
            act.wait_ge(hs_stored[h % 2].sem, hs_stored[h % 2].after(l, g * 32 + h // 2 * 16))
            act.dma_start(SIN[h % 2][:],
                          a["state_hgrn"][ds(l, 1), :, ds(g * 4 + h, 1)].rearrange("o b h k v -> k (o b h) v")
                          ).then_inc(hs_in[h % 2].sem, 16)

        def hgrn(l, g):
            hgrn_state_in(l, g, 0)
            hgrn_state_in(l, g, 1)
            for c in range(8):
                u = unit(U_IN + c, g, 8)
                act.wait_ge(unit_done.sem, unit_done.after(l, u[1]) + 1)
                split_hi(l, ahead(u))
                b = 2 * (c % 4)
                ps = PS[:, b:b + 2, 0:T]
                h = slice(2 * (c % 2), 2 * (c % 2) + 2)
                if c == 0:
                    act.wait_ge(ohl_ready.sem, ohl_ready.after(l, g))
                if c < 2:
                    nc.scalar.activation(PRE[:, h], ps, ACT.Sigmoid).then_inc(fsig_ready.sem, 1)
                    nc.scalar.activation(KF[:, h], ps, ACT.Sigmoid, scale=-1.0).then_inc(fsig_ready.sem, 1)
                elif c < 4:
                    copy(QF[:, h], ps, QSCALE).then_inc(q_ready.sem, 1)
                elif c < 6:
                    copy(VF[:, h], ps).then_inc(v_ready.sem, 1)
                else:
                    nc.scalar.activation(GO[:, h], ps, ACT.Silu).then_inc(go_ready.sem, 1)
            for j, n in enumerate(TURNS):
                tn = TILES[n][1]
                act.wait_ge(vturn_ready.sem, vturn_ready.after(l, g * 3 + j + 1))
                copy(VTOK[0:tn, n, :], PS[0:tn, 6 + j % 2, :]).then_inc(vtok_ready.sem, 1)
            for j, n in enumerate(TURNS):
                tn = TILES[n][1]
                act.wait_ge(kturn_ready.sem, kturn_ready.after(l, g * 3 + j + 1))
                copy(KTOK[0:tn, n, :], PS[0:tn, 6 + j % 2, :]).then_inc(ktok_ready.sem, 1)
            act.wait_ge(sp1_ready.sem, sp1_ready.after(l, g + 1))
            copy(S1[:], PS[:, 4, :].rearrange("p (h v) -> p h v", v=KD)).then_inc(s1_ready.sem, 1)
            act.wait_ge(s2_ready.sem, s2_ready.after(l, g + 1))
            act.dma_start(o["hgrn_prompt"][ds(l, 1), 0, ds(g * 4, 4)].rearrange("o h k v -> k (o h) v"),
                          S2[:]).then_inc(s2_stored.sem, 16)
            for h in range(HG):
                act.wait_ge(o_ready.sem, o_ready.after(l, g * 4 + h + 1))
                nc.scalar.activation(SQO[:, h], PS[:, h, 0:T], ACT.Square).then_inc(sqo_ready.sem, 1)
                act.wait_ge(snew_ready.sem, snew_ready.after(l, g * 4 + h + 1))
                act.dma_start(o["hgrn_sample"][ds(l, 1), :, ds(g * 4 + h, 1)].rearrange("o b h k v -> k (o b h) v"),
                              SIN[h % 2][:]).then_inc(hs_stored[h % 2].sem, 16)
                if h < 2:
                    hgrn_state_in(l, g, h + 2)
            act.wait_ge(ostat_ready.sem, ostat_ready.after(l, g + 1))
            nc.scalar.activation(RTO[:], PS[:, 4:8, 0:T], ACT.Sqrt, bias=EPST[:], scale=1.0 / KD).then_inc(oroot_ready.sem, 1)
            act.wait_ge(ohg_ready.sem, ohg_ready.after(l, g * 4 + 4))
            copy(HH[:, ds(g * 4, 4), :], SQO[:]).then_inc(ohh_ready.sem, 1)

        def ssm_state_in(l, i):
            act.wait_ge(ms_stored[i % 2].sem, ms_stored[i % 2].after(l, i // 2 * 16))
            act.dma_start(SIN[i % 2][:],
                          a["state_ssm"][ds(l, 1), :, 2 * i:2 * i + 2].rearrange("o b h p n -> (h p) (o b) n")
                          ).then_inc(ms_in[i % 2].sem, 16)

        def mamba(l):
            act.wait_ge(hs_stored[0].sem, hs_stored[0].after(l, 64))
            act.wait_ge(hs_stored[1].sem, hs_stored[1].after(l, 64))
            ssm_state_in(l, 0)
            ssm_state_in(l, 1)
            act.wait_ge(ohl_ready.sem, ohl_ready.after(l, 2))
            act.dma_start(CROW[:], a["state_conv"][ds(l, 1)].rearrange("o b j c -> (o b j) c")).then_inc(crow_in.sem, 16)
            with act.Fori(0, 3) as i:
                for s in range(2):
                    u = unit(U_IN + 16 + s, i)
                    act.wait_ge(unit_done.sem, unit_done.after(l, u[1]) + 1)
                    split_hi(l, ahead(u))
                    c = i * 4 + 2 * s
                    copy(XB[:, ds(c, 2), CW - 1:PADP], PS[:, 2 * s:2 * s + 2, 0:SEQ]).then_inc(xb_ready.sem, 1)
                    copy(XB[:, ds(c, 2), PADP:].rearrange("p c (b j) -> p c b j", j=PADS)[:, :, :, CW - 1:],
                         PS[:, 2 * s:2 * s + 2, SEQ:T].rearrange("p c (b j) -> p c b j", j=SL)).then_inc(xb_ready.sem, 1)
            with act.Fori(0, 2) as i:
                for s in range(2):
                    u = unit(U_IN + 22 + s, i)
                    act.wait_ge(unit_done.sem, unit_done.after(l, u[1]) + 1)
                    split_hi(l, ahead(u))
                    nc.scalar.activation(Z[:, ds(i * 4 + 2 * s, 2), :], PS[:, 4 + 2 * s:6 + 2 * s, 0:T],
                                         ACT.Silu).then_inc(z_ready.sem, 1)
            act.wait_ge(cturn_ready.sem, cturn_ready.after(l, 1))
            copy(XB[:, :, PADP:].rearrange("p c (b j) -> p c b j", j=PADS)[:, :, :, 0:CW - 1],
                 PS[:, 0, 0:CT * 24].rearrange("p (c b j) -> p c b j", b=NB, j=CW - 1)).then_inc(pads_ready.sem, 1)
            act.wait_ge(pads_ready.sem, pads_ready.after(l, 1))
            act.wait_ge(xb_ready.sem, xb_ready.after(l, 12))
            act.wait_ge(zeros_ready.sem, zeros_ready.after(l, 1))
            for q in range(3):
                if q:
                    act.wait_ge(xc_ready.sem, xc_ready.after(l, 2 * q))
                for c in range(4):
                    k = 4 * q + c
                    nc.scalar.activation(ACC[:, c, 0:CVW], XB[:, k, CW - 1:XBW], ACT.Identity, bias=col(C_CB + k),
                                         scale=col(C_CW + 3 * CT + k)).then_inc(acc_ready.sem, 1)
                act.wait_ge(tap_ready.sem, tap_ready.after(l, 12 * q + 12))
                nc.scalar.activation(XC[:, 4 * q:4 * q + 4, 0:SEQ], ACC[:, :, 0:SEQ], ACT.Silu).then_inc(xc_ready.sem, 1)
                nc.scalar.activation(
                    XC[:, 4 * q:4 * q + 4, SEQ:].rearrange("p c (b j) -> p c b j", j=SL),
                    ACC[:, :, PADP:].rearrange("p c (b j) -> p c b j", j=PADS)[:, :, :, 0:SL], ACT.Silu).then_inc(xc_ready.sem, 1)
            for f in range(2):
                for r, n in ROWS:
                    if f == 0:
                        act.wait_ge(dt_step.sem, dt_step.after(l, 4))
                        nc.scalar.activation(DTW[r, 2, n], DTW[r, 1, n], ACT.Exp).then_inc(dt_exp.sem, 1)
                    else:
                        act.wait_ge(dt_exp.sem, dt_exp.after(l, 2))
                        nc.scalar.activation(DTW[r, 3, n], DTW[r, 2, n], ACT.Ln, bias=1.0).then_inc(dt_exp.sem, 1)
            act.wait_ge(remp_ready.sem, remp_ready.after(l, 1))
            for k, (r, n) in enumerate(ROWS):
                nc.scalar.activation(REM[r, n], PS[r, 1, 0:48].rearrange("p (n h) -> p n h", h=MH)[:, n], ACT.Exp).then_inc(rem_ready.sem, 1)
            for j, n in enumerate(TURNS):
                tn = TILES[n][1]
                act.wait_ge(xturn_ready.sem, xturn_ready.after(l, j + 1))
                copy(BTOK[0:tn, n, :], PS[0:tn, 5 if j == 1 else 2, 0:2 * P]).then_inc(btok_ready.sem, 1)
            act.wait_ge(ht1p_ready.sem, ht1p_ready.after(l, 1))
            copy(HT1[:].rearrange("p (g c) -> p g c", g=2), PS[:, 0:2, :]).then_inc(ht1_ready.sem, 1)
            act.wait_ge(csturn_ready.sem, csturn_ready.after(l, 1))
            copy(CO[:].rearrange("p (b c) -> p b c", b=3), PS[0:27, 5:8, :]).then_inc(co_ready.sem, 1)
            act.wait_ge(co_ready.sem, co_ready.after(l, 1))
            act.dma_start(o["conv_prompt"][ds(l, 1), 0].rearrange("o j c -> (o j) c"), CO[0:3, :]).then_inc(co_stored.sem, 16)
            act.dma_start(o["conv_sample"][ds(l, 1)].rearrange("o b j c -> (o b j) c"), CO[3:27, :]).then_inc(co_stored.sem, 16)
            for i in range(PAIRS):
                act.wait_ge(seg_ready.sem, seg_ready.after(l, i + 1))
                if i:
                    act.wait_ge(y_ready.sem, y_ready.after(l, i))
                    act.wait_ge(ssm_new.sem, ssm_new.after(l, i))
                    act.wait_ge(spn_ready.sem, spn_ready.after(l, i))
                nc.scalar.activation(ST[:].rearrange("p n h t -> p (n h t)"), PS[:, 4, :], ACT.Exp).then_inc(e_ready.sem, 1)
                nc.scalar.activation(STS[:].rearrange("p h t -> p (h t)"), PS[0:NS, 5, 0:P], ACT.Exp).then_inc(e_ready.sem, 1)
                nc.scalar.activation(EC[:], PS[:, 5, P:P + T], ACT.Exp).then_inc(e_ready.sem, 1)
                act.wait_ge(hts_turned.sem, hts_turned.after(l, i + 1))
                if i:
                    act.wait_ge(y2_ready.sem, y2_ready.after(l, i))
                copy(HTS[:].rearrange("p (c b) n -> p c (b n)", c=2), PS[:, 6:8, :]).then_inc(hts_ready.sem, 1)
                act.wait_ge(spn_ready.sem, spn_ready.after(l, i + 1))
                act.dma_start(o["ssm_prompt"][ds(l, 1), 0, 2 * i:2 * i + 2].rearrange("o h p n -> (o h p) n"),
                              SP[:, i % 2, :]).then_inc(sp_stored[i % 2].sem, 16)
                act.wait_ge(ssm_new.sem, ssm_new.after(l, i + 1))
                act.dma_start(o["ssm_sample"][ds(l, 1), :, 2 * i:2 * i + 2].rearrange("o b h p n -> (h p) (o b) n"),
                              SIN[i % 2][:]).then_inc(ms_stored[i % 2].sem, 16)
                if i + 2 < PAIRS:
                    ssm_state_in(l, i + 2)
            for g in range(2):
                act.wait_ge(yz_ready.sem, yz_ready.after(l, g + 1))
                nc.scalar.activation(SQS[:, 4 * g:4 * g + 4], Z[:, 4 * g:4 * g + 4], ACT.Square).then_inc(sqs_ready.sem, 1)
            act.wait_ge(sstat_ready.sem, sstat_ready.after(l, 1))
            nc.scalar.activation(SQS[:, 0:2], PS[:, 4:6, 0:T], ACT.Sqrt, bias=EPST[:], scale=2.0 / D).then_inc(sroot_ready.sem, 1)
            act.wait_ge(co_stored.sem, co_stored.after(l, 32))
            for c in range(4):
                act.wait_ge(ysn_ready.sem, ysn_ready.after(l, 2 * c + 2))
                copy(HH[:, 8 + 2 * c:10 + 2 * c, :], Z[:, 2 * c:2 * c + 2]).then_inc(yh_ready.sem, 1)
            for s in (0, 1):
                act.wait_ge(ms_stored[s].sem, ms_stored[s].after(l, 64))
                act.wait_ge(sp_stored[s].sem, sp_stored[s].after(l, 64))
            act.wait_ge(s2_stored.sem, s2_stored.after(l, 32))
            with act.Fori(0, 4) as i:
                split_hi(l, unit(U_OUT + 2, i))
                split_hi(l, unit(U_OUT + 3, i))

        with act.Fori(0, LAYERS) as l:
            act.dma_start(WDT[:], a["w_in"][ds(l, 1), :, COL_DT:COL_DT + MH].rearrange("o (k p) h -> p (o k) h", p=P)
                          ).then_inc(wdt_in.sem, 16)
            split_hi(l, unit(0))
            split_hi(l, unit(1))
            pre_norm(l, 0)
            ffn(l, 0, U_UP1, U_DOWN1)
            post_norm(l, 0, U_DOWN1 + 10)
            pre_norm(l, 1)
            with act.Fori(0, 2) as g:
                hgrn(l, g)
            mamba(l)
            post_norm(l, 1, U_OUT + 7)
            pre_norm(l, 2)
            ffn(l, 1, U_UP2, U_DOWN2)
            post_norm(l, 2, U_DOWN2 + 10)
        for n, (t0, tn) in enumerate(TILES):
            act.wait_ge(yout_turned.sem, n + 1)
            copy(YROW[0:tn, n, :].rearrange("p (b c) -> p b c", b=2), PS[0:tn, 2 * n:2 * n + 2, :]).then_inc(yout_ready.sem, 1)

    @block.vector
    def _(dve):
        V = nc.vector

        def split_lo(l, u):
            slot, n, _ = u
            dve.wait_ge(hi_ready.sem, hi_ready.after(l, n) + 1)
            V.tensor_tensor(WL[:, slot, :], RAW[:, slot, :], WH[:, slot, :].bitcast(F32), ALU.subtract).then_inc(lo_ready.sem, 1)

        def ahead(u):
            return u[0], u[1] + 2, u[2] + 1

        for s in (lo_ready, h_ready, z_ready):
            for _ in range(2):
                V.memset(FREEV[:], 0.0).then_inc(s.sem, 1)
                dve.wait_ge(s.sem, 1 + _)
        V.memset(FREEV[:], 0.0).then_inc(ohg_ready.sem, 1)
        dve.wait_ge(ohg_ready.sem, 1)
        V.memset(FREEV[:], 0.0).then_inc(ohl_ready.sem, 1)
        V.memset(ONES[:], 1.0).then_inc(const_step.sem, 1)
        V.memset(EPST[:], EPS).then_inc(const_step.sem, 1)
        dve.wait_ge(iota_done.sem, 3)
        V.tensor_tensor(IX[:], IT[:], IS[:], ALU.bitwise_xor).then_inc(const_step.sem, 1)
        V.tensor_tensor(FIT[:], IT[:], IS[:], ALU.subtract).then_inc(const_step.sem, 1)
        dve.wait_ge(const_step.sem, 4)
        V.tensor_copy(FIX[:], IX[:]).then_inc(const_step.sem, 1)
        V.tensor_scalar(IDENT[:], FIT[:], 0.0, None, ALU.is_equal).then_inc(const_step.sem, 1)
        V.tensor_scalar(TRI[:], FIT[:], 0.0, None, ALU.is_ge).then_inc(const_step.sem, 1)
        V.tensor_scalar(USTR[:], FIT[:], 0.0, None, ALU.is_lt).then_inc(const_step.sem, 1)
        dve.wait_ge(const_step.sem, 8)
        V.scalar_tensor_tensor(TRI8[:], FIX[0:NS, 0:NS], 8.0, TRI[0:NS, 0:NS], ALU.is_lt, ALU.mult).then_inc(const_step.sem, 1)
        V.scalar_tensor_tensor(USTR8[:], FIX[0:NS, 0:NS], 8.0, USTR[0:NS, 0:NS], ALU.is_lt, ALU.mult).then_inc(const_step.sem, 1)
        V.tensor_tensor(FIT[:], FIX[:], TRI[:], ALU.mult).then_inc(const_step.sem, 1)
        dve.wait_ge(const_step.sem, 11)
        for i in range(8):
            V.tensor_scalar(FGE[:, i], FIT[:], float(1 << i), None, ALU.is_ge).then_inc(const_step.sem, 1)
        dve.wait_ge(const_step.sem, 19)
        V.tensor_copy(MASK[:, 0], IDENT[:]).then_inc(const_step.sem, 1)
        V.tensor_tensor(MASK[:, 1:8], FGE[:, 0:7], FGE[:, 1:8], ALU.subtract).then_inc(const_step.sem, 1)
        V.tensor_scalar(FB[:, 0], IBK[:], 0.0, None, ALU.is_ge).then_inc(const_step.sem, 1)
        V.tensor_scalar(FB[:, 1], IBK[:], float(SL), None, ALU.is_ge).then_inc(const_step.sem, 1)
        dve.wait_ge(const_step.sem, 23)
        V.tensor_tensor(BLK[:], FB[:, 0], FB[:, 1], ALU.subtract).then_inc(consts_done.sem, 1)
        dve.wait_ge(params_in.sem, 16 * 12)
        dve.wait_ge(params_turned.sem, 1)
        pa = PS[:, 6, 0:2 * NROW_A].rearrange("p (l c) -> p l c", l=2)
        V.tensor_copy(PALL[:, :, 0:C_CW], pa[:, :, 0:C_CW]).then_inc(params_done.sem, 1)
        V.tensor_copy(LBW[:, 0:2], pa[:, :, C_CW:NROW_A]).then_inc(params_done.sem, 1)
        V.tensor_copy(PALL[:, :, C_CW:C_LBF], PS[:, 7, 0:96].rearrange("p (l c) -> p l c", l=2)).then_inc(params_done.sem, 1)
        dve.wait_ge(params_done.sem, 3)
        V.tensor_scalar(PALL[:, :, C_GAIN + 8:C_GAIN + 16], PALL[:, :, C_GAIN + 8:C_GAIN + 16], 0.5, None, ALU.mult).then_inc(params_done.sem, 1)
        V.tensor_scalar(PALL[:, :, C_GAIN + 40:C_GAIN + 48], PALL[:, :, C_GAIN + 40:C_GAIN + 48], 0.5, None, ALU.mult).then_inc(params_done.sem, 1)
        V.tensor_tensor(LBW[:, 2], LBW[:, 0], LBW[:, 1], ALU.max).then_inc(lb_step.sem, 1)
        dve.wait_ge(lb_step.sem, 1)
        V.tensor_tensor(LBW[:, 3], LBW[:, 0], LBW[:, 2], ALU.subtract).then_inc(lb_step.sem, 1)
        V.tensor_tensor(LBW[:, 4], LBW[:, 1], LBW[:, 2], ALU.subtract).then_inc(lb_step.sem, 1)
        dve.wait_ge(lb_exp.sem, 2)
        V.tensor_tensor(LBW[:, 5], LBW[:, 3], LBW[:, 4], ALU.add).then_inc(lb_step.sem, 1)
        dve.wait_ge(lb_step.sem, 4)
        V.reciprocal(LBW[:, 6], LBW[:, 5]).then_inc(lb_step.sem, 1)
        dve.wait_ge(lb_step.sem, 5)
        V.tensor_tensor(LBW[:, 3], LBW[:, 3], LBW[:, 6], ALU.mult).then_inc(lb_step.sem, 1)
        V.tensor_tensor(LBW[:, 4], LBW[:, 4], LBW[:, 6], ALU.mult).then_inc(lb_step.sem, 1)
        dve.wait_ge(lb_step.sem, 7)
        V.tensor_tensor(LBW[:, 5], LBW[:, 3], LBW[:, 4], ALU.add).then_inc(lb_step.sem, 1)
        V.tensor_tensor(LBW[:, 0], LBW[:, 3], LBW[:, 3], ALU.subtract).then_inc(lb_step.sem, 1)
        dve.wait_ge(lb_step.sem, 9)
        V.tensor_tensor(LBW[:, 1], LBW[:, 5], LBW[:, 3], ALU.subtract).then_inc(lb_step.sem, 1)
        dve.wait_ge(lb_step.sem, 10)
        V.tensor_scalar(PALL[:, :, C_LBF:C_LBF + 8], LBW[:, 0:2], LB_FLOOR, None, ALU.max).then_inc(lb_step.sem, 1)
        V.tensor_scalar(PALL[:, :, C_OML:C_OML + 8], LBW[:, 0:2], -1.0, 1.0, ALU.mult, ALU.add).then_inc(lb_step.sem, 1)
        V.tensor_scalar(PALL[:, :, C_A:C_A + MH], PALL[:, :, C_A:C_A + MH], -1.0, None, ALU.mult).then_inc(lb_step.sem, 1)
        dve.wait_ge(lb_step.sem, 13)
        dve.wait_ge(params_done.sem, 5)

        def pre_norm(l, i):
            dve.wait_ge(root_ready.sem, root_ready.after(l, 2 * i + 1))
            V.reciprocal(RINV[:], ROOT[:]).then_inc(rinv_ready.sem, 1)
            dve.wait_ge(rinv_ready.sem, rinv_ready.after(l, 2 * i + 1))
            for k in range(DT_):
                V.scalar_tensor_tensor(XN[:, k], X[:, k], gain(2 * i, k), RINV[:], ALU.mult, ALU.mult).then_inc(xn_ready.sem, 1)
            for c in range(4):
                dve.wait_ge(xh_ready.sem, xh_ready.after(l, 4 * i + c + 1))
                V.tensor_tensor(XL[:, 2 * c:2 * c + 2], XN[:, 2 * c:2 * c + 2], XH[:, 2 * c:2 * c + 2].bitcast(F32),
                                ALU.subtract).then_inc(xl_ready.sem, 1)

        def post_norm(l, i):
            for c in range(4):
                dve.wait_ge(ms_ready.sem, ms_ready.after(l, 4 * i + c + 1))
                V.tensor_tensor(SQ[:, 2 * c:2 * c + 2], MS[:, 2 * c:2 * c + 2], MS[:, 2 * c:2 * c + 2], ALU.mult).then_inc(postsq_ready.sem, 1)
            dve.wait_ge(root_ready.sem, root_ready.after(l, 2 * i + 2))
            V.reciprocal(RINV[:], ROOT[:]).then_inc(rinv_ready.sem, 1)
            dve.wait_ge(rinv_ready.sem, rinv_ready.after(l, 2 * i + 2))
            for k in range(DT_):
                V.scalar_tensor_tensor(MS[:, k], MS[:, k], gain(2 * i + 1, k), RINV[:], ALU.mult, ALU.mult).then_inc(scaled_ready.sem, 1)
            for c in range(4):
                dve.wait_ge(scaled_ready.sem, scaled_ready.after(l, 8 * i + 2 * c + 2))
                V.tensor_tensor(X[:, 2 * c:2 * c + 2], X[:, 2 * c:2 * c + 2], MS[:, 2 * c:2 * c + 2], ALU.add).then_inc(x_ready.sem, 1)

        def ffn(l, f, up, down):
            def pair(j, par, hl, gate, up_):
                split_lo(l, ahead(gate))
                dve.wait_ge(sg_ready.sem, sg_ready.after(l, j) + 1)
                dve.wait_ge(unit_done.sem, unit_done.after(l, up_[1]) + 1)
                V.tensor_tensor(HF[:, par], SG[:, par], PS[:, 4 * par + 2:4 * par + 4, 0:T], ALU.mult).then_inc(h_ready.sem, 1)
                split_lo(l, ahead(up_))
                dve.wait_ge(hh_ready.sem, hh_ready.after(l, j) + 1)
                V.tensor_tensor(HL[:, hl, :], HF[:, par], HH[:, hl, :].bitcast(F32), ALU.subtract).then_inc(hl_ready.sem, 1)

            with dve.Fori(0, 5) as i:
                for s in range(2):
                    pair(i * 2 + (11 * f + s), s, ds(i * 4 + 2 * s, 2), unit(up + 2 * s, i, 4), unit(up + 2 * s + 1, i, 4))
            pair(11 * f + 10, 0, slice(20, 22), unit(up + 20), unit(up + 21))
            with dve.Fori(0, 4) as i:
                split_lo(l, unit(down + 2, i))
                split_lo(l, unit(down + 3, i))
            split_lo(l, unit(down + 10))
            if f == 0:
                split_lo(l, unit(down + 11))
                split_lo(l, unit(down + 12))

        def halves(buf, m):
            if m <= 4:
                v = buf.rearrange("p h t -> p (h t)").rearrange("p (n two m) -> p n two m", two=2, m=m)
                return v[:, :, 0, :], v[:, :, 1, :]
            v = buf[:, :, 0:SEQ].rearrange("p h (n two m) -> p h n two m", two=2, m=m)
            return v[:, :, :, 0, :], v[:, :, :, 1, :]

        def last(half, m):
            return (half[:, :, m - 1:m] if len(half.shape) == 3 else half[:, :, :, m - 1:m]).broadcast_to(list(half.shape))

        def pick(l, g, i):
            b = 3 * (i % 2)
            for n in range(2):
                q = V.copy_predicated(APR[:, n], MASK[:, i:i + 1, :].broadcast_to([P, HG, P]),
                                      PS[:, b + n, :].rearrange("p (h t) -> p h t", t=P))
            if i < 4:
                q = V.copy_predicated(ASM[:], MASK[0:NS, i:i + 1, 0:NS].broadcast_to([NS, HG, NS]),
                                      PS[0:NS, b + 2, 0:HG * NS].rearrange("p (h t) -> p h t", t=NS))
            q.then_inc(picked.sem, 1)

        def hgrn(l, g):
            for c in range(8):
                split_lo(l, ahead(unit(U_IN + c, g, 8)))
                if c in (1, 3):
                    for h in (c - 1, c):
                        dve.wait_ge(fsig_ready.sem, fsig_ready.after(l, g * 4 + c + 1))
                        w = [PAR[:, ds(g * 4 + (b + h), 1)] for b in (C_OML, C_LBF)]
                        V.tensor_scalar(PRE[:, h], PRE[:, h], w[0], w[1], ALU.mult, ALU.add).then_inc(fk_ready.sem, 1)
                        V.tensor_scalar(KF[:, h], KF[:, h], w[0], None, ALU.mult).then_inc(fk_ready.sem, 1)
            dve.wait_ge(hgz_ready.sem, hgz_ready.after(l, g * 3 + 3))
            dve.wait_ge(fk_ready.sem, fk_ready.after(l, g * 8 + 8))
            dve.wait_ge(q_ready.sem, q_ready.after(l, g * 2 + 2))
            for i, m in enumerate(LEVELS, 1):
                w1, w2 = halves(W[:, i % 2], m)
                k1, _ = halves(KF[:], m)
                _, q2 = halves(QF[:], m)
                s1, _ = halves(SUF[:], m)
                p1, p2 = halves(PRE[:], m)
                if i > 1:
                    dve.wait_ge(tree_ready.sem, tree_ready.after(l, g * 14 + 2 * (i - 1)))
                V.tensor_tensor(w1, k1, s1, ALU.mult).then_inc(w_ready.sem, 1)
                V.tensor_tensor(w2, q2, p2, ALU.mult).then_inc(w_ready.sem, 1)
                V.tensor_tensor(s1, s1, last(p2, m), ALU.mult).then_inc(tree_ready.sem, 1)
                dve.wait_ge(tree_ready.sem, tree_ready.after(l, g * 14 + 2 * i - 1))
                dve.wait_ge(score_ready.sem, score_ready.after(l, g * 8 + i))
                V.tensor_tensor(p2, p2, last(p1, m), ALU.mult).then_inc(tree_ready.sem, 1)
                pick(l, g, i - 1)
            dve.wait_ge(tree_ready.sem, tree_ready.after(l, g * 14 + 14))
            V.tensor_tensor(W[:, 0], QF[:], PRE[:], ALU.mult).then_inc(w_ready.sem, 1)
            dve.wait_ge(picked.sem, picked.after(l, g * 8 + 7))
            dve.wait_ge(score_ready.sem, score_ready.after(l, g * 8 + 8))
            V.tensor_tensor(W[:, 1], KF[:], SUF[:], ALU.mult).then_inc(w_ready.sem, 1)
            pick(l, g, 7)
            dve.wait_ge(sp2_ready.sem, sp2_ready.after(l, g + 1))
            dve.wait_ge(s1_ready.sem, s1_ready.after(l, g + 1))
            dve.wait_ge(s2_stored.sem, s2_stored.after(l, g * 16))
            for h in range(HG):
                q = V.scalar_tensor_tensor(S2[:, h], S1[:, h], PRE[:, h, SEQ - 1:SEQ], PS[:, 5, h * KD:(h + 1) * KD], ALU.mult, ALU.add)
            q.then_inc(s2_ready.sem, 1)
            for h in range(HG):
                dve.wait_ge(decayed.sem, decayed.after(l, g * 4 + h + 1))
                dve.wait_ge(upd_ready.sem, upd_ready.after(l, g * 4 + h + 1))
                s = SIN[h % 2][:].rearrange("p (c b) v -> p c (b v)", c=2)
                V.tensor_tensor(s, s, PS[:, 6:8, :], ALU.add).then_inc(snew_ready.sem, 1)
            dve.wait_ge(oroot_ready.sem, oroot_ready.after(l, g + 1))
            V.reciprocal(RTO[:], RTO[:]).then_inc(orinv_ready.sem, 1)
            dve.wait_ge(orinv_ready.sem, orinv_ready.after(l, g + 1))
            dve.wait_ge(go_ready.sem, go_ready.after(l, g * 2 + 2))
            V.tensor_tensor(GO[:], GO[:], RTO[:], ALU.mult).then_inc(gor_ready.sem, 1)
            dve.wait_ge(gor_ready.sem, gor_ready.after(l, g + 1))
            for h in range(HG):
                V.scalar_tensor_tensor(SQO[:, h], PS[:, h, 0:T], PAR[:, ds(g * 4 + (C_HGN + h), 1)], GO[:, h],
                                       ALU.mult, ALU.mult).then_inc(ohg_ready.sem, 1)
            dve.wait_ge(ohh_ready.sem, ohh_ready.after(l, g + 1))
            V.tensor_tensor(HL[:, ds(g * 4, 4), :], SQO[:], HH[:, ds(g * 4, 4), :].bitcast(F32), ALU.subtract).then_inc(ohl_ready.sem, 1)

        def dt_first(l):
            dve.wait_ge(dtp_ready.sem, dtp_ready.after(l, 1))
            for r, n in ROWS:
                V.tensor_tensor(DTW[r, 0, n], PS[r, 7, 0:48].rearrange("p (n h) -> p n h", h=MH)[:, n],
                                PAR[r, C_DTB:C_DTB + MH].rearrange("p (o h) -> p o h", o=1).broadcast_to([r.stop, n.stop - n.start, MH]),
                                ALU.add).then_inc(dt_step.sem, 1)
            dve.wait_ge(dt_step.sem, dt_step.after(l, 2))
            for r, n in ROWS:
                V.scalar_tensor_tensor(DTW[r, 1, n], DTW[r, 0, n], -1.0, DTW[r, 0, n], ALU.mult, ALU.min).then_inc(dt_step.sem, 1)

        def dt_rest(l):
            def step(k, f):
                dve.wait_ge(dt_step.sem, dt_step.after(l, 2 * k))
                for r, n in ROWS:
                    f(r, n).then_inc(dt_step.sem, 1)
            dve.wait_ge(dt_exp.sem, dt_exp.after(l, 4))
            step(2, lambda r, n: V.tensor_scalar(DTW[r, 1, n], DTW[r, 2, n], 1.0, -1.0, ALU.add, ALU.add))
            step(3, lambda r, n: V.tensor_scalar(DTW[r, 4, n], DTW[r, 1, n], 1e-30, None, ALU.max))
            step(4, lambda r, n: V.reciprocal(DTW[r, 4, n], DTW[r, 4, n]))
            step(5, lambda r, n: V.tensor_tensor(DTW[r, 3, n], DTW[r, 3, n], DTW[r, 4, n], ALU.mult))
            step(6, lambda r, n: V.scalar_tensor_tensor(DTW[r, 3, n], DTW[r, 1, n], 0.0, DTW[r, 3, n], ALU.is_equal, ALU.add))
            step(7, lambda r, n: V.tensor_tensor(DTW[r, 3, n], DTW[r, 3, n], DTW[r, 2, n], ALU.mult))
            step(8, lambda r, n: V.scalar_tensor_tensor(DTT[r, n], DTW[r, 0, n], 0.0, DTW[r, 3, n], ALU.max, ALU.add))
            step(9, lambda r, n: V.tensor_tensor(
                AT[r, n], DTT[r, n],
                PAR[r, C_A:C_A + MH].rearrange("p (o h) -> p o h", o=1).broadcast_to([r.stop, n.stop - n.start, MH]), ALU.mult))

        def masked_a(l, i):
            if i:
                dve.wait_ge(seg_ready.sem, seg_ready.after(l, i))
            V.tensor_tensor(L1[:], USTR[:].rearrange("p (n h s) -> p n h s", n=1, h=1).broadcast_to([P, 2, 2, P]),
                            AT[:, 0:2, 2 * i:2 * i + 2].rearrange("p n (h o) -> p n h o", o=1).broadcast_to([P, 2, 2, P]),
                            ALU.mult).then_inc(l1_ready.sem, 1)
            V.tensor_tensor(L1S[:], USTR8[:].rearrange("p (h s) -> p h s", h=1).broadcast_to([NS, 2, NS]),
                            AT[0:NS, 2, 2 * i:2 * i + 2].rearrange("p (h o) -> p h o", o=1).broadcast_to([NS, 2, NS]),
                            ALU.mult).then_inc(l1_ready.sem, 1)

        def mamba(l):
            with dve.Fori(0, 5) as i:
                split_lo(l, unit(U_IN + 18, i))
                split_lo(l, unit(U_IN + 19, i))
            for q in range(3):
                for j in range(3):
                    for c in range(4):
                        k = 4 * q + c
                        if j == 0:
                            dve.wait_ge(acc_ready.sem, acc_ready.after(l, k + 1))
                        else:
                            dve.wait_ge(tap_ready.sem, tap_ready.after(l, 12 * q + 4 * (j - 1) + c + 1))
                        V.scalar_tensor_tensor(ACC[:, c, 0:CVW], XB[:, k, j:j + CVW], col(C_CW + CT * j + k), ACC[:, c, 0:CVW],
                                               ALU.mult, ALU.add).then_inc(tap_ready.sem, 1)
            dt_rest(l)
            dve.wait_ge(dt_step.sem, dt_step.after(l, 20))
            for j, n in enumerate(TURNS):
                tn = TILES[n][1]
                dve.wait_ge(xturn_ready.sem, xturn_ready.after(l, j + 1))
                b = 3 if j == 1 else 0
                V.tensor_tensor(DTX[0:tn, n, :].rearrange("p (h d) -> p h d", d=HD),
                                PS[0:tn, b:b + 2, :].rearrange("p b (h d) -> p (b h) d", d=HD),
                                DTT[0:tn, n, :].rearrange("p (h o) -> p h o", o=1).broadcast_to([tn, MH, HD]),
                                ALU.mult).then_inc(dtx_ready.sem, 1)
                dve.wait_ge(g_ready.sem, g_ready.after(l, j + 1))
                tri = TRI if n < 2 else TRI8
                V.tensor_tensor(GM[0:tn, n, :, 0:tn], PS[0:tn, 6 + j % 2, 0:2 * P].rearrange("p (g t) -> p g t", g=2)[:, :, 0:tn],
                                tri[:].rearrange("p (o t) -> p o t", o=1).broadcast_to([tn, 2, tn]), ALU.mult).then_inc(gm_ready.sem, 1)
            dve.wait_ge(gm_ready.sem, gm_ready.after(l, 3))
            masked_a(l, 0)
            for i in range(PAIRS):
                g = i // 4
                dve.wait_ge(e_ready.sem, e_ready.after(l, 3 * i + 3))
                V.tensor_tensor(ST[:], ST[:], GM[:, 0:2, g:g + 1, :].broadcast_to([P, 2, 2, P]), ALU.mult).then_inc(st_ready.sem, 1)
                V.tensor_tensor(STS[:], STS[:], GM[0:NS, 2, g:g + 1, 0:NS].broadcast_to([NS, 2, NS]), ALU.mult).then_inc(st_ready.sem, 1)
                if i + 1 < PAIRS:
                    masked_a(l, i + 1)
                dve.wait_ge(y_ready.sem, y_ready.after(l, i + 1))
                V.scalar_tensor_tensor(XC[:, i], XC[:, i], col(C_DSK + i), PS[:, i % 2, 0:T], ALU.mult, ALU.add).then_inc(ystep.sem, 1)
                dve.wait_ge(sp_stored[i % 2].sem, sp_stored[i % 2].after(l, i // 2 * 16))
                V.tensor_copy(SP[:, i % 2], PS[:, i % 2, T:T + P]).then_inc(spc_ready.sem, 1)
                dve.wait_ge(y2_ready.sem, y2_ready.after(l, i + 1))
                V.tensor_tensor(Y2[:, P:T], PS[:, 2 + i % 2, P:T], EC[:, P:T], ALU.mult).then_inc(ystep.sem, 1)
                dve.wait_ge(spc_ready.sem, spc_ready.after(l, i + 1))
                V.scalar_tensor_tensor(SP[:, i % 2], SP[:, i % 2], EC[:, SEQ - 1:SEQ], PS[:, 2 + i % 2, 0:P],
                                       ALU.mult, ALU.add).then_inc(spn_ready.sem, 1)
                dve.wait_ge(ystep.sem, ystep.after(l, 2 * i + 2))
                V.tensor_tensor(XC[:, i, P:T], XC[:, i, P:T], Y2[:, P:T], ALU.add).then_inc(ydone.sem, 1)
                dve.wait_ge(supd_ready.sem, supd_ready.after(l, i + 1))
                s = SIN[i % 2]
                for b in range(NB):
                    e = SEQ + SL * b + SL - 1
                    q = V.scalar_tensor_tensor(s[:, b], s[:, b], EC[:, e:e + 1], PS[:, 6 + b // 4, (b % 4) * P:(b % 4 + 1) * P],
                                               ALU.mult, ALU.add)
                q.then_inc(ssm_new.sem, 1)
            dve.wait_ge(z_ready.sem, z_ready.after(l, 4))
            dve.wait_ge(ydone.sem, ydone.after(l, PAIRS))
            for g in range(2):
                V.tensor_tensor(Z[:, 4 * g:4 * g + 4], XC[:, 4 * g:4 * g + 4], Z[:, 4 * g:4 * g + 4], ALU.mult).then_inc(yz_ready.sem, 1)
            dve.wait_ge(sroot_ready.sem, sroot_ready.after(l, 1))
            V.reciprocal(SQS[:, 0:2], SQS[:, 0:2]).then_inc(srinv_ready.sem, 1)
            dve.wait_ge(srinv_ready.sem, srinv_ready.after(l, 1))
            for k in range(PAIRS):
                V.scalar_tensor_tensor(Z[:, k], Z[:, k], col(C_SSN + k), SQS[:, k // 4], ALU.mult, ALU.mult).then_inc(ysn_ready.sem, 1)
            for c in range(4):
                dve.wait_ge(yh_ready.sem, yh_ready.after(l, c + 1))
                V.tensor_tensor(HL[:, 8 + 2 * c:10 + 2 * c, :], Z[:, 2 * c:2 * c + 2], HH[:, 8 + 2 * c:10 + 2 * c, :].bitcast(F32),
                                ALU.subtract).then_inc(yl_ready.sem, 1)
            with dve.Fori(0, 4) as i:
                split_lo(l, unit(U_OUT + 2, i))
                split_lo(l, unit(U_OUT + 3, i))

        with dve.Fori(0, LAYERS) as l:
            V.tensor_copy(PAR[:].rearrange("p (o c) -> p o c", o=1), PALL[:, ds(l, 1), :]).then_inc(par_ready.sem, 1)
            split_lo(l, unit(0))
            split_lo(l, unit(1))
            dve.wait_ge(par_ready.sem, par_ready.after(l, 1))
            pre_norm(l, 0)
            ffn(l, 0, U_UP1, U_DOWN1)
            post_norm(l, 0)
            pre_norm(l, 1)
            dt_first(l)
            with dve.Fori(0, 2) as g:
                hgrn(l, g)
            mamba(l)
            post_norm(l, 1)
            pre_norm(l, 2)
            ffn(l, 1, U_UP2, U_DOWN2)
            post_norm(l, 2)

    @block.tensor
    def _(pe):
        pe.wait_ge(consts_done.sem, 1)
        pe.wait_ge(x_rows_in.sem, 32)
        for n, (t0, tn) in enumerate(TILES):
            for k in range(DT_):
                c = (k % 4) * P
                q = pe.transpose(PS[:, 2 * n + k // 4, c:c + tn], XROW[0:tn, n, k * P:(k + 1) * P], IDENT[0:tn, 0:tn])
            q.then_inc(x_turned.sem, 1)
        pe.wait_ge(params_in.sem, 16 * 12)
        for l in range(LAYERS):
            pe.transpose(PS[:, 6, l * NROW_A:(l + 1) * NROW_A], PROWA[:, l, :], IDENT[0:NROW_A, 0:NROW_A])
            q = pe.transpose(PS[:, 7, l * 48:(l + 1) * 48], PROWB[:, l, :], IDENT[0:48, 0:48])
        q.then_inc(params_turned.sem, 1)
        pe.wait_ge(x_ready.sem, x_ready.before)
        for s, n in ((unit_done, 2), (xb_ready, 4)):
            for _ in range(n):
                pe.matmul(PS[:, 5, 0:8], ONES[:], ONES[:, 0:8], start=True, stop=True).then_inc(s.sem, 1)

        def dense(out, slot, c, hi, lo, first, last_):
            wh, wl = WH[:, slot, c:c + P], WL[:, slot, c:c + P]
            pe.matmul(out, wh, hi, start=first, stop=False)
            pe.matmul(out, wh, lo, start=False, stop=False)
            return pe.matmul(out, wl, hi, start=False, stop=last_)

        def by_columns(l, u, banks):
            slot, n, _ = u
            pe.wait_ge(lo_ready.sem, lo_ready.after(l, n) + 1)
            for s, b in enumerate(banks):
                for k in range(DT_):
                    q = dense(PS[:, b, 0:T], slot, k * 256 + s * P, XH[:, k], XL[:, k], k == 0, k == DT_ - 1)
            q.then_inc(unit_done.sem, 1)

        def by_rows(l, u, k, first=False, last_=False):
            slot, n, _ = u
            pe.wait_ge(lo_ready.sem, lo_ready.after(l, n) + 1)
            for kk in range(2):
                hi, lo = ((HH[:, k + kk, :], HL[:, k + kk, :]) if isinstance(k, int) else
                          (HH[:, ds(k + kk, 1), :].rearrange("p o t -> p (o t)"), HL[:, ds(k + kk, 1), :].rearrange("p o t -> p (o t)")))
                for m in range(DT_):
                    q = dense(PS[:, m, 0:T], slot, kk * D + m * P, hi, lo, first and kk == 0, last_ and kk == 1)
            q.then_inc(unit_done.sem, 1)

        def stat(l, n, sem, per_tile):
            for k in range(DT_):
                if k % 2 == 0:
                    pe.wait_ge(sem.sem, sem.after(l, per_tile + k // 2 + 1))
                q = pe.matmul(PS[:, 0, 0:T], ONES[:], SQ[:, k], start=(k == 0), stop=(k == DT_ - 1))
            q.then_inc(stat_ready.sem, 1)

        def ffn(l, f, up, down):
            with pe.Fori(0, 5) as i:
                pe.wait_ge(xl_ready.sem, xl_ready.after(l, 8 * f + 4))
                for s in range(2):
                    pe.wait_ge(h_ready.sem, h_ready.after(l, i * 2 + (11 * f + s)) + (1 - 2))
                    by_columns(l, unit(up + 2 * s, i, 4), (4 * s, 4 * s + 1))
                    by_columns(l, unit(up + 2 * s + 1, i, 4), (4 * s + 2, 4 * s + 3))
            pe.wait_ge(h_ready.sem, h_ready.after(l, 11 * f + 9))
            by_columns(l, unit(up + 20), (0, 1))
            by_columns(l, unit(up + 21), (2, 3))
            pe.wait_ge(hl_ready.sem, hl_ready.after(l, 11 * f + 11))
            by_rows(l, unit(down), 0, first=True)
            with pe.Fori(0, 4) as i:
                by_rows(l, unit(down + 1, i), i * 4 + 2)
                by_rows(l, unit(down + 2, i), i * 4 + 4)
            by_rows(l, unit(down + 9), 18)
            by_rows(l, unit(down + 10), 20, last_=True)
            stat(l, 2 * f, postsq_ready, 8 * f)

        def scores(l, g, i):
            b = 3 * (i % 2)
            lhs, rhs = (KF[:], QF[:]) if i == 0 else (W[:, i % 2], W[:, i % 2])
            for h in range(HG):
                for n, (t0, tn) in enumerate(TILES if i < 4 else TILES[:2]):
                    q = pe.matmul(PS[0:tn, b + n, h * tn:(h + 1) * tn], lhs[:, h, t0:t0 + tn], rhs[:, h, t0:t0 + tn],
                                  start=True, stop=True)
            q.then_inc(score_ready.sem, 1)

        def turn(src, n, bank, sem):
            t0, tn = TILES[n]
            for h in range(HG):
                q = pe.transpose(PS[0:tn, bank, h * KD:(h + 1) * KD], src[:, h, t0:t0 + tn], IDENT[:])
            q.then_inc(sem.sem, 1)

        def hgrn(l, g):
            pe.wait_ge(xl_ready.sem, xl_ready.after(l, 8))
            pe.wait_ge(ohg_ready.sem, ohg_ready.after(l, g * 4))
            for c in range(8):
                if c == 3:
                    pe.wait_ge(dt_step.sem, dt_step.after(l, 2))
                if c in (4, 5):
                    pe.wait_ge(fsig_ready.sem, fsig_ready.after(l, g * 4 + 2 * (c - 3)))
                if c in (6, 7):
                    pe.wait_ge(q_ready.sem, q_ready.after(l, g * 2 + c - 5))
                by_columns(l, unit(U_IN + c, g, 8), (2 * (c % 4), 2 * (c % 4) + 1))
            pe.wait_ge(v_ready.sem, v_ready.after(l, g * 2 + 2))
            pe.wait_ge(go_ready.sem, go_ready.after(l, g * 2 + 2))
            for j, n in enumerate(TURNS):
                if j == 2:
                    pe.wait_ge(vtok_ready.sem, vtok_ready.after(l, g * 3 + 1))
                turn(VF[:], n, 6 + j % 2, vturn_ready)
            pe.wait_ge(fk_ready.sem, fk_ready.after(l, g * 8 + 8))
            scores(l, g, 0)
            for i in range(1, 8):
                pe.wait_ge(w_ready.sem, w_ready.after(l, g * 16 + 2 * i))
                if i > 1:
                    pe.wait_ge(picked.sem, picked.after(l, g * 8 + i - 1))
                scores(l, g, i)
            pe.wait_ge(vtok_ready.sem, vtok_ready.after(l, g * 3 + 3))
            pe.wait_ge(w_ready.sem, w_ready.after(l, g * 16 + 16))
            for j, n in enumerate(TURNS):
                if j == 2:
                    pe.wait_ge(ktok_ready.sem, ktok_ready.after(l, g * 3 + 1))
                turn(W[:, 1], n, 6 + j % 2, kturn_ready)
            pe.wait_ge(picked.sem, picked.after(l, g * 8 + 8))
            for n, s in enumerate((sp1_ready, sp2_ready)):
                pe.wait_ge(ktok_ready.sem, ktok_ready.after(l, g * 3 + 2 * n + 1))
                for h in range(HG):
                    c = slice(h * KD, (h + 1) * KD)
                    q = pe.matmul(PS[:, 4 + n, c], KTOK[:, n, c], VTOK[:, n, c], start=True, stop=True)
                q.then_inc(s.sem, 1)
            pe.wait_ge(s1_ready.sem, s1_ready.after(l, g + 1))
            for h in range(HG):
                c = slice(h * KD, (h + 1) * KD)
                pe.wait_ge(hs_in[h % 2].sem, hs_in[h % 2].after(l, g * 32 + (h // 2 + 1) * 16))
                pe.matmul(PS[:, h, 0:P], VTOK[:, 0, c], APR[:, 0, h], start=True, stop=True)
                pe.matmul(PS[:, h, P:SEQ], VTOK[:, 1, c], APR[:, 1, h], start=True, stop=False, skip_group_check=True)
                pe.matmul(PS[:, h, P:SEQ], S1[:, h], W[:, 0, h, P:SEQ], start=False, stop=True, skip_group_check=True)
                pe.matmul(PS[:, h, SEQ:T], VTOK[0:NS, 2, c], ASM[:, h], start=True, stop=False, skip_group_check=True)
                for b in range(NB):
                    t = SEQ + SL * b
                    q = pe.matmul(PS[:, h, t:t + SL], SIN[h % 2][:, b], W[:, 0, h, t:t + SL], start=False, stop=(b == NB - 1),
                                  skip_group_check=True)
                q.then_inc(o_ready.sem, 1)
                pe.wait_ge(vm_ready.sem, vm_ready.after(l, g * 4 + h + 1))
                if h:
                    pe.wait_ge(snew_ready.sem, snew_ready.after(l, g * 4 + h))
                else:
                    pe.wait_ge(ktok_ready.sem, ktok_ready.after(l, g * 3 + 3))
                for b in range(2):
                    q = pe.matmul(PS[:, 6 + b, :], KTOK[0:NS, 2, c], VM[:, 4 * b:4 * b + 4, :].rearrange("p b v -> p (b v)"),
                                  start=True, stop=True)
                q.then_inc(upd_ready.sem, 1)
            pe.wait_ge(snew_ready.sem, snew_ready.after(l, g * 4 + 4))
            pe.wait_ge(s2_ready.sem, s2_ready.after(l, g + 1))
            pe.wait_ge(sqo_ready.sem, sqo_ready.after(l, g * 4 + 4))
            for h in range(HG):
                q = pe.matmul(PS[:, 4 + h, 0:T], ONES[:], SQO[:, h], start=True, stop=True)
            q.then_inc(ostat_ready.sem, 1)

        def mamba(l):
            with pe.Fori(0, 3) as i:
                pe.wait_ge(ohg_ready.sem, ohg_ready.after(l, 8))
                for s in range(2):
                    pe.wait_ge(xb_ready.sem, xb_ready.after(l, i * 4 + 2 * s) + (2 - 4))
                    by_columns(l, unit(U_IN + 16 + s, i), (2 * s, 2 * s + 1))
            with pe.Fori(0, 2) as i:
                for s in range(2):
                    pe.wait_ge(z_ready.sem, z_ready.after(l, i * 2 + s) + (1 - 2))
                    if s == 1:
                        pe.wait_ge(xb_ready.sem, xb_ready.after(l, 12))
                        pe.wait_ge(crow_in.sem, crow_in.after(l, 16))
                    by_columns(l, unit(U_IN + 22 + s, i), (4 + 2 * s, 5 + 2 * s))
            for c in range(CT):
                q = pe.transpose(PS[:, 0, c * 24:(c + 1) * 24], CROW[:, c * P:(c + 1) * P], IDENT[0:24, 0:24])
            q.then_inc(cturn_ready.sem, 1)
            pe.wait_ge(dt_step.sem, dt_step.after(l, 20))
            for n, (t0, tn) in enumerate(TILES):
                u = USTR if n < 2 else USTR8
                q = pe.matmul(PS[0:tn, 1, n * MH:(n + 1) * MH], u[:], AT[0:tn, n, :], start=True, stop=True)
            q.then_inc(remp_ready.sem, 1)
            pe.wait_ge(xc_ready.sem, xc_ready.after(l, 6))
            pe.wait_ge(z_ready.sem, z_ready.after(l, 4))
            pe.wait_ge(rem_ready.sem, rem_ready.after(l, 2))
            for j, n in enumerate(TURNS):
                t0, tn = TILES[n]
                b, bb = (3, 5) if j == 1 else (0, 2)
                if j == 2:
                    pe.wait_ge(dtx_ready.sem, dtx_ready.after(l, 1))
                    pe.wait_ge(btok_ready.sem, btok_ready.after(l, 1))
                    pe.wait_ge(gm_ready.sem, gm_ready.after(l, 1))
                for k in range(10):
                    c = (k % 4) * P
                    q = pe.transpose(PS[0:tn, (b + k // 4) if k < 8 else bb, c:c + P], XC[:, k, t0:t0 + tn], IDENT[:])
                q.then_inc(xturn_ready.sem, 1)
                for g in range(2):
                    q = pe.matmul(PS[0:tn, 6 + j % 2, g * P:g * P + tn], XC[:, 8 + g, t0:t0 + tn], XC[:, 10 + g, t0:t0 + tn],
                                  start=True, stop=True)
                q.then_inc(g_ready.sem, 1)
            pe.wait_ge(wx_ready.sem, wx_ready.after(l, 1))
            pe.wait_ge(dtx_ready.sem, dtx_ready.after(l, 3))
            for g in range(2):
                q = pe.matmul(PS[:, g, :], BTOK[:, 0, g * P:(g + 1) * P], WX[:, 0, g * 512:(g + 1) * 512], start=True, stop=True)
            q.then_inc(ht1p_ready.sem, 1)
            pe.wait_ge(gm_ready.sem, gm_ready.after(l, 3))
            pe.wait_ge(btok_ready.sem, btok_ready.after(l, 3))
            pe.wait_ge(cs_ready.sem, cs_ready.after(l, 2))
            for c in range(CT):
                q = pe.transpose(PS[0:27, 5 + c // 4, (c % 4) * P:(c % 4 + 1) * P], CS[:, c, :], IDENT[:])
            q.then_inc(csturn_ready.sem, 1)
            pe.wait_ge(co_ready.sem, co_ready.after(l, 1))
            pe.wait_ge(wx_ready.sem, wx_ready.after(l, 3))
            for i in range(PAIRS):
                g = i // 4
                cc = slice(i * P, (i + 1) * P)
                pe.wait_ge(l1_ready.sem, l1_ready.after(l, 2 * i + 2))
                if i:
                    pe.wait_ge(e_ready.sem, e_ready.after(l, 3 * i))
                for h in range(2):
                    for n in range(2):
                        pe.matmul(PS[:, 4, (2 * n + h) * P:(2 * n + h + 1) * P], L1[:, n, h], TRI[:], start=True, stop=True)
                    pe.matmul(PS[0:NS, 5, h * NS:(h + 1) * NS], L1S[:, h], TRI8[:], start=True, stop=True)
                for n, (t0, tn) in enumerate(TILES):
                    tri = TRI if n < 2 else TRI8
                    for h in range(2):
                        q = pe.matmul(PS[HD * h:HD * h + HD, 5, P + t0:P + t0 + tn],
                                      AT[0:tn, n, 2 * i + h:2 * i + h + 1].broadcast_to([tn, HD]), tri[:], start=True, stop=True)
                q.then_inc(seg_ready.sem, 1)
                pe.wait_ge(ms_in[i % 2].sem, ms_in[i % 2].after(l, (i // 2 + 1) * 16))
                if i:
                    pe.wait_ge(ssm_new.sem, ssm_new.after(l, i))
                for b in range(NB):
                    q = pe.transpose(PS[:, 6 + b // 4, (b % 4) * P:(b % 4 + 1) * P], SIN[i % 2][:, b], IDENT[:])
                q.then_inc(hts_turned.sem, 1)
                pe.wait_ge(st_ready.sem, st_ready.after(l, 2 * i + 2))
                if i < 2:
                    pe.wait_ge(ht1_ready.sem, ht1_ready.after(l, 1))
                else:
                    pe.wait_ge(spc_ready.sem, spc_ready.after(l, i - 1))
                for h in range(2):
                    for n, (t0, tn) in enumerate(TILES):
                        c = (2 * i + h) * HD
                        pe.matmul(PS[HD * h:HD * h + HD, i % 2, t0:t0 + tn], DTX[0:tn, n, c:c + HD],
                                  ST[:, n, h] if n < 2 else STS[:, h], start=True, stop=True)
                pe.matmul(PS[:, i % 2, T:T + P], WX[:, 0, cc], BTOK[:, 0, g * P:(g + 1) * P], start=True, stop=True
                          ).then_inc(y_ready.sem, 1)
                pe.wait_ge(hts_ready.sem, hts_ready.after(l, i + 1))
                if i > 1:
                    pe.wait_ge(spn_ready.sem, spn_ready.after(l, i - 1))
                pe.matmul(PS[:, 2 + i % 2, P:SEQ], HT1[:, cc], XC[:, 10 + g, P:SEQ], start=True, stop=True)
                for b in range(NB):
                    t = SEQ + SL * b
                    pe.matmul(PS[:, 2 + i % 2, t:t + SL], HTS[:, b], XC[:, 10 + g, t:t + SL], start=True, stop=True)
                pe.matmul(PS[:, 2 + i % 2, 0:P], WX[:, 1, cc], BTOK[:, 1, g * P:(g + 1) * P], start=True, stop=True
                          ).then_inc(y2_ready.sem, 1)
                pe.wait_ge(bmk_ready.sem, bmk_ready.after(l, g + 1))
                for b in range(2):
                    q = pe.matmul(PS[:, 6 + b, :], WX[0:NS, 2, cc], BMK[:, 4 * b:4 * b + 4, :].rearrange("p b n -> p (b n)"),
                                  start=True, stop=True)
                q.then_inc(supd_ready.sem, 1)
            for g in range(2):
                pe.wait_ge(sqs_ready.sem, sqs_ready.after(l, g + 1))
                for k in range(4):
                    q = pe.matmul(PS[:, 4 + g, 0:T], ONES[:], SQS[:, 4 * g + k], start=(k == 0), stop=(k == 3))
            q.then_inc(sstat_ready.sem, 1)
            pe.wait_ge(ohl_ready.sem, ohl_ready.after(l, 2))
            pe.wait_ge(yl_ready.sem, yl_ready.after(l, 4))
            by_rows(l, unit(U_OUT), 0, first=True)
            with pe.Fori(0, 3) as i:
                by_rows(l, unit(U_OUT + 1, i), i * 4 + 2)
                by_rows(l, unit(U_OUT + 2, i), i * 4 + 4)
            by_rows(l, unit(U_OUT + 7), 14, last_=True)
            stat(l, 1, postsq_ready, 4)

        with pe.Fori(0, LAYERS) as l:
            stat(l, 0, presq_ready, 0)
            ffn(l, 0, U_UP1, U_DOWN1)
            stat(l, 1, presq_ready, 4)
            pe.wait_ge(xn_ready.sem, xn_ready.after(l, 16))
            pe.wait_ge(wdt_in.sem, wdt_in.after(l, 16))
            for n, (t0, tn) in enumerate(TILES):
                for k in range(DT_):
                    q = pe.matmul(PS[0:tn, 7, n * MH:(n + 1) * MH], XN[:, k, t0:t0 + tn], WDT[:, k], start=(k == 0), stop=(k == DT_ - 1))
            q.then_inc(dtp_ready.sem, 1)
            with pe.Fori(0, 2) as g:
                hgrn(l, g)
            mamba(l)
            stat(l, 2, presq_ready, 8)
            ffn(l, 1, U_UP2, U_DOWN2)
        for n, (t0, tn) in enumerate(TILES):
            pe.wait_ge(x_ready.sem, x_ready.after(LAYERS, 0))
            for k in range(DT_):
                q = pe.transpose(PS[0:tn, 2 * n + k // 4, (k % 4) * P:(k % 4 + 1) * P], X[:, k, t0:t0 + tn], IDENT[:])
            q.then_inc(yout_turned.sem, 1)


_INS = ("x_prompt", "x_sample", "state_hgrn", "state_ssm", "state_conv", "w_in", "hg_lb_logits", "conv_w", "conv_b",
        "dt_bias", "a_log", "d_skip", "hg_norm_w", "ssm_norm_w", "w_out", "ffn1_w_gate", "ffn1_w_up", "ffn1_w_down",
        "ffn2_w_gate", "ffn2_w_up", "ffn2_w_down", "norm_gain")
_OUTS = (("y_prompt", (1, SEQ, D)), ("y_sample", (NB, SL, D)),
         ("hgrn_prompt", (LAYERS, 1, HH_, KD, KD)), ("ssm_prompt", (LAYERS, 1, MH, HD, P)),
         ("conv_prompt", (LAYERS, 1, CW - 1, CT * P)), ("hgrn_sample", (LAYERS, NB, HH_, KD, KD)),
         ("ssm_sample", (LAYERS, NB, MH, HD, P)), ("conv_sample", (LAYERS, NB, CW - 1, CT * P)))


def kernel(**inputs):
    import numpy as np
    import concourse.bacc as bacc
    from concourse.bass_utils import run_bass_kernel_spmd

    nc = bacc.Bacc("TRN2", target_bir_lowering=False, num_devices=1)
    arrays = {name: np.ascontiguousarray(inputs[name]) for name in _INS}
    a = {name: nc.dram_tensor(name, v.shape, F32, kind="ExternalInput").ap() for name, v in arrays.items()}
    o = {name: nc.dram_tensor(name, shape, F32, kind="ExternalOutput").ap() for name, shape in _OUTS}
    trunk(nc, a, o)
    r = run_bass_kernel_spmd(nc, [arrays], core_ids=[0])
    return tuple(r.results[0][name] for name, _ in _OUTS)
```

```python
from contextlib import ExitStack

import concourse.bass as bass
from concourse import mybir

F32 = mybir.dt.float32
F32R = mybir.dt.float32r
I32 = mybir.dt.int32
U8 = mybir.dt.uint8
ACT = mybir.ActivationFunctionType
ALU = mybir.AluOpType
ds = bass.ds

P = 128
LAYERS = 2
D = 1024
DT_ = D // P
SEQ = 256
NB, SL = 8, 8
NS = NB * SL
T = SEQ + NS
FF = 2816
FT = FF // P
KD = 128
HH_ = 8
HG = 4
MH, HD = 16, 64
PAIRS = MH // 2
CT = 12
CW = 4
PADP = CW - 1 + SEQ
PADS = CW - 1 + SL
XBW = PADP + NB * PADS
CVW = XBW - (CW - 1)
D_IN = 6672
COL_Q, COL_F, COL_V, COL_GO, COL_Z, COL_X, COL_DT = 0, 1024, 2048, 3072, 4096, 5120, 6656
EPS = 1e-6
LB_FLOOR = 1e-30
QSCALE = KD ** -0.5

UNIT = 2048
U_UP1 = 0
U_DOWN1 = U_UP1 + FT
U_IN = U_DOWN1 + FT // 2
U_OUT = U_IN + 26
U_UP2 = U_OUT + 8
U_DOWN2 = U_UP2 + FT
UNITS = U_DOWN2 + FT // 2
LEVELS = (1, 2, 4, 8, 16, 32, 64)
BESIDE = (((), (), (0,), (), (1,), (), (2,), (), (3,), (4,), (5,), (6,), (7,)),
          ((), (), (0,), (), (1,), (), (), (), (2,), (3,), (4,), (), (5,)))

C_GAIN, C_HGN, C_SSN, C_CB, C_CW, C_LBF, C_OML, C_DSK, C_DTB, C_A, C_END = (
    0, 48, 56, 64, 76, 124, 132, 140, 148, 164, 180)
NROW_A = 84

TILES = ((0, 128), (128, 128), (256, 64))
TURNS = (0, 2, 1)
ROWS = ((slice(0, 128), slice(0, 2)), (slice(0, 64), slice(2, 3)))


class Signal:

    def __init__(self, ctx, nc, name, per_layer, before=0):
        self.sem = ctx.enter_context(nc.semaphore(name))
        self.per_layer, self.before = per_layer, before

    def after(self, l, n):
        return l * self.per_layer + (n + self.before)


def trunk(nc, a, o):
    with ExitStack() as ctx:
        build(nc, a, o, ctx)


def build(nc, a, o, ctx):
    base = (nc.sbuf_base + 31) // 32 * 32
    top = nc.sbuf_usable_end

    def place(name, shape, dtype, at):
        size = 4 if dtype in (F32, F32R, I32) else 1
        n = size
        for s in shape[1:]:
            n *= s
        assert at + n <= top, (name, at + n, top)
        return nc.alloc_sbuf_tensor_at(name, shape, dtype, offset=at), (at + n + 31) // 32 * 32

    at = base
    X, at = place("X", [P, DT_, T], F32, at)
    at_xh = at
    XH, at = place("XH", [P, DT_, T], F32R, at)
    at_xl = at
    XL, at = place("XL", [P, DT_, T], F32R, at)
    at_hh = at
    HH, at = place("HH", [P, FT, T], F32R, at)
    at_hl = at
    HL, at = place("HL", [P, FT, T], F32R, at)
    RAW, at = place("RAW", [P, 2, UNIT], F32, at)
    WH, at = place("WH", [P, 2, UNIT], F32R, at)
    WL, at = place("WL", [P, 2, UNIT], F32R, at)
    IDENT, at = place("IDENT", [P, P], F32, at)
    ONES, at = place("ONES", [P, P], F32, at)
    TRI, at = place("TRI", [P, P], F32, at)
    USTR, at = place("USTR", [P, P], F32, at)
    TRI8, at = place("TRI8", [NS, NS], F32, at)
    USTR8, at = place("USTR8", [NS, NS], F32, at)
    MASK, at = place("MASK", [P, 8, P], U8, at)
    BLK, at = place("BLK", [NS, NB], F32, at)
    PALL, at = place("PALL", [P, LAYERS, C_END], F32, at)
    PAR, at = place("PAR", [P, C_END], F32, at)
    EPST, at = place("EPST", [P, 1], F32, at)
    FREE, at = place("FREE", [P, 1], F32, at)
    FREEV, at = place("FREEV", [P, 1], F32, at)
    ROOT, at = place("ROOT", [P, T], F32, at)
    RINV, at = place("RINV", [P, T], F32, at)
    WDT, at = place("WDT", [P, DT_, MH], F32, at)
    DTT, at = place("DTT", [P, 3, MH], F32, at)
    DTW, at = place("DTW", [P, 5, 3, MH], F32, at)
    AT, at = place("AT", [P, 3, MH], F32, at)
    REM, at = place("REM", [P, 3, MH], F32, at)
    arena = at

    XROW, e = place("XROW", [P, 3, D], F32, arena)
    PROWA, e = place("PROWA", [NROW_A, LAYERS, P], F32, e)
    PROWB, e = place("PROWB", [48, LAYERS, P], F32, e)
    IT, e = place("IT", [P, P], I32, e)
    IS, e = place("IS", [P, P], I32, e)
    IX, e = place("IX", [P, P], I32, e)
    FIT, e = place("FIT", [P, P], F32, e)
    FIX, e = place("FIX", [P, P], F32, e)
    FGE, e = place("FGE", [P, 8, P], F32, e)
    IBK, e = place("IBK", [NS, NB], I32, e)
    FB, e = place("FB", [NS, 2, NB], F32, e)
    LBW, e = place("LBW", [P, 8, 8], F32, e)
    YROW = XROW

    MS, e = place("MS", [P, DT_, T], F32, arena)
    SQ, e = place("SQ", [P, DT_, T], F32, e)
    SG, e = place("SG", [P, 2, 2, T], F32, e)
    HF, e = place("HF", [P, 2, 2, T], F32, e)
    XN = MS

    PRE0, e = place("PRE0", [P, HG, T], F32, arena)
    KF0, e = place("KF0", [P, HG, T], F32, e)
    QF0, e = place("QF0", [P, HG, T], F32, e)
    GO0, e = place("GO0", [P, HG, T], F32, e)
    PRE1, _ = place("PRE1", [P, HG, T], F32, at_hh + 8 * T * 4)
    KF1, _ = place("KF1", [P, HG, T], F32, at_hh + 12 * T * 4)
    QF1, _ = place("QF1", [P, HG, T], F32, at_hl + 8 * T * 4)
    VF1, _ = place("VF1", [P, HG, T], F32, at_hl + 12 * T * 4)
    GO1, _ = place("GO1", [P, HG, T], F32, at_hl + 4 * T * 4)
    SUF, e = place("SUF", [P, HG, T], F32, e)
    at_w = e
    W, e = place("W", [P, 2, HG, T], F32, e)
    SQO, _ = place("SQO", [P, HG, T], F32, at_w)
    RTO, _ = place("RTO", [P, HG, T], F32, at_w + HG * T * 4)
    VF0, e = place("VF0", [P, HG, T], F32, e)
    PROJ = ((PRE0, KF0, QF0, VF0, GO0), (PRE1, KF1, QF1, VF1, GO1))
    APR, e = place("APR", [P, 2, HG, P], F32, e)
    ASM, e = place("ASM", [NS, HG, NS], F32, e)
    VTOK, e = place("VTOK", [P, 3, HG * KD], F32, e)
    KTOK, e = place("KTOK", [P, 3, HG * KD], F32, e)
    VM, e = place("VM", [NS, NB, KD], F32, e)
    tail = 16 * T * 4
    SIN0, e0 = place("SIN0", [P, NB, KD], F32, at_hh + tail)
    SIN1, e1 = place("SIN1", [P, NB, KD], F32, at_hl + tail)
    S1, e0 = place("S1", [P, HG, KD], F32, e0)
    S2, e1 = place("S2", [P, HG, KD], F32, e1)
    assert e0 <= at_hl and e1 <= at_hl + FT * T * 4


    at_xb = arena
    XB, e = place("XB", [P, CT, XBW], F32, arena)
    Z, e = place("Z", [P, PAIRS, T], F32, e)
    XC, e = place("XC", [P, CT, T], F32, e)
    at_acc = e
    ACC, e = place("ACC", [P, 4, XBW], F32, e)
    at_dtx = e
    DTX, e = place("DTX", [P, 3, MH * HD], F32, e)
    BTOK, e = place("BTOK", [P, 3, 2 * P], F32, e)
    GM, em = place("GM", [P, 3, 2, P], F32, at_hh + tail + NB * KD * 4)
    assert em <= at_hl
    CROW, _ = place("CROW", [NB * 3, CT * P], F32, at_dtx)
    CS, e2 = place("CS", [P, CT, 27], F32, at_acc)
    SIN2, _ = place("SIN2", [P, NB, KD], F32, at_acc)
    SIN = (SIN0, SIN1, SIN2)
    CO, _ = place("CO", [27, CT * P], F32, at_hh + 8 * T * 4)
    WX, e3 = place("WX", [P, 3, MH * HD], F32, at_xb)
    HT1, e3 = place("HT1", [P, MH * HD], F32, e3)
    assert e3 <= at_xb + CT * XBW * 4
    L1, e4 = place("L1", [P, 2, 2, P], F32, at_xh)
    L1S, e4 = place("L1S", [NS, 2, NS], F32, e4)
    ST, e4 = place("ST", [P, 2, 2, P], F32, e4)
    STS, e4 = place("STS", [NS, 2, NS], F32, e4)
    EC, e4 = place("EC", [P, 2, T], F32, e4)
    Y2, e4 = place("Y2", [P, T], F32, e4)
    SP, e4 = place("SP", [P, 2, P], F32, e4)
    assert e4 <= at_xl
    HTS, e5 = place("HTS", [P, NB, P], F32, at_xl)
    BMK, e5 = place("BMK", [NS, NB, P], F32, e5)
    assert e5 <= at_hh
    SQS, _ = place("SQS", [P, PAIRS, T], F32, at_xb)

    PS = ctx.enter_context(nc.psum_tensor("PS", [P, 8, 512], F32))

    def gain(i, k):
        return PAR[:, C_GAIN + 8 * i + k:C_GAIN + 8 * i + k + 1]

    def col(c):
        return PAR[:, c:c + 1]

    def sig(name, per_layer=0, before=0):
        return Signal(ctx, nc, name, per_layer, before)

    consts_done = sig("consts_done")
    iota_done = sig("iota_done")
    params_in = sig("params_in")
    params_turned = sig("params_turned")
    params_done = sig("params_done")
    x_rows_in = sig("x_rows_in")
    x_turned = sig("x_turned")
    lb_step = sig("lb_step")
    lb_exp = sig("lb_exp")
    const_step = sig("const_step")

    raw_landed = (sig("raw_landed0", 16 * UNITS // 2), sig("raw_landed1", 16 * UNITS // 2))
    hi_ready = sig("hi_ready", UNITS)
    lo_ready = sig("lo_ready", UNITS, 2)
    unit_done = sig("unit_done", UNITS, 2)

    par_ready = sig("par_ready", 1)
    presq_ready = sig("presq_ready", 12)
    postsq_ready = sig("postsq_ready", 12)
    ms_ready = sig("ms_ready", 12)
    stat_ready = sig("stat_ready", 6)
    root_ready = sig("root_ready", 6)
    rinv_ready = sig("rinv_ready", 6)
    scaled_ready = sig("scaled_ready", 24)
    xn_ready = sig("xn_ready", 24)
    xh_ready = sig("xh_ready", 12)
    xl_ready = sig("xl_ready", 12)
    x_ready = sig("x_ready", 12, 3)
    sg_ready = sig("sg_ready", FT)
    h_ready = sig("h_ready", FT, 2)
    hh_ready = sig("hh_ready", FT)
    hl_ready = sig("hl_ready", FT)
    fsig_ready = sig("fsig_ready", 2 * 4)
    fk_ready = sig("fk_ready", 2 * 8)
    q_ready = sig("q_ready", 2 * 2)
    v_ready = sig("v_ready", 2 * 2)
    go_ready = sig("go_ready", 2 * 2)
    hgz_ready = sig("hgz_ready", 2 * 3)
    w_ready = sig("w_ready", 2 * 16)
    tree_ready = sig("tree_ready", 2 * 14)
    score_ready = sig("score_ready", 2 * 8)
    picked = sig("picked", 2 * 8)
    vturn_ready = sig("vturn_ready", 2 * 3)
    vtok_ready = sig("vtok_ready", 2 * 3)
    kturn_ready = sig("kturn_ready", 2 * 3)
    ktok_ready = sig("ktok_ready", 2 * 3)
    sp1_ready = sig("sp1_ready", 2)
    s1_ready = sig("s1_ready", 2)
    sp2_ready = sig("sp2_ready", 2)
    s2_ready = sig("s2_ready", 2)
    s2_stored = sig("s2_stored", 2 * 16, 16)
    hs_in = (sig("hs_in0", 4 * 16), sig("hs_in1", 4 * 16))
    hs_stored = (sig("hs_stored0", 4 * 16, 16), sig("hs_stored1", 4 * 16, 16))
    vm_ready = sig("vm_ready", HH_)
    upd_ready = sig("upd_ready", HH_)
    decayed = sig("decayed", HH_)
    snew_ready = sig("snew_ready", HH_)
    o_ready = sig("o_ready", HH_)
    sqo_ready = sig("sqo_ready", HH_)
    ostat_ready = sig("ostat_ready", 2)
    oroot_ready = sig("oroot_ready", 2)
    orinv_ready = sig("orinv_ready", 2)
    gor_ready = sig("gor_ready", 2)
    ohg_ready = sig("ohg_ready", HH_, 1)
    ohh_ready = sig("ohh_ready", 2)
    ohl_ready = sig("ohl_ready", 2, 1)
    wdt_in = sig("wdt_in", 16)
    dtp_ready = sig("dtp_ready", 1)
    dt_step = sig("dt_step", 20)
    dt_exp = sig("dt_exp", 4)
    remp_ready = sig("remp_ready", 1)
    rem_ready = sig("rem_ready", 2)
    crow_in = sig("crow_in", 16)
    cturn_ready = sig("cturn_ready", 1)
    zeros_ready = sig("zeros_ready", 1)
    pads_ready = sig("pads_ready", 1)
    xb_ready = sig("xb_ready", 12)
    z_ready = sig("z_ready", 4)
    acc_ready = sig("acc_ready", CT)
    tap_ready = sig("tap_ready", 3 * CT)
    xc_ready = sig("xc_ready", 6)
    cs_ready = sig("cs_ready", 2)
    csturn_ready = sig("csturn_ready", 1)
    co_ready = sig("co_ready", 1)
    co_stored = sig("co_stored", 32)
    xturn_ready = sig("xturn_ready", 3)
    dtx_ready = sig("dtx_ready", 3)
    btok_ready = sig("btok_ready", 3)
    g_ready = sig("g_ready", 3)
    gm_ready = sig("gm_ready", 3)
    wx_ready = sig("wx_ready", 3)
    bmk_ready = sig("bmk_ready", 2)
    ht1p_ready = sig("ht1p_ready", 1)
    ht1_ready = sig("ht1_ready", 1)
    l1_ready = sig("l1_ready", 2 * PAIRS)
    seg_ready = sig("seg_ready", PAIRS)
    e_ready = sig("e_ready", 3 * PAIRS)
    st_ready = sig("st_ready", 2 * PAIRS)
    ms_in = tuple(sig(f"ms_in{s}", 16 * n) for s, n in enumerate((3, 3, 2)))
    ms_stored = tuple(sig(f"ms_stored{s}", 16 * n, 16) for s, n in enumerate((3, 3, 2)))
    hts_turned = sig("hts_turned", PAIRS)
    hts_ready = sig("hts_ready", PAIRS)
    y_ready = sig("y_ready", PAIRS)
    y2_ready = sig("y2_ready", PAIRS)
    ydone = sig("ydone", PAIRS)
    ystep = sig("ystep", 2 * PAIRS)
    supd_ready = sig("supd_ready", PAIRS)
    spc_ready = sig("spc_ready", PAIRS)
    spn_ready = sig("spn_ready", PAIRS)
    ssm_new = sig("ssm_new", PAIRS)
    sp_stored = (sig("sp_stored0", 4 * 16, 16), sig("sp_stored1", 4 * 16, 16))
    yz_ready = sig("yz_ready", 2)
    sqs_ready = sig("sqs_ready", 2)
    sstat_ready = sig("sstat_ready", 1)
    sroot_ready = sig("sroot_ready", 1)
    srinv_ready = sig("srinv_ready", 1)
    ysn_ready = sig("ysn_ready", PAIRS)
    yh_ready = sig("yh_ready", 4)
    yl_ready = sig("yl_ready", 4)
    yout_turned = sig("yout_turned")
    yout_ready = sig("yout_ready")
    y_stored = sig("y_stored")

    block = ctx.enter_context(nc.Block())

    def unit(u0, i=None, step=2):
        if i is None:
            return u0 % 2, u0, u0 // 2
        return u0 % 2, i * step + u0, i * (step // 2) + u0 // 2

    @block.sync
    def _(sp):
        sp.dma_start(XROW[:, 0:2, :], a["x_prompt"][0].rearrange("(n p) d -> p n d", p=P)).then_inc(x_rows_in.sem, 16)
        sp.dma_start(XROW[0:NS, 2, :], a["x_sample"].rearrange("b t d -> (b t) d")).then_inc(x_rows_in.sem, 16)
        with nc.allow_non_contiguous_dma("small parameter rows"):
            r = 0
            for name, n in (("norm_gain", 48), ("hg_norm_w", 8), ("ssm_norm_w", 8), ("conv_b", 12),
                            ("hg_lb_logits", 8)):
                src = a[name]
                if name == "norm_gain":
                    src = src.rearrange("l g d -> l (g d)")
                sp.dma_start(PROWA[r:r + n, :, :], src.rearrange("l (r p) -> r l p", p=P)).then_inc(params_in.sem, 16)
                r += n
            sp.dma_start(PROWB[:, :, :], a["conv_w"].rearrange("l j (c p) -> (j c) l p", p=P)).then_inc(params_in.sem, 16)
            for hh in range(2):
                for l in range(LAYERS):
                    src = a["d_skip"].rearrange("l (i h) -> h l i", h=2)[hh:hh + 1, l, :]
                    sp.dma_start(PALL[64 * hh:64 * hh + 64, l, C_DSK:C_DSK + PAIRS],
                                 src.broadcast_to([64, PAIRS])).then_inc(params_in.sem, 16)
            for name, c in (("dt_bias", C_DTB), ("a_log", C_A)):
                src = a[name].rearrange("(o l) h -> o l h", o=1)
                sp.dma_start(PALL[:, :, c:c + MH], src.broadcast_to([P, LAYERS, MH])).then_inc(params_in.sem, 16)

        def fetch_columns(l, w, u, c0):
            slot, n, _ = u
            sp.wait_ge(lo_ready.sem, lo_ready.after(l, n) + (1 - 2))
            src = w[ds(l, 1), :, ds(c0, 256)].rearrange("o (k p) c -> p (o k) c", p=P)
            sp.dma_start(RAW[:, slot, :].rearrange("p (k c) -> p k c", c=256), src).then_inc(raw_landed[slot].sem, 16)

        def fetch_rows(l, w, u, r0):
            slot, n, _ = u
            sp.wait_ge(lo_ready.sem, lo_ready.after(l, n) + (1 - 2))
            src = w[ds(l, 1), ds(r0, 256), :].rearrange("o (k p) c -> p (o k) c", p=P)
            sp.dma_start(RAW[:, slot, :].rearrange("p (k c) -> p k c", c=D), src).then_inc(raw_landed[slot].sem, 16)

        def ffn(l, up, down, g, u_, d):
            with sp.Fori(0, FT // 2) as j:
                fetch_columns(l, a[g], unit(up, j), j * 256)
                fetch_columns(l, a[u_], unit(up + 1, j), j * 256)
            with sp.Fori(0, 5) as j:
                fetch_rows(l, a[d], unit(down, j), j * 512)
                fetch_rows(l, a[d], unit(down + 1, j), j * 512 + 256)
            fetch_rows(l, a[d], unit(down + 10), 10 * 256)

        with sp.Fori(0, LAYERS) as l:
            ffn(l, U_UP1, U_DOWN1, "ffn1_w_gate", "ffn1_w_up", "ffn1_w_down")
            with sp.Fori(0, 2) as g:
                for c, c0 in enumerate((COL_F, COL_Q, COL_V, COL_GO)):
                    for s in range(2):
                        fetch_columns(l, a["w_in"], unit(U_IN + 2 * c + s, g, 8), g * 512 + (c0 + 256 * s))
            for first, n, c0 in ((U_IN + 16, 3, COL_X), (U_IN + 22, 2, COL_Z)):
                with sp.Fori(0, n) as i:
                    for s in range(2):
                        fetch_columns(l, a["w_in"], unit(first + s, i), i * 512 + (c0 + 256 * s))
            with sp.Fori(0, 4) as i:
                fetch_rows(l, a["w_out"], unit(U_OUT, i), i * 512)
                fetch_rows(l, a["w_out"], unit(U_OUT + 1, i), i * 512 + 256)
            ffn(l, U_UP2, U_DOWN2, "ffn2_w_gate", "ffn2_w_up", "ffn2_w_down")
        for n in range(3):
            sp.wait_ge(yout_ready.sem, n + 1)
            dst = (o["y_prompt"][0][n * P:(n + 1) * P, :] if n < 2 else o["y_sample"].rearrange("b t d -> (b t) d"))
            sp.dma_start(dst, YROW[0:TILES[n][1], n, :]).then_inc(y_stored.sem, 16)
        sp.wait_ge(y_stored.sem, 48)

    @block.gpsimd
    def _(pool):
        nc.gpsimd.iota(IT[:], pattern=[[1, P]], base=0, channel_multiplier=0).then_inc(iota_done.sem, 1)
        nc.gpsimd.iota(IS[:], pattern=[[0, P]], base=0, channel_multiplier=1).then_inc(iota_done.sem, 1)
        nc.gpsimd.iota(IBK[:], pattern=[[-SL, NB]], base=0, channel_multiplier=1).then_inc(iota_done.sem, 1)

        def blocked(src, n):
            return (src.rearrange("p (o v) -> p o v", o=1).broadcast_to([NS, NB, n]),
                    BLK[:].rearrange("p (b o) -> p b o", o=1).broadcast_to([NS, NB, n]))

        def hgrn(l, g):
            pool.wait_ge(unit_done.sem, unit_done.after(l, U_IN + 1))
            pool.wait_ge(ohl_ready.sem, ohl_ready.after(l, g))
            one = ONES[:, 0:1].rearrange("p (a b) -> p a b", a=1).broadcast_to([P, HG, T])
            nc.gpsimd.tensor_tensor(SUF[:], one, one, ALU.mult).then_inc(hgz_ready.sem, 1)
            nc.gpsimd.memset(APR[:], 0.0).then_inc(hgz_ready.sem, 1)
            nc.gpsimd.memset(ASM[:], 0.0).then_inc(hgz_ready.sem, 1)
            for h in range(HG):
                pool.wait_ge(vtok_ready.sem, vtok_ready.after(l, g * 3 + 2))
                if h:
                    pool.wait_ge(upd_ready.sem, upd_ready.after(l, g * 4 + h))
                nc.gpsimd.tensor_tensor(VM[:], *blocked(VTOK[0:NS, 2, h * KD:(h + 1) * KD], KD),
                                        ALU.mult).then_inc(vm_ready.sem, 1)
                pool.wait_ge(o_ready.sem, o_ready.after(l, g * 4 + h + 1))
                s = SIN[h % 2]
                nc.gpsimd.tensor_tensor(
                    s[:], s[:],
                    PROJ[g][0][:, h, SEQ + SL - 1:T:SL].rearrange("p (b o) -> p b o", o=1).broadcast_to([P, NB, KD]),
                    ALU.mult).then_inc(decayed.sem, 1)

        def mamba(l):
            pool.wait_ge(ohl_ready.sem, ohl_ready.after(l, 2))

            def one(*shape):
                return ONES[:, 0:1].rearrange("p (a b) -> p a b", a=1).broadcast_to([P, *shape])

            nc.gpsimd.tensor_tensor(XB[:, :, 0:CW - 1], one(CT, CW - 1), one(CT, CW - 1), ALU.subtract).then_inc(zeros_ready.sem, 1)
            pool.wait_ge(xc_ready.sem, xc_ready.after(l, 6))
            nc.gpsimd.tensor_tensor(CS[:, :, 0:3], XB[:, :, SEQ:PADP], one(CT, 3), ALU.mult).then_inc(cs_ready.sem, 1)
            nc.gpsimd.tensor_copy(
                CS[:, :, 3:27].rearrange("p c (b j) -> p c b j", j=3),
                XB[:, :, PADP:].rearrange("p c (b j) -> p c b j", j=PADS)[:, :, :, SL:]).then_inc(cs_ready.sem, 1)
            pool.wait_ge(rem_ready.sem, rem_ready.after(l, 2))
            pool.wait_ge(cs_ready.sem, cs_ready.after(l, 2))
            for j, n in enumerate(TURNS):
                tn = TILES[n][1]
                pool.wait_ge(dtx_ready.sem, dtx_ready.after(l, j + 1))
                nc.gpsimd.tensor_tensor(
                    WX[0:tn, n, :].rearrange("p (h d) -> p h d", d=HD),
                    DTX[0:tn, n, :].rearrange("p (h d) -> p h d", d=HD),
                    REM[0:tn, n, :].rearrange("p (h o) -> p h o", o=1).broadcast_to([tn, MH, HD]),
                    ALU.mult).then_inc(wx_ready.sem, 1)
            for g in range(2):
                pool.wait_ge(btok_ready.sem, btok_ready.after(l, 3))
                if g:
                    pool.wait_ge(supd_ready.sem, supd_ready.after(l, 4))
                nc.gpsimd.tensor_tensor(BMK[:], *blocked(BTOK[0:NS, 2, g * P:(g + 1) * P], P),
                                        ALU.mult).then_inc(bmk_ready.sem, 1)

        with pool.Fori(0, LAYERS) as l:
            for g in range(2):
                hgrn(l, g)
            mamba(l)

    @block.scalar
    def _(act):
        def copy(out, in_, scale=1.0):
            return nc.scalar.activation(out, in_, ACT.Copy, scale=scale)

        def split_hi(l, u):
            slot, n, k = u
            act.wait_ge(raw_landed[slot].sem, raw_landed[slot].after(l, k * 16 + 16))
            act.wait_ge(unit_done.sem, unit_done.after(l, n) + (1 - 2))
            copy(WH[:, slot, :], RAW[:, slot, :]).then_inc(hi_ready.sem, 1)

        def ahead(u):
            return u[0], u[1] + 2, u[2] + 1

        act.wait_ge(consts_done.sem, 1)
        for n, (t0, tn) in enumerate(TILES):
            act.wait_ge(x_turned.sem, n + 1)
            copy(X[:, :, t0:t0 + tn],
                 PS[:, 2 * n:2 * n + 2, :].rearrange("p b (k t) -> p (b k) t", t=P)[:, :, 0:tn]).then_inc(x_ready.sem, 1)
        act.wait_ge(lb_step.sem, 3)
        nc.scalar.activation(LBW[:, 3:5], LBW[:, 3:5], ACT.Exp).then_inc(lb_exp.sem, 1)
        nc.scalar.activation(PALL[:, :, C_A:C_A + MH], PALL[:, :, C_A:C_A + MH], ACT.Exp).then_inc(lb_exp.sem, 1)
        for s in (s2_stored, *hs_stored, *ms_stored, *sp_stored):
            copy(FREE[:], EPST[:]).then_inc(s.sem, 16)
            act.wait_ge(s.sem, 16)

        def pre_norm(l, i):
            for c in range(4):
                act.wait_ge(x_ready.sem, x_ready.after(l, 4 * i + c - 3 if i else 0))
                nc.scalar.activation(SQ[:, 2 * c:2 * c + 2], X[:, 2 * c:2 * c + 2], ACT.Square).then_inc(presq_ready.sem, 1)
            act.wait_ge(stat_ready.sem, stat_ready.after(l, 2 * i + 1))
            nc.scalar.activation(ROOT[:], PS[:, 0, 0:T], ACT.Sqrt, bias=EPST[:], scale=1.0 / D).then_inc(root_ready.sem, 1)
            for c in range(4):
                act.wait_ge(xn_ready.sem, xn_ready.after(l, 8 * i + 2 * c + 2))
                copy(XH[:, 2 * c:2 * c + 2], XN[:, 2 * c:2 * c + 2]).then_inc(xh_ready.sem, 1)

        def post_norm(l, i, last_unit):
            act.wait_ge(unit_done.sem, unit_done.after(l, last_unit + 1))
            for c in range(4):
                copy(MS[:, 2 * c:2 * c + 2], PS[:, 2 * c:2 * c + 2, 0:T]).then_inc(ms_ready.sem, 1)
            act.wait_ge(stat_ready.sem, stat_ready.after(l, 2 * i + 2))
            nc.scalar.activation(ROOT[:], PS[:, 0, 0:T], ACT.Sqrt, bias=EPST[:], scale=1.0 / D).then_inc(root_ready.sem, 1)

        def ffn(l, f, up, down):
            def pair(j, par, gate, up_):
                act.wait_ge(unit_done.sem, unit_done.after(l, gate[1]) + 1)
                split_hi(l, ahead(gate))
                nc.scalar.activation(SG[:, par], PS[:, 4 * par:4 * par + 2, 0:T], ACT.Silu).then_inc(sg_ready.sem, 1)
                split_hi(l, ahead(up_))
                act.wait_ge(h_ready.sem, h_ready.after(l, j) + 1)
                copy(HH[:, ds(j * 2 - 22 * f, 2), :], HF[:, par]).then_inc(hh_ready.sem, 1)

            with act.Fori(0, 5) as i:
                for s in range(2):
                    pair(i * 2 + (11 * f + s), s, unit(up + 2 * s, i, 4), unit(up + 2 * s + 1, i, 4))
            act.wait_ge(unit_done.sem, unit_done.after(l, up + 20) + 1)
            split_hi(l, unit(up + 22))
            nc.scalar.activation(SG[:, 0], PS[:, 0:2, 0:T], ACT.Silu).then_inc(sg_ready.sem, 1)
            split_hi(l, unit(up + 23))
            act.wait_ge(h_ready.sem, h_ready.after(l, 11 * f + 11))
            copy(HH[:, 20:22, :], HF[:, 0]).then_inc(hh_ready.sem, 1)
            with act.Fori(0, 4) as i:
                split_hi(l, unit(down + 2, i))
                split_hi(l, unit(down + 3, i))
            split_hi(l, unit(down + 10))
            if f == 0:
                split_hi(l, unit(down + 11))
                split_hi(l, unit(down + 12))

        def hgrn_state_in(l, g, h):
            act.wait_ge(hs_stored[h % 2].sem, hs_stored[h % 2].after(l, g * 32 + h // 2 * 16))
            act.dma_start(SIN[h % 2][:],
                          a["state_hgrn"][ds(l, 1), :, ds(g * 4 + h, 1)].rearrange("o b h k v -> k (o b h) v")
                          ).then_inc(hs_in[h % 2].sem, 16)

        def projected(l, g, c):
            u = unit(U_IN + 8 * g + c)
            act.wait_ge(unit_done.sem, unit_done.after(l, u[1]) + 1)
            split_hi(l, ahead(u))
            b = 6 if g else 2 * (c % 4)
            ps = PS[:, b:b + 2, 0:T]
            h = slice(2 * (c % 2), 2 * (c % 2) + 2)
            pre, kf, qf, vf, go = PROJ[g]
            if c < 2:
                nc.scalar.activation(pre[:, h], ps, ACT.Sigmoid).then_inc(fsig_ready.sem, 1)
                nc.scalar.activation(kf[:, h], ps, ACT.Sigmoid, scale=-1.0).then_inc(fsig_ready.sem, 1)
            elif c < 4:
                copy(qf[:, h], ps, QSCALE).then_inc(q_ready.sem, 1)
            elif c < 6:
                copy(vf[:, h], ps).then_inc(v_ready.sem, 1)
            else:
                nc.scalar.activation(go[:, h], ps, ACT.Silu).then_inc(go_ready.sem, 1)

        def conv_input(l, j):
            u = unit(U_IN + 16 + j)
            act.wait_ge(unit_done.sem, unit_done.after(l, u[1]) + 1)
            split_hi(l, ahead(u))
            if j == 0:
                act.wait_ge(ohl_ready.sem, ohl_ready.after(l, 1))
            copy(XB[:, 2 * j:2 * j + 2, CW - 1:PADP], PS[:, 6:8, 0:SEQ]).then_inc(xb_ready.sem, 1)
            copy(XB[:, 2 * j:2 * j + 2, PADP:].rearrange("p c (b j) -> p c b j", j=PADS)[:, :, :, CW - 1:],
                 PS[:, 6:8, SEQ:T].rearrange("p c (b j) -> p c b j", j=SL)).then_inc(xb_ready.sem, 1)

        def hgrn(l, g):
            def beside(place):
                for j in BESIDE[g][place]:
                    projected(l, 1, j) if g == 0 else conv_input(l, j)

            hgrn_state_in(l, g, 0)
            hgrn_state_in(l, g, 1)
            for j, n in enumerate(TURNS):
                tn = TILES[n][1]
                act.wait_ge(vturn_ready.sem, vturn_ready.after(l, g * 3 + j + 1))
                copy(VTOK[0:tn, n, :], PS[0:tn, 4 + j % 2, :]).then_inc(vtok_ready.sem, 1)
            for i in range(1, 8):
                beside(i)
            for j, n in enumerate(TURNS):
                tn = TILES[n][1]
                act.wait_ge(kturn_ready.sem, kturn_ready.after(l, g * 3 + j + 1))
                copy(KTOK[0:tn, n, :], PS[0:tn, j % 2, :]).then_inc(ktok_ready.sem, 1)
            act.wait_ge(sp1_ready.sem, sp1_ready.after(l, g + 1))
            copy(S1[:], PS[:, 4, :].rearrange("p (h v) -> p h v", v=KD)).then_inc(s1_ready.sem, 1)
            act.wait_ge(s2_ready.sem, s2_ready.after(l, g + 1))
            act.dma_start(o["hgrn_prompt"][ds(l, 1), 0, ds(g * 4, 4)].rearrange("o h k v -> k (o h) v"),
                          S2[:]).then_inc(s2_stored.sem, 16)
            for h in range(HG):
                act.wait_ge(o_ready.sem, o_ready.after(l, g * 4 + h + 1))
                nc.scalar.activation(SQO[:, h], PS[:, h, 0:T], ACT.Square).then_inc(sqo_ready.sem, 1)
                beside(8 + h)
                act.wait_ge(snew_ready.sem, snew_ready.after(l, g * 4 + h + 1))
                act.dma_start(o["hgrn_sample"][ds(l, 1), :, ds(g * 4 + h, 1)].rearrange("o b h k v -> k (o b h) v"),
                              SIN[h % 2][:]).then_inc(hs_stored[h % 2].sem, 16)
                if h < 2:
                    hgrn_state_in(l, g, h + 2)
            act.wait_ge(ostat_ready.sem, ostat_ready.after(l, g + 1))
            nc.scalar.activation(RTO[:], PS[:, 4:8, 0:T], ACT.Sqrt, bias=EPST[:], scale=1.0 / KD).then_inc(oroot_ready.sem, 1)
            if g == 0:
                beside(12)
            act.wait_ge(ohg_ready.sem, ohg_ready.after(l, g * 4 + 4))
            copy(HH[:, 4 * g:4 * g + 4, :], SQO[:]).then_inc(ohh_ready.sem, 1)
            if g == 1:
                beside(12)

        def softplus(l):
            for f in range(2):
                for r, n in ROWS:
                    if f == 0:
                        act.wait_ge(dt_step.sem, dt_step.after(l, 4))
                        nc.scalar.activation(DTW[r, 2, n], DTW[r, 1, n], ACT.Exp).then_inc(dt_exp.sem, 1)
                    else:
                        act.wait_ge(dt_exp.sem, dt_exp.after(l, 2))
                        nc.scalar.activation(DTW[r, 3, n], DTW[r, 2, n], ACT.Ln, bias=1.0).then_inc(dt_exp.sem, 1)

        def ssm_state_in(l, i):
            act.wait_ge(ms_stored[i % 3].sem, ms_stored[i % 3].after(l, i // 3 * 16))
            act.dma_start(SIN[i % 3][:],
                          a["state_ssm"][ds(l, 1), :, 2 * i:2 * i + 2].rearrange("o b h p n -> (h p) (o b) n")
                          ).then_inc(ms_in[i % 3].sem, 16)

        def mamba(l):
            act.wait_ge(hs_stored[0].sem, hs_stored[0].after(l, 64))
            act.wait_ge(hs_stored[1].sem, hs_stored[1].after(l, 64))
            ssm_state_in(l, 0)
            ssm_state_in(l, 1)
            act.wait_ge(ohl_ready.sem, ohl_ready.after(l, 2))
            act.dma_start(CROW[:], a["state_conv"][ds(l, 1)].rearrange("o b j c -> (o b j) c")).then_inc(crow_in.sem, 16)
            def gate(j):
                u = unit(U_IN + 22 + j)
                act.wait_ge(unit_done.sem, unit_done.after(l, u[1]) + 1)
                split_hi(l, ahead(u))
                b = 4 + 2 * (j % 2)
                nc.scalar.activation(Z[:, 2 * j:2 * j + 2, :], PS[:, b:b + 2, 0:T], ACT.Silu).then_inc(z_ready.sem, 1)

            gate(0)
            act.wait_ge(cturn_ready.sem, cturn_ready.after(l, 1))
            copy(XB[:, :, PADP:].rearrange("p c (b j) -> p c b j", j=PADS)[:, :, :, 0:CW - 1],
                 PS[:, 0, 0:CT * 24].rearrange("p (c b j) -> p c b j", b=NB, j=CW - 1)).then_inc(pads_ready.sem, 1)
            act.wait_ge(pads_ready.sem, pads_ready.after(l, 1))
            act.wait_ge(xb_ready.sem, xb_ready.after(l, 12))
            act.wait_ge(zeros_ready.sem, zeros_ready.after(l, 1))
            for q in range(3):
                if q:
                    act.wait_ge(xc_ready.sem, xc_ready.after(l, 2 * q))
                for c in range(4):
                    k = 4 * q + c
                    nc.scalar.activation(ACC[:, c, 0:CVW], XB[:, k, CW - 1:XBW], ACT.Identity, bias=col(C_CB + k),
                                         scale=col(C_CW + 3 * CT + k)).then_inc(acc_ready.sem, 1)
                gate(q + 1)
                act.wait_ge(tap_ready.sem, tap_ready.after(l, 12 * q + 12))
                nc.scalar.activation(XC[:, 4 * q:4 * q + 4, 0:SEQ], ACC[:, :, 0:SEQ], ACT.Silu).then_inc(xc_ready.sem, 1)
                nc.scalar.activation(
                    XC[:, 4 * q:4 * q + 4, SEQ:].rearrange("p c (b j) -> p c b j", j=SL),
                    ACC[:, :, PADP:].rearrange("p c (b j) -> p c b j", j=PADS)[:, :, :, 0:SL], ACT.Silu).then_inc(xc_ready.sem, 1)
            act.wait_ge(remp_ready.sem, remp_ready.after(l, 1))
            for k, (r, n) in enumerate(ROWS):
                nc.scalar.activation(REM[r, n], PS[r, 1, 0:48].rearrange("p (n h) -> p n h", h=MH)[:, n], ACT.Exp).then_inc(rem_ready.sem, 1)
            for j, n in enumerate(TURNS):
                tn = TILES[n][1]
                act.wait_ge(xturn_ready.sem, xturn_ready.after(l, j + 1))
                copy(BTOK[0:tn, n, :], PS[0:tn, 5 if j == 1 else 2, 0:2 * P]).then_inc(btok_ready.sem, 1)
            act.wait_ge(ht1p_ready.sem, ht1p_ready.after(l, 1))
            copy(HT1[:].rearrange("p (g c) -> p g c", g=2), PS[:, 0:2, :]).then_inc(ht1_ready.sem, 1)
            act.wait_ge(csturn_ready.sem, csturn_ready.after(l, 1))
            copy(CO[:].rearrange("p (b c) -> p b c", b=3), PS[0:27, 5:8, :]).then_inc(co_ready.sem, 1)
            act.wait_ge(co_ready.sem, co_ready.after(l, 1))
            act.dma_start(o["conv_prompt"][ds(l, 1), 0].rearrange("o j c -> (o j) c"), CO[0:3, :]).then_inc(co_stored.sem, 16)
            act.dma_start(o["conv_sample"][ds(l, 1)].rearrange("o b j c -> (o b j) c"), CO[3:27, :]).then_inc(co_stored.sem, 16)
            ssm_state_in(l, 2)

            def decays(i):
                act.wait_ge(seg_ready.sem, seg_ready.after(l, i + 1))
                if i:
                    act.wait_ge(y_ready.sem, y_ready.after(l, i))
                nc.scalar.activation(ST[:].rearrange("p n h t -> p (n h t)"), PS[:, 4, :], ACT.Exp).then_inc(e_ready.sem, 1)
                nc.scalar.activation(STS[:].rearrange("p h t -> p (h t)"), PS[0:NS, 5, 0:P], ACT.Exp).then_inc(e_ready.sem, 1)
                nc.scalar.activation(EC[:, i % 2], PS[:, 5, P:P + T], ACT.Exp).then_inc(e_ready.sem, 1)

            def states_out(i):
                act.wait_ge(spn_ready.sem, spn_ready.after(l, i + 1))
                act.dma_start(o["ssm_prompt"][ds(l, 1), 0, 2 * i:2 * i + 2].rearrange("o h p n -> (o h p) n"),
                              SP[:, i % 2, :]).then_inc(sp_stored[i % 2].sem, 16)
                act.wait_ge(ssm_new.sem, ssm_new.after(l, i + 1))
                act.dma_start(o["ssm_sample"][ds(l, 1), :, 2 * i:2 * i + 2].rearrange("o b h p n -> (h p) (o b) n"),
                              SIN[i % 3][:]).then_inc(ms_stored[i % 3].sem, 16)

            decays(0)
            for i in range(PAIRS):
                act.wait_ge(hts_turned.sem, hts_turned.after(l, i + 1))
                if i:
                    act.wait_ge(y2_ready.sem, y2_ready.after(l, i))
                copy(HTS[:].rearrange("p (c b) n -> p c (b n)", c=2), PS[:, 6:8, :]).then_inc(hts_ready.sem, 1)
                if i:
                    states_out(i - 1)
                if i + 1 < PAIRS:
                    decays(i + 1)
                if i and i + 2 < PAIRS:
                    ssm_state_in(l, i + 2)
            states_out(PAIRS - 1)
            for g in range(2):
                act.wait_ge(yz_ready.sem, yz_ready.after(l, g + 1))
                nc.scalar.activation(SQS[:, 4 * g:4 * g + 4], Z[:, 4 * g:4 * g + 4], ACT.Square).then_inc(sqs_ready.sem, 1)
            act.wait_ge(sstat_ready.sem, sstat_ready.after(l, 1))
            nc.scalar.activation(SQS[:, 0:2], PS[:, 4:6, 0:T], ACT.Sqrt, bias=EPST[:], scale=2.0 / D).then_inc(sroot_ready.sem, 1)
            act.wait_ge(co_stored.sem, co_stored.after(l, 32))
            for c in range(4):
                act.wait_ge(ysn_ready.sem, ysn_ready.after(l, 2 * c + 2))
                copy(HH[:, 8 + 2 * c:10 + 2 * c, :], Z[:, 2 * c:2 * c + 2]).then_inc(yh_ready.sem, 1)
            for s in ms_stored + sp_stored:
                act.wait_ge(s.sem, s.after(l, s.per_layer))
            act.wait_ge(s2_stored.sem, s2_stored.after(l, 32))
            with act.Fori(0, 4) as i:
                split_hi(l, unit(U_OUT + 2, i))
                split_hi(l, unit(U_OUT + 3, i))

        with act.Fori(0, LAYERS) as l:
            act.dma_start(WDT[:], a["w_in"][ds(l, 1), :, COL_DT:COL_DT + MH].rearrange("o (k p) h -> p (o k) h", p=P)
                          ).then_inc(wdt_in.sem, 16)
            split_hi(l, unit(0))
            split_hi(l, unit(1))
            pre_norm(l, 0)
            ffn(l, 0, U_UP1, U_DOWN1)
            post_norm(l, 0, U_DOWN1 + 10)
            pre_norm(l, 1)
            for c in range(8):
                projected(l, 0, c)
                if c == 1:
                    softplus(l)
            for g in range(2):
                hgrn(l, g)
            mamba(l)
            post_norm(l, 1, U_OUT + 7)
            pre_norm(l, 2)
            ffn(l, 1, U_UP2, U_DOWN2)
            post_norm(l, 2, U_DOWN2 + 10)
        for n, (t0, tn) in enumerate(TILES):
            act.wait_ge(yout_turned.sem, n + 1)
            copy(YROW[0:tn, n, :].rearrange("p (b c) -> p b c", b=2), PS[0:tn, 2 * n:2 * n + 2, :]).then_inc(yout_ready.sem, 1)

    @block.vector
    def _(dve):
        V = nc.vector

        def split_lo(l, u):
            slot, n, _ = u
            dve.wait_ge(hi_ready.sem, hi_ready.after(l, n) + 1)
            V.tensor_tensor(WL[:, slot, :], RAW[:, slot, :], WH[:, slot, :].bitcast(F32), ALU.subtract).then_inc(lo_ready.sem, 1)

        def ahead(u):
            return u[0], u[1] + 2, u[2] + 1

        for s in (lo_ready, h_ready):
            for n in range(2):
                V.memset(FREEV[:], 0.0).then_inc(s.sem, 1)
                dve.wait_ge(s.sem, n + 1)
        V.memset(FREEV[:], 0.0).then_inc(ohg_ready.sem, 1)
        dve.wait_ge(ohg_ready.sem, 1)
        V.memset(FREEV[:], 0.0).then_inc(ohl_ready.sem, 1)
        V.memset(ONES[:], 1.0).then_inc(const_step.sem, 1)
        V.memset(EPST[:], EPS).then_inc(const_step.sem, 1)
        dve.wait_ge(iota_done.sem, 3)
        V.tensor_tensor(IX[:], IT[:], IS[:], ALU.bitwise_xor).then_inc(const_step.sem, 1)
        V.tensor_tensor(FIT[:], IT[:], IS[:], ALU.subtract).then_inc(const_step.sem, 1)
        dve.wait_ge(const_step.sem, 4)
        V.tensor_copy(FIX[:], IX[:]).then_inc(const_step.sem, 1)
        V.tensor_scalar(IDENT[:], FIT[:], 0.0, None, ALU.is_equal).then_inc(const_step.sem, 1)
        V.tensor_scalar(TRI[:], FIT[:], 0.0, None, ALU.is_ge).then_inc(const_step.sem, 1)
        V.tensor_scalar(USTR[:], FIT[:], 0.0, None, ALU.is_lt).then_inc(const_step.sem, 1)
        dve.wait_ge(const_step.sem, 8)
        V.scalar_tensor_tensor(TRI8[:], FIX[0:NS, 0:NS], 8.0, TRI[0:NS, 0:NS], ALU.is_lt, ALU.mult).then_inc(const_step.sem, 1)
        V.scalar_tensor_tensor(USTR8[:], FIX[0:NS, 0:NS], 8.0, USTR[0:NS, 0:NS], ALU.is_lt, ALU.mult).then_inc(const_step.sem, 1)
        V.tensor_tensor(FIT[:], FIX[:], TRI[:], ALU.mult).then_inc(const_step.sem, 1)
        dve.wait_ge(const_step.sem, 11)
        for i in range(8):
            V.tensor_scalar(FGE[:, i], FIT[:], float(1 << i), None, ALU.is_ge).then_inc(const_step.sem, 1)
        dve.wait_ge(const_step.sem, 19)
        V.tensor_copy(MASK[:, 0], IDENT[:]).then_inc(const_step.sem, 1)
        V.tensor_tensor(MASK[:, 1:8], FGE[:, 0:7], FGE[:, 1:8], ALU.subtract).then_inc(const_step.sem, 1)
        V.tensor_scalar(FB[:, 0], IBK[:], 0.0, None, ALU.is_ge).then_inc(const_step.sem, 1)
        V.tensor_scalar(FB[:, 1], IBK[:], float(SL), None, ALU.is_ge).then_inc(const_step.sem, 1)
        dve.wait_ge(const_step.sem, 23)
        V.tensor_tensor(BLK[:], FB[:, 0], FB[:, 1], ALU.subtract).then_inc(consts_done.sem, 1)
        dve.wait_ge(params_in.sem, 16 * 12)
        dve.wait_ge(params_turned.sem, 1)
        pa = PS[:, 6, 0:2 * NROW_A].rearrange("p (l c) -> p l c", l=2)
        V.tensor_copy(PALL[:, :, 0:C_CW], pa[:, :, 0:C_CW]).then_inc(params_done.sem, 1)
        V.tensor_copy(LBW[:, 0:2], pa[:, :, C_CW:NROW_A]).then_inc(params_done.sem, 1)
        V.tensor_copy(PALL[:, :, C_CW:C_LBF], PS[:, 7, 0:96].rearrange("p (l c) -> p l c", l=2)).then_inc(params_done.sem, 1)
        dve.wait_ge(params_done.sem, 3)
        V.tensor_scalar(PALL[:, :, C_GAIN + 8:C_GAIN + 16], PALL[:, :, C_GAIN + 8:C_GAIN + 16], 0.5, None, ALU.mult).then_inc(params_done.sem, 1)
        V.tensor_scalar(PALL[:, :, C_GAIN + 40:C_GAIN + 48], PALL[:, :, C_GAIN + 40:C_GAIN + 48], 0.5, None, ALU.mult).then_inc(params_done.sem, 1)
        V.tensor_tensor(LBW[:, 2], LBW[:, 0], LBW[:, 1], ALU.max).then_inc(lb_step.sem, 1)
        dve.wait_ge(lb_step.sem, 1)
        V.tensor_tensor(LBW[:, 3], LBW[:, 0], LBW[:, 2], ALU.subtract).then_inc(lb_step.sem, 1)
        V.tensor_tensor(LBW[:, 4], LBW[:, 1], LBW[:, 2], ALU.subtract).then_inc(lb_step.sem, 1)
        dve.wait_ge(lb_exp.sem, 2)
        V.tensor_tensor(LBW[:, 5], LBW[:, 3], LBW[:, 4], ALU.add).then_inc(lb_step.sem, 1)
        dve.wait_ge(lb_step.sem, 4)
        V.reciprocal(LBW[:, 6], LBW[:, 5]).then_inc(lb_step.sem, 1)
        dve.wait_ge(lb_step.sem, 5)
        V.tensor_tensor(LBW[:, 3], LBW[:, 3], LBW[:, 6], ALU.mult).then_inc(lb_step.sem, 1)
        V.tensor_tensor(LBW[:, 4], LBW[:, 4], LBW[:, 6], ALU.mult).then_inc(lb_step.sem, 1)
        dve.wait_ge(lb_step.sem, 7)
        V.tensor_tensor(LBW[:, 5], LBW[:, 3], LBW[:, 4], ALU.add).then_inc(lb_step.sem, 1)
        V.tensor_tensor(LBW[:, 0], LBW[:, 3], LBW[:, 3], ALU.subtract).then_inc(lb_step.sem, 1)
        dve.wait_ge(lb_step.sem, 9)
        V.tensor_tensor(LBW[:, 1], LBW[:, 5], LBW[:, 3], ALU.subtract).then_inc(lb_step.sem, 1)
        dve.wait_ge(lb_step.sem, 10)
        V.tensor_scalar(PALL[:, :, C_LBF:C_LBF + 8], LBW[:, 0:2], LB_FLOOR, None, ALU.max).then_inc(lb_step.sem, 1)
        V.tensor_scalar(PALL[:, :, C_OML:C_OML + 8], LBW[:, 0:2], -1.0, 1.0, ALU.mult, ALU.add).then_inc(lb_step.sem, 1)
        V.tensor_scalar(PALL[:, :, C_A:C_A + MH], PALL[:, :, C_A:C_A + MH], -1.0, None, ALU.mult).then_inc(lb_step.sem, 1)
        dve.wait_ge(lb_step.sem, 13)
        dve.wait_ge(params_done.sem, 5)

        def pre_norm(l, i):
            dve.wait_ge(root_ready.sem, root_ready.after(l, 2 * i + 1))
            V.reciprocal(RINV[:], ROOT[:]).then_inc(rinv_ready.sem, 1)
            dve.wait_ge(rinv_ready.sem, rinv_ready.after(l, 2 * i + 1))
            for k in range(DT_):
                V.scalar_tensor_tensor(XN[:, k], X[:, k], gain(2 * i, k), RINV[:], ALU.mult, ALU.mult).then_inc(xn_ready.sem, 1)
            for c in range(4):
                dve.wait_ge(xh_ready.sem, xh_ready.after(l, 4 * i + c + 1))
                V.tensor_tensor(XL[:, 2 * c:2 * c + 2], XN[:, 2 * c:2 * c + 2], XH[:, 2 * c:2 * c + 2].bitcast(F32),
                                ALU.subtract).then_inc(xl_ready.sem, 1)

        def post_norm(l, i):
            for c in range(4):
                dve.wait_ge(ms_ready.sem, ms_ready.after(l, 4 * i + c + 1))
                V.tensor_tensor(SQ[:, 2 * c:2 * c + 2], MS[:, 2 * c:2 * c + 2], MS[:, 2 * c:2 * c + 2], ALU.mult).then_inc(postsq_ready.sem, 1)
            dve.wait_ge(root_ready.sem, root_ready.after(l, 2 * i + 2))
            V.reciprocal(RINV[:], ROOT[:]).then_inc(rinv_ready.sem, 1)
            dve.wait_ge(rinv_ready.sem, rinv_ready.after(l, 2 * i + 2))
            for k in range(DT_):
                V.scalar_tensor_tensor(MS[:, k], MS[:, k], gain(2 * i + 1, k), RINV[:], ALU.mult, ALU.mult).then_inc(scaled_ready.sem, 1)
            for c in range(4):
                dve.wait_ge(scaled_ready.sem, scaled_ready.after(l, 8 * i + 2 * c + 2))
                V.tensor_tensor(X[:, 2 * c:2 * c + 2], X[:, 2 * c:2 * c + 2], MS[:, 2 * c:2 * c + 2], ALU.add).then_inc(x_ready.sem, 1)

        def ffn(l, f, up, down):
            def pair(j, par, hl, gate, up_):
                split_lo(l, ahead(gate))
                dve.wait_ge(sg_ready.sem, sg_ready.after(l, j) + 1)
                dve.wait_ge(unit_done.sem, unit_done.after(l, up_[1]) + 1)
                V.tensor_tensor(HF[:, par], SG[:, par], PS[:, 4 * par + 2:4 * par + 4, 0:T], ALU.mult).then_inc(h_ready.sem, 1)
                split_lo(l, ahead(up_))
                dve.wait_ge(hh_ready.sem, hh_ready.after(l, j) + 1)
                V.tensor_tensor(HL[:, hl, :], HF[:, par], HH[:, hl, :].bitcast(F32), ALU.subtract).then_inc(hl_ready.sem, 1)

            with dve.Fori(0, 5) as i:
                for s in range(2):
                    pair(i * 2 + (11 * f + s), s, ds(i * 4 + 2 * s, 2), unit(up + 2 * s, i, 4), unit(up + 2 * s + 1, i, 4))
            pair(11 * f + 10, 0, slice(20, 22), unit(up + 20), unit(up + 21))
            with dve.Fori(0, 4) as i:
                split_lo(l, unit(down + 2, i))
                split_lo(l, unit(down + 3, i))
            split_lo(l, unit(down + 10))
            if f == 0:
                split_lo(l, unit(down + 11))
                split_lo(l, unit(down + 12))

        def halves(buf, m):
            if m <= 4:
                v = buf.rearrange("p h t -> p (h t)").rearrange("p (n two m) -> p n two m", two=2, m=m)
                return v[:, :, 0, :], v[:, :, 1, :]
            v = buf[:, :, 0:SEQ].rearrange("p h (n two m) -> p h n two m", two=2, m=m)
            return v[:, :, :, 0, :], v[:, :, :, 1, :]

        def last(half, m):
            return (half[:, :, m - 1:m] if len(half.shape) == 3 else half[:, :, :, m - 1:m]).broadcast_to(list(half.shape))

        def pick(l, g, i):
            b = 3 * (i % 2)
            for n in range(2):
                q = V.copy_predicated(APR[:, n], MASK[:, i:i + 1, :].broadcast_to([P, HG, P]),
                                      PS[:, b + n, :].rearrange("p (h t) -> p h t", t=P))
            if i < 4:
                q = V.copy_predicated(ASM[:], MASK[0:NS, i:i + 1, 0:NS].broadcast_to([NS, HG, NS]),
                                      PS[0:NS, b + 2, 0:HG * NS].rearrange("p (h t) -> p h t", t=NS))
            q.then_inc(picked.sem, 1)

        def decays(l, g):
            pre, kf = PROJ[g][0:2]
            dve.wait_ge(fsig_ready.sem, fsig_ready.after(l, g * 4 + 4))
            for h in range(HG):
                w = [col(g * 4 + (b + h)) for b in (C_OML, C_LBF)]
                V.tensor_scalar(pre[:, h], pre[:, h], w[0], w[1], ALU.mult, ALU.add).then_inc(fk_ready.sem, 1)
                V.tensor_scalar(kf[:, h], kf[:, h], w[0], None, ALU.mult).then_inc(fk_ready.sem, 1)

        def hgrn(l, g):
            PRE, KF, QF, _, GO = PROJ[g]

            def beside(place):
                for j in BESIDE[g][place]:
                    split_lo(l, ahead(unit(U_IN + 8 + 8 * g + j)))

            dve.wait_ge(hgz_ready.sem, hgz_ready.after(l, g * 3 + 3))
            dve.wait_ge(fk_ready.sem, fk_ready.after(l, g * 8 + 8))
            dve.wait_ge(q_ready.sem, q_ready.after(l, g * 2 + 2))
            for i, m in enumerate(LEVELS, 1):
                w1, w2 = halves(W[:, i % 2], m)
                k1, _ = halves(KF[:], m)
                _, q2 = halves(QF[:], m)
                s1, _ = halves(SUF[:], m)
                p1, p2 = halves(PRE[:], m)
                if i > 1:
                    dve.wait_ge(tree_ready.sem, tree_ready.after(l, g * 14 + 2 * (i - 1)))
                V.tensor_tensor(w1, k1, s1, ALU.mult).then_inc(w_ready.sem, 1)
                V.tensor_tensor(w2, q2, p2, ALU.mult).then_inc(w_ready.sem, 1)
                if i > 2:
                    beside(i - 2)
                V.tensor_tensor(s1, s1, last(p2, m), ALU.mult).then_inc(tree_ready.sem, 1)
                dve.wait_ge(tree_ready.sem, tree_ready.after(l, g * 14 + 2 * i - 1))
                dve.wait_ge(score_ready.sem, score_ready.after(l, g * 8 + i))
                V.tensor_tensor(p2, p2, last(p1, m), ALU.mult).then_inc(tree_ready.sem, 1)
                pick(l, g, i - 1)
            dve.wait_ge(tree_ready.sem, tree_ready.after(l, g * 14 + 14))
            V.tensor_tensor(W[:, 0], QF[:], PRE[:], ALU.mult).then_inc(w_ready.sem, 1)
            beside(6)
            dve.wait_ge(picked.sem, picked.after(l, g * 8 + 7))
            dve.wait_ge(score_ready.sem, score_ready.after(l, g * 8 + 8))
            V.tensor_tensor(W[:, 1], KF[:], SUF[:], ALU.mult).then_inc(w_ready.sem, 1)
            pick(l, g, 7)
            beside(7)
            dve.wait_ge(sp2_ready.sem, sp2_ready.after(l, g + 1))
            dve.wait_ge(s1_ready.sem, s1_ready.after(l, g + 1))
            dve.wait_ge(s2_stored.sem, s2_stored.after(l, g * 16))
            for h in range(HG):
                q = V.scalar_tensor_tensor(S2[:, h], S1[:, h], PRE[:, h, SEQ - 1:SEQ], PS[:, 5, h * KD:(h + 1) * KD], ALU.mult, ALU.add)
            q.then_inc(s2_ready.sem, 1)
            for h in range(HG):
                dve.wait_ge(decayed.sem, decayed.after(l, g * 4 + h + 1))
                dve.wait_ge(upd_ready.sem, upd_ready.after(l, g * 4 + h + 1))
                s = SIN[h % 2][:].rearrange("p (c b) v -> p c (b v)", c=2)
                V.tensor_tensor(s, s, PS[:, 4:6, :], ALU.add).then_inc(snew_ready.sem, 1)
                beside(8 + h)
            if g == 0:
                decays(l, 1)
            dve.wait_ge(oroot_ready.sem, oroot_ready.after(l, g + 1))
            V.reciprocal(RTO[:], RTO[:]).then_inc(orinv_ready.sem, 1)
            if g == 0:
                beside(12)
            dve.wait_ge(orinv_ready.sem, orinv_ready.after(l, g + 1))
            dve.wait_ge(go_ready.sem, go_ready.after(l, g * 2 + 2))
            V.tensor_tensor(GO[:], GO[:], RTO[:], ALU.mult).then_inc(gor_ready.sem, 1)
            dve.wait_ge(gor_ready.sem, gor_ready.after(l, g + 1))
            for h in range(HG):
                V.scalar_tensor_tensor(SQO[:, h], PS[:, h, 0:T], col(C_HGN + 4 * g + h), GO[:, h],
                                       ALU.mult, ALU.mult).then_inc(ohg_ready.sem, 1)
            dve.wait_ge(ohh_ready.sem, ohh_ready.after(l, g + 1))
            c = slice(4 * g, 4 * g + 4)
            V.tensor_tensor(HL[:, c, :], SQO[:], HH[:, c, :].bitcast(F32), ALU.subtract).then_inc(ohl_ready.sem, 1)
            if g == 1:
                beside(12)

        def dt_first(l):
            dve.wait_ge(dtp_ready.sem, dtp_ready.after(l, 1))
            for r, n in ROWS:
                V.tensor_tensor(DTW[r, 0, n], PS[r, 7, 0:48].rearrange("p (n h) -> p n h", h=MH)[:, n],
                                PAR[r, C_DTB:C_DTB + MH].rearrange("p (o h) -> p o h", o=1).broadcast_to([r.stop, n.stop - n.start, MH]),
                                ALU.add).then_inc(dt_step.sem, 1)
            dve.wait_ge(dt_step.sem, dt_step.after(l, 2))
            for r, n in ROWS:
                V.scalar_tensor_tensor(DTW[r, 1, n], DTW[r, 0, n], -1.0, DTW[r, 0, n], ALU.mult, ALU.min).then_inc(dt_step.sem, 1)

        def dt_rest(l):
            def step(k, f):
                dve.wait_ge(dt_step.sem, dt_step.after(l, 2 * k))
                for r, n in ROWS:
                    f(r, n).then_inc(dt_step.sem, 1)
            dve.wait_ge(dt_exp.sem, dt_exp.after(l, 4))
            step(2, lambda r, n: V.tensor_scalar(DTW[r, 1, n], DTW[r, 2, n], 1.0, -1.0, ALU.add, ALU.add))
            step(3, lambda r, n: V.tensor_scalar(DTW[r, 4, n], DTW[r, 1, n], 1e-30, None, ALU.max))
            step(4, lambda r, n: V.reciprocal(DTW[r, 4, n], DTW[r, 4, n]))
            step(5, lambda r, n: V.tensor_tensor(DTW[r, 3, n], DTW[r, 3, n], DTW[r, 4, n], ALU.mult))
            step(6, lambda r, n: V.scalar_tensor_tensor(DTW[r, 3, n], DTW[r, 1, n], 0.0, DTW[r, 3, n], ALU.is_equal, ALU.add))
            step(7, lambda r, n: V.tensor_tensor(DTW[r, 3, n], DTW[r, 3, n], DTW[r, 2, n], ALU.mult))
            step(8, lambda r, n: V.scalar_tensor_tensor(DTT[r, n], DTW[r, 0, n], 0.0, DTW[r, 3, n], ALU.max, ALU.add))
            step(9, lambda r, n: V.tensor_tensor(
                AT[r, n], DTT[r, n],
                PAR[r, C_A:C_A + MH].rearrange("p (o h) -> p o h", o=1).broadcast_to([r.stop, n.stop - n.start, MH]), ALU.mult))

        def masked_a(l, i):
            if i:
                dve.wait_ge(seg_ready.sem, seg_ready.after(l, i))
            V.tensor_tensor(L1[:], USTR[:].rearrange("p (n h s) -> p n h s", n=1, h=1).broadcast_to([P, 2, 2, P]),
                            AT[:, 0:2, 2 * i:2 * i + 2].rearrange("p n (h o) -> p n h o", o=1).broadcast_to([P, 2, 2, P]),
                            ALU.mult).then_inc(l1_ready.sem, 1)
            V.tensor_tensor(L1S[:], USTR8[:].rearrange("p (h s) -> p h s", h=1).broadcast_to([NS, 2, NS]),
                            AT[0:NS, 2, 2 * i:2 * i + 2].rearrange("p (h o) -> p h o", o=1).broadcast_to([NS, 2, NS]),
                            ALU.mult).then_inc(l1_ready.sem, 1)

        def mamba(l):
            split_lo(l, ahead(unit(U_IN + 22)))
            for q in range(3):
                for j in range(3):
                    for c in range(4):
                        k = 4 * q + c
                        if j == 0:
                            dve.wait_ge(acc_ready.sem, acc_ready.after(l, k + 1))
                        else:
                            dve.wait_ge(tap_ready.sem, tap_ready.after(l, 12 * q + 4 * (j - 1) + c + 1))
                        V.scalar_tensor_tensor(ACC[:, c, 0:CVW], XB[:, k, j:j + CVW], col(C_CW + CT * j + k), ACC[:, c, 0:CVW],
                                               ALU.mult, ALU.add).then_inc(tap_ready.sem, 1)
                split_lo(l, ahead(unit(U_IN + 23 + q)))
            dve.wait_ge(dt_step.sem, dt_step.after(l, 20))
            for j, n in enumerate(TURNS):
                tn = TILES[n][1]
                dve.wait_ge(xturn_ready.sem, xturn_ready.after(l, j + 1))
                b = 3 if j == 1 else 0
                V.tensor_tensor(DTX[0:tn, n, :].rearrange("p (h d) -> p h d", d=HD),
                                PS[0:tn, b:b + 2, :].rearrange("p b (h d) -> p (b h) d", d=HD),
                                DTT[0:tn, n, :].rearrange("p (h o) -> p h o", o=1).broadcast_to([tn, MH, HD]),
                                ALU.mult).then_inc(dtx_ready.sem, 1)
                dve.wait_ge(g_ready.sem, g_ready.after(l, j + 1))
                tri = TRI if n < 2 else TRI8
                V.tensor_tensor(GM[0:tn, n, :, 0:tn], PS[0:tn, 6 + j % 2, 0:2 * P].rearrange("p (g t) -> p g t", g=2)[:, :, 0:tn],
                                tri[:].rearrange("p (o t) -> p o t", o=1).broadcast_to([tn, 2, tn]), ALU.mult).then_inc(gm_ready.sem, 1)
            dve.wait_ge(gm_ready.sem, gm_ready.after(l, 3))

            def weigh(i):
                g = i // 4
                dve.wait_ge(e_ready.sem, e_ready.after(l, 3 * i + 3))
                V.tensor_tensor(ST[:], ST[:], GM[:, 0:2, g:g + 1, :].broadcast_to([P, 2, 2, P]), ALU.mult).then_inc(st_ready.sem, 1)
                V.tensor_tensor(STS[:], STS[:], GM[0:NS, 2, g:g + 1, 0:NS].broadcast_to([NS, 2, NS]), ALU.mult).then_inc(st_ready.sem, 1)

            masked_a(l, 0)
            weigh(0)
            masked_a(l, 1)
            for i in range(PAIRS):
                dve.wait_ge(y_ready.sem, y_ready.after(l, i + 1))
                V.scalar_tensor_tensor(XC[:, i], XC[:, i], col(C_DSK + i), PS[:, 0, 0:T], ALU.mult, ALU.add).then_inc(ystep.sem, 1)
                dve.wait_ge(sp_stored[i % 2].sem, sp_stored[i % 2].after(l, i // 2 * 16))
                V.tensor_copy(SP[:, i % 2], PS[:, 0, T:T + P]).then_inc(spc_ready.sem, 1)
                if i + 2 < PAIRS:
                    masked_a(l, i + 2)
                if i + 1 < PAIRS:
                    weigh(i + 1)
                dve.wait_ge(y2_ready.sem, y2_ready.after(l, i + 1))
                if i:
                    dve.wait_ge(ydone.sem, ydone.after(l, i))
                V.tensor_tensor(Y2[:, P:T], PS[:, 1, P:T], EC[:, i % 2, P:T], ALU.mult).then_inc(ystep.sem, 1)
                dve.wait_ge(spc_ready.sem, spc_ready.after(l, i + 1))
                V.scalar_tensor_tensor(SP[:, i % 2], SP[:, i % 2], EC[:, i % 2, SEQ - 1:SEQ], PS[:, 1, 0:P],
                                       ALU.mult, ALU.add).then_inc(spn_ready.sem, 1)
                dve.wait_ge(ystep.sem, ystep.after(l, 2 * i + 2))
                V.tensor_tensor(XC[:, i, P:T], XC[:, i, P:T], Y2[:, P:T], ALU.add).then_inc(ydone.sem, 1)
                dve.wait_ge(supd_ready.sem, supd_ready.after(l, i + 1))
                s = SIN[i % 3]
                for b in range(NB):
                    e = SEQ + SL * b + SL - 1
                    q = V.scalar_tensor_tensor(s[:, b], s[:, b], EC[:, i % 2, e:e + 1], PS[:, 2 + b // 4, (b % 4) * P:(b % 4 + 1) * P],
                                               ALU.mult, ALU.add)
                q.then_inc(ssm_new.sem, 1)
            dve.wait_ge(z_ready.sem, z_ready.after(l, 4))
            dve.wait_ge(ydone.sem, ydone.after(l, PAIRS))
            for g in range(2):
                V.tensor_tensor(Z[:, 4 * g:4 * g + 4], XC[:, 4 * g:4 * g + 4], Z[:, 4 * g:4 * g + 4], ALU.mult).then_inc(yz_ready.sem, 1)
            dve.wait_ge(sroot_ready.sem, sroot_ready.after(l, 1))
            V.reciprocal(SQS[:, 0:2], SQS[:, 0:2]).then_inc(srinv_ready.sem, 1)
            dve.wait_ge(srinv_ready.sem, srinv_ready.after(l, 1))
            for k in range(PAIRS):
                V.scalar_tensor_tensor(Z[:, k], Z[:, k], col(C_SSN + k), SQS[:, k // 4], ALU.mult, ALU.mult).then_inc(ysn_ready.sem, 1)
            for c in range(4):
                dve.wait_ge(yh_ready.sem, yh_ready.after(l, c + 1))
                V.tensor_tensor(HL[:, 8 + 2 * c:10 + 2 * c, :], Z[:, 2 * c:2 * c + 2], HH[:, 8 + 2 * c:10 + 2 * c, :].bitcast(F32),
                                ALU.subtract).then_inc(yl_ready.sem, 1)
            with dve.Fori(0, 4) as i:
                split_lo(l, unit(U_OUT + 2, i))
                split_lo(l, unit(U_OUT + 3, i))

        with dve.Fori(0, LAYERS) as l:
            V.tensor_copy(PAR[:].rearrange("p (o c) -> p o c", o=1), PALL[:, ds(l, 1), :]).then_inc(par_ready.sem, 1)
            split_lo(l, unit(0))
            split_lo(l, unit(1))
            dve.wait_ge(par_ready.sem, par_ready.after(l, 1))
            pre_norm(l, 0)
            ffn(l, 0, U_UP1, U_DOWN1)
            post_norm(l, 0)
            pre_norm(l, 1)
            dt_first(l)
            for c in range(8):
                split_lo(l, ahead(unit(U_IN + c)))
                if c == 3:
                    dt_rest(l)
                if c == 5:
                    decays(l, 0)
            for g in range(2):
                hgrn(l, g)
            mamba(l)
            post_norm(l, 1)
            pre_norm(l, 2)
            ffn(l, 1, U_UP2, U_DOWN2)
            post_norm(l, 2)

    @block.tensor
    def _(pe):
        pe.wait_ge(consts_done.sem, 1)
        pe.wait_ge(x_rows_in.sem, 32)
        for n, (t0, tn) in enumerate(TILES):
            for k in range(DT_):
                c = (k % 4) * P
                q = pe.transpose(PS[:, 2 * n + k // 4, c:c + tn], XROW[0:tn, n, k * P:(k + 1) * P], IDENT[0:tn, 0:tn])
            q.then_inc(x_turned.sem, 1)
        pe.wait_ge(params_in.sem, 16 * 12)
        for l in range(LAYERS):
            pe.transpose(PS[:, 6, l * NROW_A:(l + 1) * NROW_A], PROWA[:, l, :], IDENT[0:NROW_A, 0:NROW_A])
            q = pe.transpose(PS[:, 7, l * 48:(l + 1) * 48], PROWB[:, l, :], IDENT[0:48, 0:48])
        q.then_inc(params_turned.sem, 1)
        pe.wait_ge(x_ready.sem, x_ready.before)
        for _ in range(2):
            pe.matmul(PS[:, 5, 0:8], ONES[:], ONES[:, 0:8], start=True, stop=True).then_inc(unit_done.sem, 1)

        def dense(out, slot, c, hi, lo, first, last_):
            wh, wl = WH[:, slot, c:c + P], WL[:, slot, c:c + P]
            pe.matmul(out, wh, hi, start=first, stop=False)
            pe.matmul(out, wh, lo, start=False, stop=False)
            return pe.matmul(out, wl, hi, start=False, stop=last_)

        def by_columns(l, u, banks, between=None):
            slot, n, _ = u
            pe.wait_ge(lo_ready.sem, lo_ready.after(l, n) + 1)
            for s, b in enumerate(banks):
                if s and between:
                    between()
                for k in range(DT_):
                    q = dense(PS[:, b, 0:T], slot, k * 256 + s * P, XH[:, k], XL[:, k], k == 0, k == DT_ - 1)
            q.then_inc(unit_done.sem, 1)

        def by_rows(l, u, k, first=False, last_=False):
            slot, n, _ = u
            pe.wait_ge(lo_ready.sem, lo_ready.after(l, n) + 1)
            for kk in range(2):
                hi, lo = ((HH[:, k + kk, :], HL[:, k + kk, :]) if isinstance(k, int) else
                          (HH[:, ds(k + kk, 1), :].rearrange("p o t -> p (o t)"), HL[:, ds(k + kk, 1), :].rearrange("p o t -> p (o t)")))
                for m in range(DT_):
                    q = dense(PS[:, m, 0:T], slot, kk * D + m * P, hi, lo, first and kk == 0, last_ and kk == 1)
            q.then_inc(unit_done.sem, 1)

        def stat(l, n, sem, per_tile):
            for k in range(DT_):
                if k % 2 == 0:
                    pe.wait_ge(sem.sem, sem.after(l, per_tile + k // 2 + 1))
                q = pe.matmul(PS[:, 0, 0:T], ONES[:], SQ[:, k], start=(k == 0), stop=(k == DT_ - 1))
            q.then_inc(stat_ready.sem, 1)

        def ffn(l, f, up, down):
            with pe.Fori(0, 5) as i:
                pe.wait_ge(xl_ready.sem, xl_ready.after(l, 8 * f + 4))
                for s in range(2):
                    pe.wait_ge(h_ready.sem, h_ready.after(l, i * 2 + (11 * f + s)) + (1 - 2))
                    by_columns(l, unit(up + 2 * s, i, 4), (4 * s, 4 * s + 1))
                    by_columns(l, unit(up + 2 * s + 1, i, 4), (4 * s + 2, 4 * s + 3))
            pe.wait_ge(h_ready.sem, h_ready.after(l, 11 * f + 9))
            by_columns(l, unit(up + 20), (0, 1))
            by_columns(l, unit(up + 21), (2, 3))
            pe.wait_ge(hl_ready.sem, hl_ready.after(l, 11 * f + 11))
            by_rows(l, unit(down), 0, first=True)
            with pe.Fori(0, 4) as i:
                by_rows(l, unit(down + 1, i), i * 4 + 2)
                by_rows(l, unit(down + 2, i), i * 4 + 4)
            by_rows(l, unit(down + 9), 18)
            by_rows(l, unit(down + 10), 20, last_=True)
            stat(l, 2 * f, postsq_ready, 8 * f)

        def scores(l, g, i):
            b = 3 * (i % 2)
            lhs, rhs = (PROJ[g][1][:], PROJ[g][2][:]) if i == 0 else (W[:, i % 2], W[:, i % 2])
            for h in range(HG):
                for n, (t0, tn) in enumerate(TILES if i < 4 else TILES[:2]):
                    q = pe.matmul(PS[0:tn, b + n, h * tn:(h + 1) * tn], lhs[:, h, t0:t0 + tn], rhs[:, h, t0:t0 + tn],
                                  start=True, stop=True)
            q.then_inc(score_ready.sem, 1)

        def turn(src, n, bank, sem):
            t0, tn = TILES[n]
            for h in range(HG):
                q = pe.transpose(PS[0:tn, bank, h * KD:(h + 1) * KD], src[:, h, t0:t0 + tn], IDENT[:])
            q.then_inc(sem.sem, 1)

        def first_heads(l):
            pe.wait_ge(xl_ready.sem, xl_ready.after(l, 8))
            for c in range(8):
                if c == 3:
                    pe.wait_ge(dt_step.sem, dt_step.after(l, 2))
                if c in (4, 5):
                    pe.wait_ge(fsig_ready.sem, fsig_ready.after(l, 2 * (c - 3)))
                if c in (6, 7):
                    pe.wait_ge(q_ready.sem, q_ready.after(l, c - 5))
                by_columns(l, unit(U_IN + c), (2 * (c % 4), 2 * (c % 4) + 1))

        def evacuated(l, u):
            return ((fsig_ready, 6), (fsig_ready, 8), (q_ready, 3), (q_ready, 4), (v_ready, 3), (v_ready, 4), (go_ready, 3),
                    (go_ready, 4), *((xb_ready, 2 * j + 2) for j in range(6)))[u]

        def hgrn(l, g):
            def beside(place):
                for j in BESIDE[g][place]:
                    u = 8 * g + j
                    if u:
                        s, n = evacuated(l, u - 1)
                        pe.wait_ge(s.sem, s.after(l, n))
                    if place == 12:
                        pe.wait_ge(oroot_ready.sem, oroot_ready.after(l, g + 1))
                    by_columns(l, unit(U_IN + 8 + u), (6, 7))

            pe.wait_ge(v_ready.sem, v_ready.after(l, g * 2 + 2))
            pe.wait_ge(go_ready.sem, go_ready.after(l, g * 2 + 2))
            if g:
                pe.wait_ge(oroot_ready.sem, oroot_ready.after(l, g))
            for j, n in enumerate(TURNS):
                if j == 2:
                    pe.wait_ge(vtok_ready.sem, vtok_ready.after(l, g * 3 + 1))
                turn(PROJ[g][3][:], n, 4 + j % 2, vturn_ready)
            pe.wait_ge(fk_ready.sem, fk_ready.after(l, g * 8 + 8))
            pe.wait_ge(q_ready.sem, q_ready.after(l, g * 2 + 2))
            pe.wait_ge(ohg_ready.sem, ohg_ready.after(l, g * 4))
            scores(l, g, 0)
            for i in range(1, 8):
                pe.wait_ge(w_ready.sem, w_ready.after(l, g * 16 + 2 * i))
                if i == 1:
                    pe.wait_ge(vtok_ready.sem, vtok_ready.after(l, g * 3 + 3))
                else:
                    pe.wait_ge(picked.sem, picked.after(l, g * 8 + i - 1))
                scores(l, g, i)
                if i < 7:
                    beside(i)
            beside(7)
            pe.wait_ge(w_ready.sem, w_ready.after(l, g * 16 + 16))
            for j, n in enumerate(TURNS):
                if j == 2:
                    pe.wait_ge(ktok_ready.sem, ktok_ready.after(l, g * 3 + 1))
                turn(W[:, 1], n, j % 2, kturn_ready)
            pe.wait_ge(picked.sem, picked.after(l, g * 8 + 8))
            for n, s in enumerate((sp1_ready, sp2_ready)):
                pe.wait_ge(ktok_ready.sem, ktok_ready.after(l, g * 3 + 2 * n + 1))
                for h in range(HG):
                    c = slice(h * KD, (h + 1) * KD)
                    q = pe.matmul(PS[:, 4 + n, c], KTOK[:, n, c], VTOK[:, n, c], start=True, stop=True)
                q.then_inc(s.sem, 1)
            pe.wait_ge(s1_ready.sem, s1_ready.after(l, g + 1))
            for h in range(HG):
                c = slice(h * KD, (h + 1) * KD)
                pe.wait_ge(hs_in[h % 2].sem, hs_in[h % 2].after(l, g * 32 + (h // 2 + 1) * 16))
                pe.matmul(PS[:, h, 0:P], VTOK[:, 0, c], APR[:, 0, h], start=True, stop=True)
                pe.matmul(PS[:, h, P:SEQ], VTOK[:, 1, c], APR[:, 1, h], start=True, stop=False, skip_group_check=True)
                pe.matmul(PS[:, h, P:SEQ], S1[:, h], W[:, 0, h, P:SEQ], start=False, stop=True, skip_group_check=True)
                pe.matmul(PS[:, h, SEQ:T], VTOK[0:NS, 2, c], ASM[:, h], start=True, stop=False, skip_group_check=True)
                for b in range(NB):
                    t = SEQ + SL * b
                    q = pe.matmul(PS[:, h, t:t + SL], SIN[h % 2][:, b], W[:, 0, h, t:t + SL], start=False, stop=(b == NB - 1),
                                  skip_group_check=True)
                q.then_inc(o_ready.sem, 1)
                pe.wait_ge(vm_ready.sem, vm_ready.after(l, g * 4 + h + 1))
                if h:
                    pe.wait_ge(snew_ready.sem, snew_ready.after(l, g * 4 + h))
                else:
                    pe.wait_ge(s2_ready.sem, s2_ready.after(l, g + 1))
                for b in range(2):
                    q = pe.matmul(PS[:, 4 + b, :], KTOK[0:NS, 2, c], VM[:, 4 * b:4 * b + 4, :].rearrange("p b v -> p (b v)"),
                                  start=True, stop=True)
                q.then_inc(upd_ready.sem, 1)
                beside(8 + h)
            pe.wait_ge(snew_ready.sem, snew_ready.after(l, g * 4 + 4))
            s, n = evacuated(l, 8 * g + max(j for place in range(12) for j in BESIDE[g][place]))
            pe.wait_ge(s.sem, s.after(l, n))
            pe.wait_ge(sqo_ready.sem, sqo_ready.after(l, g * 4 + 4))
            for h in range(HG):
                q = pe.matmul(PS[:, 4 + h, 0:T], ONES[:], SQO[:, h], start=True, stop=True)
            q.then_inc(ostat_ready.sem, 1)
            beside(12)

        def mamba(l):
            pe.wait_ge(oroot_ready.sem, oroot_ready.after(l, 2))

            def for_turns():
                pe.wait_ge(ohg_ready.sem, ohg_ready.after(l, 8))
                pe.wait_ge(crow_in.sem, crow_in.after(l, 16))

            by_columns(l, unit(U_IN + 22), (4, 5), between=for_turns)
            for c in range(CT):
                q = pe.transpose(PS[:, 0, c * 24:(c + 1) * 24], CROW[:, c * P:(c + 1) * P], IDENT[0:24, 0:24])
            q.then_inc(cturn_ready.sem, 1)
            for j in range(1, 4):
                if j == 1:
                    pe.wait_ge(xb_ready.sem, xb_ready.after(l, 12))
                else:
                    pe.wait_ge(z_ready.sem, z_ready.after(l, j - 1))
                by_columns(l, unit(U_IN + 22 + j), (4 + 2 * (j % 2), 5 + 2 * (j % 2)))
            pe.wait_ge(dt_step.sem, dt_step.after(l, 20))
            for n, (t0, tn) in enumerate(TILES):
                u = USTR if n < 2 else USTR8
                q = pe.matmul(PS[0:tn, 1, n * MH:(n + 1) * MH], u[:], AT[0:tn, n, :], start=True, stop=True)
            q.then_inc(remp_ready.sem, 1)
            pe.wait_ge(xc_ready.sem, xc_ready.after(l, 6))
            pe.wait_ge(z_ready.sem, z_ready.after(l, 4))
            pe.wait_ge(rem_ready.sem, rem_ready.after(l, 2))
            for j, n in enumerate(TURNS):
                t0, tn = TILES[n]
                b, bb = (3, 5) if j == 1 else (0, 2)
                if j == 2:
                    pe.wait_ge(dtx_ready.sem, dtx_ready.after(l, 1))
                    pe.wait_ge(btok_ready.sem, btok_ready.after(l, 1))
                    pe.wait_ge(gm_ready.sem, gm_ready.after(l, 1))
                for k in range(10):
                    c = (k % 4) * P
                    q = pe.transpose(PS[0:tn, (b + k // 4) if k < 8 else bb, c:c + P], XC[:, k, t0:t0 + tn], IDENT[:])
                q.then_inc(xturn_ready.sem, 1)
                for g in range(2):
                    q = pe.matmul(PS[0:tn, 6 + j % 2, g * P:g * P + tn], XC[:, 8 + g, t0:t0 + tn], XC[:, 10 + g, t0:t0 + tn],
                                  start=True, stop=True)
                q.then_inc(g_ready.sem, 1)
            pe.wait_ge(wx_ready.sem, wx_ready.after(l, 1))
            pe.wait_ge(dtx_ready.sem, dtx_ready.after(l, 3))
            for g in range(2):
                q = pe.matmul(PS[:, g, :], BTOK[:, 0, g * P:(g + 1) * P], WX[:, 0, g * 512:(g + 1) * 512], start=True, stop=True)
            q.then_inc(ht1p_ready.sem, 1)
            pe.wait_ge(gm_ready.sem, gm_ready.after(l, 3))
            pe.wait_ge(btok_ready.sem, btok_ready.after(l, 3))
            pe.wait_ge(cs_ready.sem, cs_ready.after(l, 2))
            for c in range(CT):
                q = pe.transpose(PS[0:27, 5 + c // 4, (c % 4) * P:(c % 4 + 1) * P], CS[:, c, :], IDENT[:])
            q.then_inc(csturn_ready.sem, 1)
            pe.wait_ge(co_ready.sem, co_ready.after(l, 1))
            pe.wait_ge(wx_ready.sem, wx_ready.after(l, 3))
            def segment_sums(i):
                pe.wait_ge(l1_ready.sem, l1_ready.after(l, 2 * i + 2))
                if i:
                    pe.wait_ge(e_ready.sem, e_ready.after(l, 3 * i))
                for h in range(2):
                    for n in range(2):
                        pe.matmul(PS[:, 4, (2 * n + h) * P:(2 * n + h + 1) * P], L1[:, n, h], TRI[:], start=True, stop=True)
                    pe.matmul(PS[0:NS, 5, h * NS:(h + 1) * NS], L1S[:, h], TRI8[:], start=True, stop=True)
                for n, (t0, tn) in enumerate(TILES):
                    tri = TRI if n < 2 else TRI8
                    for h in range(2):
                        q = pe.matmul(PS[HD * h:HD * h + HD, 5, P + t0:P + t0 + tn],
                                      AT[0:tn, n, 2 * i + h:2 * i + h + 1].broadcast_to([tn, HD]), tri[:], start=True, stop=True)
                q.then_inc(seg_ready.sem, 1)

            segment_sums(0)
            for i in range(PAIRS):
                g = i // 4
                cc = slice(i * P, (i + 1) * P)
                pe.wait_ge(st_ready.sem, st_ready.after(l, 2 * i + 2))
                if i:
                    pe.wait_ge(spc_ready.sem, spc_ready.after(l, i))
                else:
                    pe.wait_ge(ht1_ready.sem, ht1_ready.after(l, 1))
                for h in range(2):
                    for n, (t0, tn) in enumerate(TILES):
                        c = (2 * i + h) * HD
                        pe.matmul(PS[HD * h:HD * h + HD, 0, t0:t0 + tn], DTX[0:tn, n, c:c + HD],
                                  ST[:, n, h] if n < 2 else STS[:, h], start=True, stop=True)
                pe.matmul(PS[:, 0, T:T + P], WX[:, 0, cc], BTOK[:, 0, g * P:(g + 1) * P], start=True, stop=True
                          ).then_inc(y_ready.sem, 1)
                pe.wait_ge(ms_in[i % 3].sem, ms_in[i % 3].after(l, (i // 3 + 1) * 16))
                if i:
                    pe.wait_ge(hts_ready.sem, hts_ready.after(l, i))
                for b in range(NB):
                    q = pe.transpose(PS[:, 6 + b // 4, (b % 4) * P:(b % 4 + 1) * P], SIN[i % 3][:, b], IDENT[:])
                q.then_inc(hts_turned.sem, 1)
                if i + 1 < PAIRS:
                    segment_sums(i + 1)
                pe.wait_ge(hts_ready.sem, hts_ready.after(l, i + 1))
                if i:
                    pe.wait_ge(spn_ready.sem, spn_ready.after(l, i))
                pe.matmul(PS[:, 1, P:SEQ], HT1[:, cc], XC[:, 10 + g, P:SEQ], start=True, stop=True)
                for b in range(NB):
                    t = SEQ + SL * b
                    pe.matmul(PS[:, 1, t:t + SL], HTS[:, b], XC[:, 10 + g, t:t + SL], start=True, stop=True)
                pe.matmul(PS[:, 1, 0:P], WX[:, 1, cc], BTOK[:, 1, g * P:(g + 1) * P], start=True, stop=True
                          ).then_inc(y2_ready.sem, 1)
                pe.wait_ge(bmk_ready.sem, bmk_ready.after(l, g + 1))
                if i:
                    pe.wait_ge(ssm_new.sem, ssm_new.after(l, i))
                for b in range(2):
                    q = pe.matmul(PS[:, 2 + b, :], WX[0:NS, 2, cc], BMK[:, 4 * b:4 * b + 4, :].rearrange("p b n -> p (b n)"),
                                  start=True, stop=True)
                q.then_inc(supd_ready.sem, 1)
            for g in range(2):
                pe.wait_ge(sqs_ready.sem, sqs_ready.after(l, g + 1))
                for k in range(4):
                    q = pe.matmul(PS[:, 4 + g, 0:T], ONES[:], SQS[:, 4 * g + k], start=(k == 0), stop=(k == 3))
            q.then_inc(sstat_ready.sem, 1)
            pe.wait_ge(ohl_ready.sem, ohl_ready.after(l, 2))
            pe.wait_ge(yl_ready.sem, yl_ready.after(l, 4))
            by_rows(l, unit(U_OUT), 0, first=True)
            with pe.Fori(0, 3) as i:
                by_rows(l, unit(U_OUT + 1, i), i * 4 + 2)
                by_rows(l, unit(U_OUT + 2, i), i * 4 + 4)
            by_rows(l, unit(U_OUT + 7), 14, last_=True)
            stat(l, 1, postsq_ready, 4)

        with pe.Fori(0, LAYERS) as l:
            stat(l, 0, presq_ready, 0)
            ffn(l, 0, U_UP1, U_DOWN1)
            stat(l, 1, presq_ready, 4)
            pe.wait_ge(xn_ready.sem, xn_ready.after(l, 16))
            pe.wait_ge(wdt_in.sem, wdt_in.after(l, 16))
            for n, (t0, tn) in enumerate(TILES):
                for k in range(DT_):
                    q = pe.matmul(PS[0:tn, 7, n * MH:(n + 1) * MH], XN[:, k, t0:t0 + tn], WDT[:, k], start=(k == 0), stop=(k == DT_ - 1))
            q.then_inc(dtp_ready.sem, 1)
            first_heads(l)
            for g in range(2):
                hgrn(l, g)
            mamba(l)
            stat(l, 2, presq_ready, 8)
            ffn(l, 1, U_UP2, U_DOWN2)
        for n, (t0, tn) in enumerate(TILES):
            pe.wait_ge(x_ready.sem, x_ready.after(LAYERS, 0))
            for k in range(DT_):
                q = pe.transpose(PS[0:tn, 2 * n + k // 4, (k % 4) * P:(k % 4 + 1) * P], X[:, k, t0:t0 + tn], IDENT[:])
            q.then_inc(yout_turned.sem, 1)


_INS = ("x_prompt", "x_sample", "state_hgrn", "state_ssm", "state_conv", "w_in", "hg_lb_logits", "conv_w", "conv_b",
        "dt_bias", "a_log", "d_skip", "hg_norm_w", "ssm_norm_w", "w_out", "ffn1_w_gate", "ffn1_w_up", "ffn1_w_down",
        "ffn2_w_gate", "ffn2_w_up", "ffn2_w_down", "norm_gain")
_OUTS = (("y_prompt", (1, SEQ, D)), ("y_sample", (NB, SL, D)),
         ("hgrn_prompt", (LAYERS, 1, HH_, KD, KD)), ("ssm_prompt", (LAYERS, 1, MH, HD, P)),
         ("conv_prompt", (LAYERS, 1, CW - 1, CT * P)), ("hgrn_sample", (LAYERS, NB, HH_, KD, KD)),
         ("ssm_sample", (LAYERS, NB, MH, HD, P)), ("conv_sample", (LAYERS, NB, CW - 1, CT * P)))


def kernel(**inputs):
    import numpy as np
    import concourse.bacc as bacc
    from concourse.bass_utils import run_bass_kernel_spmd

    nc = bacc.Bacc("TRN2", target_bir_lowering=False, num_devices=1)
    arrays = {name: np.ascontiguousarray(inputs[name]) for name in _INS}
    a = {name: nc.dram_tensor(name, v.shape, F32, kind="ExternalInput").ap() for name, v in arrays.items()}
    o = {name: nc.dram_tensor(name, shape, F32, kind="ExternalOutput").ap() for name, shape in _OUTS}
    trunk(nc, a, o)
    r = run_bass_kernel_spmd(nc, [arrays], core_ids=[0])
    return tuple(r.results[0][name] for name, _ in _OUTS)
```

```python
from contextlib import ExitStack

import concourse.bass as bass
from concourse import mybir

F32 = mybir.dt.float32
F32R = mybir.dt.float32r
I32 = mybir.dt.int32
U8 = mybir.dt.uint8
ACT = mybir.ActivationFunctionType
ALU = mybir.AluOpType
ds = bass.ds

P = 128
LAYERS = 2
D = 1024
DT_ = D // P
SEQ = 256
NB, SL = 8, 8
NS = NB * SL
T = SEQ + NS
FF = 2816
FT = FF // P
KD = 128
HH_ = 8
HG = 4
MH, HD = 16, 64
PAIRS = MH // 2
CT = 12
CW = 4
PADP = CW - 1 + SEQ
PADS = CW - 1 + SL
XBW = PADP + NB * PADS
CVW = XBW - (CW - 1)
D_IN = 6672
COL_Q, COL_F, COL_V, COL_GO, COL_Z, COL_X, COL_DT = 0, 1024, 2048, 3072, 4096, 5120, 6656
EPS = 1e-6
LB_FLOOR = 1e-30
QSCALE = KD ** -0.5

UNIT = 2048
U_UP1 = 0
U_DOWN1 = U_UP1 + FT
U_IN = U_DOWN1 + FT // 2
U_OUT = U_IN + 26
U_UP2 = U_OUT + 8
U_DOWN2 = U_UP2 + FT
UNITS = U_DOWN2 + FT // 2
LEVELS = (1, 2, 4, 8, 16, 32, 64)
SLOT_HEADS = (2, 1, 1)
BESIDE = (((), (), (0,), (), (1,), (), (2,), (3,), (4,), (), (5,), (6,), (7,)),
          ((), (), (0,), (), (1,), (), (2,), (), (3,), (4,), (), (5,), ()))

C_GAIN, C_HGN, C_SSN, C_CB, C_CW, C_LBF, C_OML, C_DSK, C_DTB, C_A, C_END = (
    0, 48, 56, 64, 76, 124, 132, 140, 148, 164, 180)
NROW_A = 84

TILES = ((0, 128), (128, 128), (256, 64))
TURNS = (0, 2, 1)
SPARE = ((0, 0, 192), (1, 192, 128))
ROWS = ((slice(0, 128), slice(0, 2)), (slice(0, 64), slice(2, 3)))


class Signal:

    def __init__(self, ctx, nc, name, per_layer, before=0):
        self.sem = ctx.enter_context(nc.semaphore(name))
        self.per_layer, self.before = per_layer, before

    def after(self, l, n):
        return l * self.per_layer + (n + self.before)


def trunk(nc, a, o):
    with ExitStack() as ctx:
        build(nc, a, o, ctx)


def build(nc, a, o, ctx):
    base = (nc.sbuf_base + 31) // 32 * 32
    top = nc.sbuf_usable_end

    def place(name, shape, dtype, at):
        size = 4 if dtype in (F32, F32R, I32) else 1
        n = size
        for s in shape[1:]:
            n *= s
        assert at + n <= top, (name, at + n, top)
        return nc.alloc_sbuf_tensor_at(name, shape, dtype, offset=at), (at + n + 31) // 32 * 32

    at = base
    X, at = place("X", [P, DT_, T], F32, at)
    at_xh = at
    XH, at = place("XH", [P, DT_, T], F32R, at)
    at_xl = at
    XL, at = place("XL", [P, DT_, T], F32R, at)
    at_hh = at
    HH, at = place("HH", [P, FT, T], F32R, at)
    at_hl = at
    HL, at = place("HL", [P, FT, T], F32R, at)
    RAW, at = place("RAW", [P, 2, UNIT], F32, at)
    WH, at = place("WH", [P, 2, UNIT], F32R, at)
    WL, at = place("WL", [P, 2, UNIT], F32R, at)
    IDENT, at = place("IDENT", [P, P], F32, at)
    ONES, at = place("ONES", [P, P], F32, at)
    TRI, at = place("TRI", [P, P], F32, at)
    USTR, at = place("USTR", [P, P], F32, at)
    TRI8, at = place("TRI8", [NS, NS], F32, at)
    USTR8, at = place("USTR8", [NS, NS], F32, at)
    MASK, at = place("MASK", [P, 8, P], U8, at)
    BLK, at = place("BLK", [NS, NB], F32, at)
    SEL, at = place("SEL", [P, HG, P], F32, at)
    PALL, at = place("PALL", [P, LAYERS, C_END], F32, at)
    PAR, at = place("PAR", [P, C_END], F32, at)
    EPST, at = place("EPST", [P, 1], F32, at)
    FREE, at = place("FREE", [P, 1], F32, at)
    FREEV, at = place("FREEV", [P, 1], F32, at)
    ROOT, at = place("ROOT", [P, T], F32, at)
    RINV, at = place("RINV", [P, T], F32, at)
    WDT, at = place("WDT", [P, DT_, MH], F32, at)
    DTT, at = place("DTT", [P, 3, MH], F32, at)
    DTW, at = place("DTW", [P, 5, 3, MH], F32, at)
    AT, at = place("AT", [P, 3, MH], F32, at)
    REM, at = place("REM", [P, 3, MH], F32, at)
    arena = at

    XROW, e = place("XROW", [P, 3, D], F32, arena)
    PROWA, e = place("PROWA", [NROW_A, LAYERS, P], F32, e)
    PROWB, e = place("PROWB", [48, LAYERS, P], F32, e)
    IT, e = place("IT", [P, P], I32, e)
    IS, e = place("IS", [P, P], I32, e)
    IX, e = place("IX", [P, P], I32, e)
    FIT, e = place("FIT", [P, P], F32, e)
    FIX, e = place("FIX", [P, P], F32, e)
    FGE, e = place("FGE", [P, 8, P], F32, e)
    IBK, e = place("IBK", [NS, NB], I32, e)
    FB, e = place("FB", [NS, 2, NB], F32, e)
    LBW, e = place("LBW", [P, 8, 8], F32, e)
    YROW = XROW

    MS, e = place("MS", [P, DT_, T], F32, arena)
    SQ, e = place("SQ", [P, DT_, T], F32, e)
    SG, e = place("SG", [P, 2, 2, T], F32, e)
    HF, e = place("HF", [P, 2, 2, T], F32, e)
    SR, e = place("SR", [P, 2, 2, T], F32, e)
    XN = MS

    PRE0, e = place("PRE0", [P, HG, T], F32, arena)
    KF0, e = place("KF0", [P, HG, T], F32, e)
    QF0, e = place("QF0", [P, HG, T], F32, e)
    GO0, e = place("GO0", [P, HG, T], F32, e)
    PRE1, _ = place("PRE1", [P, HG, T], F32, at_hh + 8 * T * 4)
    KF1, _ = place("KF1", [P, HG, T], F32, at_hh + 12 * T * 4)
    QF1, _ = place("QF1", [P, HG, T], F32, at_hl + 8 * T * 4)
    VF1, _ = place("VF1", [P, HG, T], F32, at_hl + 12 * T * 4)
    GO1, _ = place("GO1", [P, HG, T], F32, at_hl + 4 * T * 4)
    SUF, e = place("SUF", [P, HG, T], F32, e)
    at_w = e
    W, e = place("W", [P, 2, HG, T], F32, e)
    SQO, _ = place("SQO", [P, HG, T], F32, at_w)
    RTO, _ = place("RTO", [P, T], F32, at_w + HG * T * 4)
    VF0, e = place("VF0", [P, HG, T], F32, e)
    PROJ = ((PRE0, KF0, QF0, VF0, GO0), (PRE1, KF1, QF1, VF1, GO1))
    APR, e = place("APR", [P, 2, HG, P], F32, e)
    ASM, e = place("ASM", [NS, HG, NS], F32, e)
    VTOK, e = place("VTOK", [P, 3, HG * KD], F32, e)
    KTOK, e = place("KTOK", [P, 3, HG * KD], F32, e)
    VM, e = place("VM", [NS, NB, KD], F32, e)
    tail = 16 * T * 4
    SIN0, e0 = place("SIN0", [P, NB, KD], F32, at_hh + tail)
    SIN1, e1 = place("SIN1", [P, NB, KD], F32, at_hl + tail)
    S1, e0 = place("S1", [P, HG, KD], F32, e0)
    S2, e1 = place("S2", [P, HG, KD], F32, e1)
    assert e0 <= at_hl and e1 <= at_hl + FT * T * 4


    at_xb = arena
    XB, e = place("XB", [P, CT, XBW], F32, arena)
    at_acc = e
    ACC, e = place("ACC", [P, 2, 4, XBW], F32, e)
    XC, e = place("XC", [P, CT, T], F32, e)
    Z, _ = place("Z", [P, PAIRS, T], F32, at_hl + 8 * T * 4)
    at_dtx = e
    DTX, e = place("DTX", [P, 3, MH * HD], F32, e)
    BTOK, e = place("BTOK", [P, 3, 2 * P], F32, e)
    GM, em = place("GM", [P, 3, 2, P], F32, at_hh + tail + NB * KD * 4)
    assert em <= at_hl
    CROW, ec = place("CROW", [NB * 3 * 4, CT * P // 4], F32, at_hh + tail + (NB + HG) * KD * 4)
    assert ec <= at_hl
    CS, e2 = place("CS", [P, CT, 27], F32, at_acc)
    SIN2, _ = place("SIN2", [P, NB, KD], F32, at_acc)
    SIN = (SIN0, SIN1, SIN2)
    HSIN2 = [place(f"HSIN2{g}", [P, NB, KD], F32, at_hh + (4, 12)[g] * T * 4)[0] for g in range(2)]
    HSIN = [(SIN0, SIN1, s) for s in HSIN2]
    CO, _ = place("CO", [27, CT * P], F32, at_hh + 8 * T * 4)
    WX, e3 = place("WX", [P, 3, MH * HD], F32, at_xb)
    HT1, e3 = place("HT1", [P, MH * HD], F32, e3)
    assert e3 <= at_xb + CT * XBW * 4
    L1, e4 = place("L1", [P, 2, 2, P], F32, at_xh)
    L1S, e4 = place("L1S", [NS, 2, NS], F32, e4)
    ST, e4 = place("ST", [P, 2, 2, P], F32, e4)
    STS, e4 = place("STS", [NS, 2, NS], F32, e4)
    EC, e4 = place("EC", [P, 2, T], F32, e4)
    Y2, e4 = place("Y2", [P, T], F32, e4)
    SP, e4 = place("SP", [P, 2, P], F32, e4)
    assert e4 <= at_xl
    HTS, e5 = place("HTS", [P, NB, P], F32, at_xl)
    BMK, e5 = place("BMK", [NS, NB, P], F32, e5)
    assert e5 <= at_hh
    SQS, _ = place("SQS", [P, PAIRS, T], F32, at_xb)

    PS = ctx.enter_context(nc.psum_tensor("PS", [P, 8, 512], F32))

    def gain(i, k):
        return PAR[:, C_GAIN + 8 * i + k:C_GAIN + 8 * i + k + 1]

    def col(c):
        return PAR[:, c:c + 1]

    def sig(name, per_layer=0, before=0):
        return Signal(ctx, nc, name, per_layer, before)

    consts_done = sig("consts_done")
    iota_done = sig("iota_done")
    params_in = sig("params_in")
    params_turned = sig("params_turned")
    params_done = sig("params_done")
    x_rows_in = sig("x_rows_in")
    x_turned = sig("x_turned")
    lb_step = sig("lb_step")
    lb_exp = sig("lb_exp")
    const_step = sig("const_step")

    raw_landed = (sig("raw_landed0", 16 * UNITS // 2), sig("raw_landed1", 16 * UNITS // 2))
    hi_ready = sig("hi_ready", UNITS)
    lo_ready = sig("lo_ready", UNITS, 2)
    unit_done = sig("unit_done", UNITS, 2)

    par_ready = sig("par_ready", 1)
    presq_ready = sig("presq_ready", 12)
    postsq_ready = sig("postsq_ready", 12)
    ms_ready = sig("ms_ready", 12)
    stat_ready = sig("stat_ready", 6)
    root_ready = sig("root_ready", 6)
    rinv_ready = sig("rinv_ready", 6)
    scaled_ready = sig("scaled_ready", 24)
    xn_ready = sig("xn_ready", 24)
    xh_ready = sig("xh_ready", 12)
    xl_ready = sig("xl_ready", 12)
    x_ready = sig("x_ready", 12, 3)
    gr_ready = sig("gr_ready", FT)
    sg_ready = sig("sg_ready", FT)
    sr_ready = sig("sr_ready", FT)
    h_ready = sig("h_ready", FT, 2)
    hh_ready = sig("hh_ready", FT)
    hl_ready = sig("hl_ready", FT)
    fsig_ready = sig("fsig_ready", 2 * 4)
    fk_ready = sig("fk_ready", 2 * 8)
    q_ready = sig("q_ready", 2 * 2)
    v_ready = sig("v_ready", 2 * 2)
    go_ready = sig("go_ready", 2 * 2)
    hgz_ready = sig("hgz_ready", 2 * 3)
    w_ready = sig("w_ready", 2 * 16)
    tree_ready = sig("tree_ready", 2 * 14)
    score_ready = sig("score_ready", 2 * 8)
    picked = sig("picked", 2 * 8)
    vturn_ready = sig("vturn_ready", 2 * 3)
    vtok_ready = sig("vtok_ready", 2 * 3)
    kturn_ready = sig("kturn_ready", 2 * 3)
    ktok_ready = sig("ktok_ready", 2 * 3)
    sp1_ready = sig("sp1_ready", 2)
    s1_ready = sig("s1_ready", 2)
    sp2_ready = sig("sp2_ready", 2)
    s2_ready = sig("s2_ready", 2)
    s2_stored = sig("s2_stored", 2 * 16, 16)
    hs_in = tuple(sig(f"hs_in{s}", 2 * 16 * n) for s, n in enumerate(SLOT_HEADS))
    hs_stored = tuple(sig(f"hs_stored{s}", 2 * 16 * n, 16) for s, n in enumerate(SLOT_HEADS))
    vm_ready = sig("vm_ready", HH_)
    upd_ready = sig("upd_ready", HH_)
    decayed = sig("decayed", HH_)
    snew_ready = sig("snew_ready", HH_)
    o_ready = sig("o_ready", HH_)
    sqo_ready = sig("sqo_ready", HH_)
    ostat_ready = sig("ostat_ready", 2)
    oroot_ready = sig("oroot_ready", 2)
    orinv_ready = sig("orinv_ready", 2)
    obc_ready = sig("obc_ready", 4)
    gor_ready = sig("gor_ready", 4)
    ohg_ready = sig("ohg_ready", HH_, 1)
    ohh_ready = sig("ohh_ready", 2)
    ohl_ready = sig("ohl_ready", 2, 1)
    wdt_in = sig("wdt_in", 16)
    dtp_ready = sig("dtp_ready", 1)
    dt_step = sig("dt_step", 20)
    dt_exp = sig("dt_exp", 4)
    remp_ready = sig("remp_ready", 1)
    rem_ready = sig("rem_ready", 2)
    crow_in = sig("crow_in", 16)
    cturn_ready = sig("cturn_ready", 1)
    zeros_ready = sig("zeros_ready", 1)
    pads_ready = sig("pads_ready", 3)
    xb_ready = sig("xb_ready", 12)
    z_ready = sig("z_ready", 4)
    acc_ready = sig("acc_ready", CT)
    tap_ready = sig("tap_ready", 3 * CT)
    xc_ready = sig("xc_ready", 6)
    cs_ready = sig("cs_ready", 2)
    csturn_ready = sig("csturn_ready", 1)
    co_ready = sig("co_ready", 1)
    co_stored = sig("co_stored", 32)
    xturn_ready = sig("xturn_ready", 3)
    dtx_ready = sig("dtx_ready", 3)
    btok_ready = sig("btok_ready", 3)
    g_ready = sig("g_ready", 3)
    gm_ready = sig("gm_ready", 3)
    wx_ready = sig("wx_ready", 3)
    bmk_ready = sig("bmk_ready", 2)
    ht1p_ready = sig("ht1p_ready", 1)
    ht1_ready = sig("ht1_ready", 1)
    l1_ready = sig("l1_ready", 2 * PAIRS)
    seg_ready = sig("seg_ready", PAIRS)
    e_ready = sig("e_ready", 3 * PAIRS)
    st_ready = sig("st_ready", 2 * PAIRS)
    ms_in = tuple(sig(f"ms_in{s}", 16 * n) for s, n in enumerate((3, 3, 2)))
    ms_stored = tuple(sig(f"ms_stored{s}", 16 * n, 16) for s, n in enumerate((3, 3, 2)))
    hts_turned = sig("hts_turned", PAIRS)
    hts_ready = sig("hts_ready", PAIRS)
    y_ready = sig("y_ready", PAIRS)
    y2_ready = sig("y2_ready", PAIRS)
    ydone = sig("ydone", PAIRS)
    ystep = sig("ystep", 2 * PAIRS)
    supd_ready = sig("supd_ready", PAIRS)
    spc_ready = sig("spc_ready", PAIRS)
    spn_ready = sig("spn_ready", PAIRS)
    ssm_new = sig("ssm_new", PAIRS)
    sp_stored = (sig("sp_stored0", 4 * 16, 16), sig("sp_stored1", 4 * 16, 16))
    yz_ready = sig("yz_ready", 2)
    sqs_ready = sig("sqs_ready", 2)
    sstat_ready = sig("sstat_ready", 1)
    sroot_ready = sig("sroot_ready", 2)
    srinv_ready = sig("srinv_ready", 1)
    ysn_ready = sig("ysn_ready", PAIRS)
    yh_ready = sig("yh_ready", 4)
    yl_ready = sig("yl_ready", 4)
    yout_turned = sig("yout_turned")
    yout_ready = sig("yout_ready")
    y_stored = sig("y_stored")

    block = ctx.enter_context(nc.Block())

    def unit(u0, i=None, step=2):
        if i is None:
            return u0 % 2, u0, u0 // 2
        return u0 % 2, i * step + u0, i * (step // 2) + u0 // 2

    @block.sync
    def _(sp):
        sp.dma_start(XROW[:, 0:2, :], a["x_prompt"][0].rearrange("(n p) d -> p n d", p=P)).then_inc(x_rows_in.sem, 16)
        sp.dma_start(XROW[0:NS, 2, :], a["x_sample"].rearrange("b t d -> (b t) d")).then_inc(x_rows_in.sem, 16)
        with nc.allow_non_contiguous_dma("small parameter rows"):
            r = 0
            for name, n in (("norm_gain", 48), ("hg_norm_w", 8), ("ssm_norm_w", 8), ("conv_b", 12),
                            ("hg_lb_logits", 8)):
                src = a[name]
                if name == "norm_gain":
                    src = src.rearrange("l g d -> l (g d)")
                sp.dma_start(PROWA[r:r + n, :, :], src.rearrange("l (r p) -> r l p", p=P)).then_inc(params_in.sem, 16)
                r += n
            sp.dma_start(PROWB[:, :, :], a["conv_w"].rearrange("l j (c p) -> (j c) l p", p=P)).then_inc(params_in.sem, 16)
            for hh in range(2):
                for l in range(LAYERS):
                    src = a["d_skip"].rearrange("l (i h) -> h l i", h=2)[hh:hh + 1, l, :]
                    sp.dma_start(PALL[64 * hh:64 * hh + 64, l, C_DSK:C_DSK + PAIRS],
                                 src.broadcast_to([64, PAIRS])).then_inc(params_in.sem, 16)
            for name, c in (("dt_bias", C_DTB), ("a_log", C_A)):
                src = a[name].rearrange("(o l) h -> o l h", o=1)
                sp.dma_start(PALL[:, :, c:c + MH], src.broadcast_to([P, LAYERS, MH])).then_inc(params_in.sem, 16)

        def fetch_columns(l, w, u, c0):
            slot, n, _ = u
            sp.wait_ge(lo_ready.sem, lo_ready.after(l, n) + (1 - 2))
            src = w[ds(l, 1), :, ds(c0, 256)].rearrange("o (k p) c -> p (o k) c", p=P)
            sp.dma_start(RAW[:, slot, :].rearrange("p (k c) -> p k c", c=256), src).then_inc(raw_landed[slot].sem, 16)

        def fetch_rows(l, w, u, r0):
            slot, n, _ = u
            sp.wait_ge(lo_ready.sem, lo_ready.after(l, n) + (1 - 2))
            src = w[ds(l, 1), ds(r0, 256), :].rearrange("o (k p) c -> p (o k) c", p=P)
            sp.dma_start(RAW[:, slot, :].rearrange("p (k c) -> p k c", c=D), src).then_inc(raw_landed[slot].sem, 16)

        def ffn(l, up, down, g, u_, d):
            with sp.Fori(0, FT // 2) as j:
                fetch_columns(l, a[g], unit(up, j), j * 256)
                fetch_columns(l, a[u_], unit(up + 1, j), j * 256)
            with sp.Fori(0, 5) as j:
                fetch_rows(l, a[d], unit(down, j), j * 512)
                fetch_rows(l, a[d], unit(down + 1, j), j * 512 + 256)
            fetch_rows(l, a[d], unit(down + 10), 10 * 256)

        with sp.Fori(0, LAYERS) as l:
            ffn(l, U_UP1, U_DOWN1, "ffn1_w_gate", "ffn1_w_up", "ffn1_w_down")
            with sp.Fori(0, 2) as g:
                for c, c0 in enumerate((COL_F, COL_Q, COL_V, COL_GO)):
                    for s in range(2):
                        fetch_columns(l, a["w_in"], unit(U_IN + 2 * c + s, g, 8), g * 512 + (c0 + 256 * s))
            for first, n, c0 in ((U_IN + 16, 3, COL_X), (U_IN + 22, 2, COL_Z)):
                with sp.Fori(0, n) as i:
                    for s in range(2):
                        fetch_columns(l, a["w_in"], unit(first + s, i), i * 512 + (c0 + 256 * s))
            with sp.Fori(0, 4) as i:
                fetch_rows(l, a["w_out"], unit(U_OUT, i), i * 512)
                fetch_rows(l, a["w_out"], unit(U_OUT + 1, i), i * 512 + 256)
            ffn(l, U_UP2, U_DOWN2, "ffn2_w_gate", "ffn2_w_up", "ffn2_w_down")
        for n in range(3):
            sp.wait_ge(yout_ready.sem, n + 1)
            dst = (o["y_prompt"][0][n * P:(n + 1) * P, :] if n < 2 else o["y_sample"].rearrange("b t d -> (b t) d"))
            sp.dma_start(dst, YROW[0:TILES[n][1], n, :]).then_inc(y_stored.sem, 16)
        sp.wait_ge(y_stored.sem, 48)

    @block.gpsimd
    def _(pool):
        nc.gpsimd.iota(IT[:], pattern=[[1, P]], base=0, channel_multiplier=0).then_inc(iota_done.sem, 1)
        nc.gpsimd.iota(IS[:], pattern=[[0, P]], base=0, channel_multiplier=1).then_inc(iota_done.sem, 1)
        nc.gpsimd.iota(IBK[:], pattern=[[-SL, NB]], base=0, channel_multiplier=1).then_inc(iota_done.sem, 1)

        def blocked(src, n):
            return (src.rearrange("p (o v) -> p o v", o=1).broadcast_to([NS, NB, n]),
                    BLK[:].rearrange("p (b o) -> p b o", o=1).broadcast_to([NS, NB, n]))

        def hgrn(l, g):
            if g == 0:
                pool.wait_ge(unit_done.sem, unit_done.after(l, U_IN + 1))
                pool.wait_ge(ohl_ready.sem, ohl_ready.after(l, 0))
            else:
                pool.wait_ge(w_ready.sem, w_ready.after(l, 16))
            one = ONES[:, 0:1].rearrange("p (a b) -> p a b", a=1).broadcast_to([P, HG, T])
            nc.gpsimd.tensor_tensor(SUF[:], one, one, ALU.mult).then_inc(hgz_ready.sem, 1)

            nc.gpsimd.memset(APR[:], 0.0).then_inc(hgz_ready.sem, 1)
            nc.gpsimd.memset(ASM[:], 0.0).then_inc(hgz_ready.sem, 1)
            for h in range(HG):
                pool.wait_ge(vtok_ready.sem, vtok_ready.after(l, g * 3 + 2))
                if h:
                    pool.wait_ge(upd_ready.sem, upd_ready.after(l, g * 4 + h))
                if g == 1 and h == 0:
                    pool.wait_ge(ohl_ready.sem, ohl_ready.after(l, 1))
                nc.gpsimd.tensor_tensor(VM[:], *blocked(VTOK[0:NS, 2, h * KD:(h + 1) * KD], KD),
                                        ALU.mult).then_inc(vm_ready.sem, 1)
                if g == 1 and h == 0:
                    nc.gpsimd.memset(XB[:, :, 0:CW - 1], 0.0).then_inc(zeros_ready.sem, 1)
                pool.wait_ge(o_ready.sem, o_ready.after(l, g * 4 + h + 1))
                s = HSIN[g][h % 3]
                nc.gpsimd.tensor_tensor(
                    s[:], s[:],
                    PROJ[g][0][:, h, SEQ + SL - 1:T:SL].rearrange("p (b o) -> p b o", o=1).broadcast_to([P, NB, KD]),
                    ALU.mult).then_inc(decayed.sem, 1)

        def mamba(l):
            pool.wait_ge(xc_ready.sem, xc_ready.after(l, 6))
            nc.gpsimd.tensor_tensor(CS[:, :, 0:3], XB[:, :, SEQ:PADP],
                                    ONES[:, 0:1].rearrange("p (a b) -> p a b", a=1).broadcast_to([P, CT, 3]),
                                    ALU.mult).then_inc(cs_ready.sem, 1)
            nc.gpsimd.tensor_copy(
                CS[:, :, 3:27].rearrange("p c (b j) -> p c b j", j=3),
                XB[:, :, PADP:].rearrange("p c (b j) -> p c b j", j=PADS)[:, :, :, SL:]).then_inc(cs_ready.sem, 1)
            pool.wait_ge(rem_ready.sem, rem_ready.after(l, 2))
            pool.wait_ge(cs_ready.sem, cs_ready.after(l, 2))
            for j, n in enumerate(TURNS):
                tn = TILES[n][1]
                pool.wait_ge(dtx_ready.sem, dtx_ready.after(l, j + 1))
                nc.gpsimd.tensor_tensor(
                    WX[0:tn, n, :].rearrange("p (h d) -> p h d", d=HD),
                    DTX[0:tn, n, :].rearrange("p (h d) -> p h d", d=HD),
                    REM[0:tn, n, :].rearrange("p (h o) -> p h o", o=1).broadcast_to([tn, MH, HD]),
                    ALU.mult).then_inc(wx_ready.sem, 1)
            for g in range(2):
                pool.wait_ge(btok_ready.sem, btok_ready.after(l, 3))
                if g:
                    pool.wait_ge(supd_ready.sem, supd_ready.after(l, 4))
                nc.gpsimd.tensor_tensor(BMK[:], *blocked(BTOK[0:NS, 2, g * P:(g + 1) * P], P),
                                        ALU.mult).then_inc(bmk_ready.sem, 1)

        def ffn(l, f):
            def pair(j, par):
                pool.wait_ge(sg_ready.sem, sg_ready.after(l, j) + 1)
                nc.gpsimd.tensor_tensor(SR[:, par], SG[:, par],
                                        RINV[:].rearrange("p (o t) -> p o t", o=1).broadcast_to([P, 2, T]),
                                        ALU.mult).then_inc(sr_ready.sem, 1)

            with pool.Fori(0, 5) as i:
                for s in range(2):
                    pair(i * 2 + (11 * f + s), s)
            pair(11 * f + 10, 0)

        with pool.Fori(0, LAYERS) as l:
            ffn(l, 0)
            for g in range(2):
                hgrn(l, g)
            mamba(l)
            ffn(l, 1)

    @block.scalar
    def _(act):
        def copy(out, in_, scale=1.0):
            return nc.scalar.activation(out, in_, ACT.Copy, scale=scale)

        def split_hi(l, u):
            slot, n, k = u
            act.wait_ge(raw_landed[slot].sem, raw_landed[slot].after(l, k * 16 + 16))
            act.wait_ge(unit_done.sem, unit_done.after(l, n) + (1 - 2))
            copy(WH[:, slot, :], RAW[:, slot, :]).then_inc(hi_ready.sem, 1)

        def ahead(u):
            return u[0], u[1] + 2, u[2] + 1

        act.wait_ge(consts_done.sem, 1)
        for n, (t0, tn) in enumerate(TILES):
            act.wait_ge(x_turned.sem, n + 1)
            copy(X[:, :, t0:t0 + tn],
                 PS[:, 2 * n:2 * n + 2, :].rearrange("p b (k t) -> p (b k) t", t=P)[:, :, 0:tn]).then_inc(x_ready.sem, 1)
        act.wait_ge(lb_step.sem, 3)
        nc.scalar.activation(LBW[:, 3:5], LBW[:, 3:5], ACT.Exp).then_inc(lb_exp.sem, 1)
        nc.scalar.activation(PALL[:, :, C_A:C_A + MH], PALL[:, :, C_A:C_A + MH], ACT.Exp).then_inc(lb_exp.sem, 1)
        for s in (s2_stored, *hs_stored, *ms_stored, *sp_stored):
            copy(FREE[:], EPST[:]).then_inc(s.sem, 16)
            act.wait_ge(s.sem, 16)

        def high(l, i, c):
            act.wait_ge(xn_ready.sem, xn_ready.after(l, 8 * i + 2 * c + 2))
            copy(XH[:, 2 * c:2 * c + 2], XN[:, 2 * c:2 * c + 2]).then_inc(xh_ready.sem, 1)

        def pre_norm(l, i):
            for c in range(4):
                act.wait_ge(x_ready.sem, x_ready.after(l, 4 * i + c - 3 if i else 0))
                nc.scalar.activation(SQ[:, 2 * c:2 * c + 2], X[:, 2 * c:2 * c + 2], ACT.Square).then_inc(presq_ready.sem, 1)
                if i != 1:
                    high(l, i, c)
                if i == 0 and c == 1:
                    split_hi(l, unit(0))
            act.wait_ge(stat_ready.sem, stat_ready.after(l, 2 * i + 1))
            nc.scalar.activation(ROOT[:], PS[:, 0 if i == 1 else 7, 0:T], ACT.Sqrt, bias=EPST[:], scale=1.0 / D
                                 ).then_inc(root_ready.sem, 1)
            if i == 1:
                for c in range(4):
                    high(l, i, c)

        def post_norm(l, i, last_unit):
            act.wait_ge(unit_done.sem, unit_done.after(l, last_unit + 1))
            for c in range(4):
                copy(MS[:, 2 * c:2 * c + 2], PS[:, 2 * c:2 * c + 2, 0:T]).then_inc(ms_ready.sem, 1)
            if i < 2:
                split_hi(l, unit(last_unit + 2))
            act.wait_ge(stat_ready.sem, stat_ready.after(l, 2 * i + 2))
            nc.scalar.activation(ROOT[:], PS[:, 0, 0:T], ACT.Sqrt, bias=EPST[:], scale=1.0 / D).then_inc(root_ready.sem, 1)

        def ffn(l, f, up, down):
            def pair(j, par, gate, up_):
                act.wait_ge(unit_done.sem, unit_done.after(l, gate[1]) + 1)
                split_hi(l, ahead(gate))
                act.wait_ge(gr_ready.sem, gr_ready.after(l, j) + 1)
                nc.scalar.activation(SG[:, par], SG[:, par], ACT.Silu).then_inc(sg_ready.sem, 1)
                split_hi(l, ahead(up_))
                act.wait_ge(h_ready.sem, h_ready.after(l, j) + 1)
                copy(HH[:, ds(j * 2 - 22 * f, 2), :], HF[:, par]).then_inc(hh_ready.sem, 1)

            with act.Fori(0, 5) as i:
                for s in range(2):
                    pair(i * 2 + (11 * f + s), s, unit(up + 2 * s, i, 4), unit(up + 2 * s + 1, i, 4))
            act.wait_ge(unit_done.sem, unit_done.after(l, up + 20) + 1)
            split_hi(l, unit(up + 22))
            act.wait_ge(gr_ready.sem, gr_ready.after(l, 11 * f + 11))
            nc.scalar.activation(SG[:, 0], SG[:, 0], ACT.Silu).then_inc(sg_ready.sem, 1)
            split_hi(l, unit(up + 23))
            act.wait_ge(h_ready.sem, h_ready.after(l, 11 * f + 11))
            copy(HH[:, 20:22, :], HF[:, 0]).then_inc(hh_ready.sem, 1)
            with act.Fori(0, 4) as i:
                split_hi(l, unit(down + 2, i))
                split_hi(l, unit(down + 3, i))
            split_hi(l, unit(down + 10))
            if f == 0:
                split_hi(l, unit(down + 11))

        def hgrn_state_in(l, g, h):
            s = h % 3
            act.wait_ge(hs_stored[s].sem, hs_stored[s].after(l, 16 * (g * SLOT_HEADS[s] + h // 3)))
            act.dma_start(HSIN[g][s][:],
                          a["state_hgrn"][ds(l, 1), :, ds(g * 4 + h, 1)].rearrange("o b h k v -> k (o b h) v")
                          ).then_inc(hs_in[s].sem, 16)

        def projected(l, g, c):
            u = unit(U_IN + 8 * g + c)
            act.wait_ge(unit_done.sem, unit_done.after(l, u[1]) + 1)
            split_hi(l, ahead(u))
            b = 6 if g else 2 * (c % 4)
            ps = PS[:, b:b + 2, 0:T]
            h = slice(2 * (c % 2), 2 * (c % 2) + 2)
            pre, kf, qf, vf, go = PROJ[g]
            if c < 2:
                nc.scalar.activation(pre[:, h], ps, ACT.Sigmoid).then_inc(fsig_ready.sem, 1)
                nc.scalar.activation(kf[:, h], ps, ACT.Sigmoid, scale=-1.0).then_inc(fsig_ready.sem, 1)
            elif c < 4:
                copy(qf[:, h], ps, QSCALE).then_inc(q_ready.sem, 1)
            elif c < 6:
                copy(vf[:, h], ps).then_inc(v_ready.sem, 1)
            else:
                nc.scalar.activation(go[:, h], ps, ACT.Silu).then_inc(go_ready.sem, 1)

        def conv_input(l, j):
            u = unit(U_IN + 16 + j)
            act.wait_ge(unit_done.sem, unit_done.after(l, u[1]) + 1)
            split_hi(l, ahead(u))
            if j == 0:
                act.wait_ge(ohl_ready.sem, ohl_ready.after(l, 1))
            copy(XB[:, 2 * j:2 * j + 2, CW - 1:PADP], PS[:, 6:8, 0:SEQ]).then_inc(xb_ready.sem, 1)
            copy(XB[:, 2 * j:2 * j + 2, PADP:].rearrange("p c (b j) -> p c b j", j=PADS)[:, :, :, CW - 1:],
                 PS[:, 6:8, SEQ:T].rearrange("p c (b j) -> p c b j", j=SL)).then_inc(xb_ready.sem, 1)

        def values(l, g):
            for j, n in enumerate(TURNS):
                tn = TILES[n][1]
                act.wait_ge(vturn_ready.sem, vturn_ready.after(l, g * 3 + j + 1))
                copy(VTOK[0:tn, n, :], PS[0:tn, 4 + j % 2, :]).then_inc(vtok_ready.sem, 1)

        def newest_tap(l, q):
            if q == 0:
                act.wait_ge(pads_ready.sem, pads_ready.after(l, 3))
                act.wait_ge(zeros_ready.sem, zeros_ready.after(l, 1))
            act.wait_ge(xb_ready.sem, xb_ready.after(l, 4 * q + 4))
            for c in range(4):
                k = 4 * q + c
                nc.scalar.activation(ACC[:, q % 2, c, 0:CVW], XB[:, k, CW - 1:XBW], ACT.Identity, bias=col(C_CB + k),
                                     scale=col(C_CW + 3 * CT + k)).then_inc(acc_ready.sem, 1)

        def conv_silu(l, q):
            act.wait_ge(tap_ready.sem, tap_ready.after(l, 12 * q + 12))
            nc.scalar.activation(XC[:, 4 * q:4 * q + 4, 0:SEQ], ACC[:, q % 2, :, 0:SEQ], ACT.Silu).then_inc(xc_ready.sem, 1)
            nc.scalar.activation(
                XC[:, 4 * q:4 * q + 4, SEQ:].rearrange("p c (b j) -> p c b j", j=SL),
                ACC[:, q % 2, :, PADP:].rearrange("p c (b j) -> p c b j", j=PADS)[:, :, :, 0:SL], ACT.Silu).then_inc(xc_ready.sem, 1)

        def gate(l, j):
            u = unit(U_IN + 22 + j)
            act.wait_ge(unit_done.sem, unit_done.after(l, u[1]) + 1)
            split_hi(l, ahead(u))
            b = 6 - 2 * (j % 2)
            nc.scalar.activation(Z[:, 2 * j:2 * j + 2, :], PS[:, b:b + 2, 0:T], ACT.Silu).then_inc(z_ready.sem, 1)

        def hgrn(l, g):
            def beside(place):
                for j in BESIDE[g][place]:
                    projected(l, 1, j) if g == 0 else conv_input(l, j)

            hgrn_state_in(l, g, 0)
            hgrn_state_in(l, g, 1)
            if g == 0:
                hgrn_state_in(l, 0, 2)
                values(l, 0)
            for i in range(1, 8):
                beside(i)
            if g == 1:
                act.wait_ge(cturn_ready.sem, cturn_ready.after(l, 1))
                for c in range(3):
                    copy(XB[:, c::3, PADP:].rearrange("p q (b j) -> p q b j", j=PADS)[:, :, :, 0:CW - 1],
                         PS[:, 5, c * 96:(c + 1) * 96].rearrange("p (b j q) -> p q b j", b=NB, q=4)).then_inc(pads_ready.sem, 1)
            for j, n in enumerate(TURNS):
                tn = TILES[n][1]
                act.wait_ge(kturn_ready.sem, kturn_ready.after(l, g * 3 + j + 1))
                copy(KTOK[0:tn, n, :], PS[0:tn, j % 2, :]).then_inc(ktok_ready.sem, 1)
            if g == 1:
                hgrn_state_in(l, 1, 2)
            act.wait_ge(sp1_ready.sem, sp1_ready.after(l, g + 1))
            copy(S1[:], PS[:, 4, :].rearrange("p (h v) -> p h v", v=KD)).then_inc(s1_ready.sem, 1)
            act.wait_ge(s2_ready.sem, s2_ready.after(l, g + 1))
            act.dma_start(o["hgrn_prompt"][ds(l, 1), 0, ds(g * 4, 4)].rearrange("o h k v -> k (o h) v"),
                          S2[:]).then_inc(s2_stored.sem, 16)
            for h in range(HG):
                act.wait_ge(o_ready.sem, o_ready.after(l, g * 4 + h + 1))
                nc.scalar.activation(SQO[:, h], PS[:, h, 0:T], ACT.Square).then_inc(sqo_ready.sem, 1)
                beside(8 + h)
                if g == 1 and h == 0:
                    newest_tap(l, 0)
                act.wait_ge(snew_ready.sem, snew_ready.after(l, g * 4 + h + 1))
                act.dma_start(o["hgrn_sample"][ds(l, 1), :, ds(g * 4 + h, 1)].rearrange("o b h k v -> k (o b h) v"),
                              HSIN[g][h % 3][:]).then_inc(hs_stored[h % 3].sem, 16)
                if h == 0:
                    hgrn_state_in(l, g, 3)
            act.wait_ge(ostat_ready.sem, ostat_ready.after(l, g + 1))
            nc.scalar.activation(RTO[:], PS[:, 4, 0:T], ACT.Sqrt, bias=EPST[:], scale=1.0 / KD).then_inc(oroot_ready.sem, 1)
            if g == 0:
                beside(12)
                values(l, 1)
            else:
                gate(l, 0)
            act.wait_ge(ohg_ready.sem, ohg_ready.after(l, g * 4 + 4))
            if g == 1:
                act.wait_ge(hs_stored[2].sem, hs_stored[2].after(l, 16))
            copy(HH[:, 4 * g:4 * g + 4, :], SQO[:]).then_inc(ohh_ready.sem, 1)

        def softplus(l):
            for f in range(2):
                for r, n in ROWS:
                    if f == 0:
                        act.wait_ge(dt_step.sem, dt_step.after(l, 4))
                        nc.scalar.activation(DTW[r, 2, n], DTW[r, 1, n], ACT.Exp).then_inc(dt_exp.sem, 1)
                    else:
                        act.wait_ge(dt_exp.sem, dt_exp.after(l, 2))
                        nc.scalar.activation(DTW[r, 3, n], DTW[r, 2, n], ACT.Ln, bias=1.0).then_inc(dt_exp.sem, 1)

        def ssm_state_in(l, i):
            act.wait_ge(ms_stored[i % 3].sem, ms_stored[i % 3].after(l, i // 3 * 16))
            act.dma_start(SIN[i % 3][:],
                          a["state_ssm"][ds(l, 1), :, 2 * i:2 * i + 2].rearrange("o b h p n -> (h p) (o b) n")
                          ).then_inc(ms_in[i % 3].sem, 16)

        def mamba(l):
            for s in hs_stored:
                act.wait_ge(s.sem, s.after(l, s.per_layer))
            ssm_state_in(l, 0)
            ssm_state_in(l, 1)
            act.wait_ge(ohl_ready.sem, ohl_ready.after(l, 2))
            gate(l, 1)
            newest_tap(l, 1)
            conv_silu(l, 0)
            gate(l, 2)
            act.wait_ge(xc_ready.sem, xc_ready.after(l, 2))
            newest_tap(l, 2)
            conv_silu(l, 1)
            gate(l, 3)
            act.wait_ge(remp_ready.sem, remp_ready.after(l, 1))
            for k, (r, n) in enumerate(ROWS):
                nc.scalar.activation(REM[r, n], PS[r, 1, 0:48].rearrange("p (n h) -> p n h", h=MH)[:, n], ACT.Exp).then_inc(rem_ready.sem, 1)

            def decays(i):
                act.wait_ge(seg_ready.sem, seg_ready.after(l, i + 1))
                if i:
                    act.wait_ge(y_ready.sem, y_ready.after(l, i))
                nc.scalar.activation(ST[:].rearrange("p n h t -> p (n h t)"), PS[:, 4, :], ACT.Exp).then_inc(e_ready.sem, 1)
                nc.scalar.activation(STS[:].rearrange("p h t -> p (h t)"), PS[0:NS, 5, 0:P], ACT.Exp).then_inc(e_ready.sem, 1)
                nc.scalar.activation(EC[:, i % 2], PS[:, 5, P:P + T], ACT.Exp).then_inc(e_ready.sem, 1)

            decays(0)
            conv_silu(l, 2)
            for j, n in enumerate(TURNS):
                tn = TILES[n][1]
                act.wait_ge(xturn_ready.sem, xturn_ready.after(l, j + 1))
                copy(BTOK[0:tn, n, :], PS[0:tn, 5 if j == 1 else 2, 0:2 * P]).then_inc(btok_ready.sem, 1)
            act.wait_ge(ht1p_ready.sem, ht1p_ready.after(l, 1))
            copy(HT1[:].rearrange("p (g c) -> p g c", g=2), PS[:, 0:2, :]).then_inc(ht1_ready.sem, 1)
            act.wait_ge(csturn_ready.sem, csturn_ready.after(l, 1))
            copy(CO[:].rearrange("p (b c) -> p b c", b=3), PS[0:27, 5:8, :]).then_inc(co_ready.sem, 1)
            act.wait_ge(co_ready.sem, co_ready.after(l, 1))
            act.dma_start(o["conv_prompt"][ds(l, 1), 0].rearrange("o j c -> (o j) c"), CO[0:3, :]).then_inc(co_stored.sem, 16)
            act.dma_start(o["conv_sample"][ds(l, 1)].rearrange("o b j c -> (o b j) c"), CO[3:27, :]).then_inc(co_stored.sem, 16)
            ssm_state_in(l, 2)

            def states_out(i):
                act.wait_ge(spn_ready.sem, spn_ready.after(l, i + 1))
                act.dma_start(o["ssm_prompt"][ds(l, 1), 0, 2 * i:2 * i + 2].rearrange("o h p n -> (o h p) n"),
                              SP[:, i % 2, :]).then_inc(sp_stored[i % 2].sem, 16)
                act.wait_ge(ssm_new.sem, ssm_new.after(l, i + 1))
                act.dma_start(o["ssm_sample"][ds(l, 1), :, 2 * i:2 * i + 2].rearrange("o b h p n -> (h p) (o b) n"),
                              SIN[i % 3][:]).then_inc(ms_stored[i % 3].sem, 16)

            for i in range(PAIRS):
                act.wait_ge(hts_turned.sem, hts_turned.after(l, i + 1))
                if i:
                    act.wait_ge(y2_ready.sem, y2_ready.after(l, i))
                copy(HTS[:].rearrange("p (c b) n -> p c (b n)", c=2), PS[:, 6:8, :]).then_inc(hts_ready.sem, 1)
                if i:
                    states_out(i - 1)
                if i + 1 < PAIRS:
                    decays(i + 1)
                if i and i + 2 < PAIRS:
                    ssm_state_in(l, i + 2)
            states_out(PAIRS - 1)
            for g in range(2):
                act.wait_ge(yz_ready.sem, yz_ready.after(l, g + 1))
                nc.scalar.activation(SQS[:, 4 * g:4 * g + 4], Z[:, 4 * g:4 * g + 4], ACT.Square).then_inc(sqs_ready.sem, 1)
            split_hi(l, unit(U_OUT + 2))
            split_hi(l, unit(U_OUT + 3))
            act.wait_ge(sstat_ready.sem, sstat_ready.after(l, 1))
            for b, t, n in SPARE:
                nc.scalar.activation(SQS[:, 0:2, t:t + n], PS[:, b:8:4, T:T + n], ACT.Sqrt, bias=EPST[:], scale=2.0 / D
                                     ).then_inc(sroot_ready.sem, 1)
            act.wait_ge(co_stored.sem, co_stored.after(l, 32))
            for c in range(4):
                act.wait_ge(ysn_ready.sem, ysn_ready.after(l, 2 * c + 2))
                copy(HH[:, 8 + 2 * c:10 + 2 * c, :], Z[:, 2 * c:2 * c + 2]).then_inc(yh_ready.sem, 1)
            for s in ms_stored + sp_stored:
                act.wait_ge(s.sem, s.after(l, s.per_layer))
            act.wait_ge(s2_stored.sem, s2_stored.after(l, 32))
            with act.Fori(0, 2) as i:
                split_hi(l, unit(U_OUT + 4, i))
                split_hi(l, unit(U_OUT + 5, i))
            split_hi(l, unit(U_OUT + 8))

        with act.Fori(0, LAYERS) as l:
            act.dma_start(WDT[:], a["w_in"][ds(l, 1), :, COL_DT:COL_DT + MH].rearrange("o (k p) h -> p (o k) h", p=P)
                          ).then_inc(wdt_in.sem, 16)
            pre_norm(l, 0)
            split_hi(l, unit(1))
            ffn(l, 0, U_UP1, U_DOWN1)
            post_norm(l, 0, U_DOWN1 + 10)
            act.dma_start(CROW[:], a["state_conv"][ds(l, 1)].rearrange("o b j (q c) -> (o b j q) c", q=4)).then_inc(crow_in.sem, 16)
            pre_norm(l, 1)
            for c in range(8):
                if c == 0:
                    act.wait_ge(dtp_ready.sem, dtp_ready.after(l, 1))
                projected(l, 0, c)
                if c == 1:
                    softplus(l)
            for g in range(2):
                hgrn(l, g)
            mamba(l)
            post_norm(l, 1, U_OUT + 7)
            pre_norm(l, 2)
            ffn(l, 1, U_UP2, U_DOWN2)
            post_norm(l, 2, U_DOWN2 + 10)
        for n, (t0, tn) in enumerate(TILES):
            act.wait_ge(yout_turned.sem, n + 1)
            copy(YROW[0:tn, n, :].rearrange("p (b c) -> p b c", b=2), PS[0:tn, 2 * n:2 * n + 2, :]).then_inc(yout_ready.sem, 1)

    @block.vector
    def _(dve):
        V = nc.vector

        def split_lo(l, u):
            slot, n, _ = u
            dve.wait_ge(hi_ready.sem, hi_ready.after(l, n) + 1)
            V.tensor_tensor(WL[:, slot, :], RAW[:, slot, :], WH[:, slot, :].bitcast(F32), ALU.subtract).then_inc(lo_ready.sem, 1)

        def ahead(u):
            return u[0], u[1] + 2, u[2] + 1

        for s in (lo_ready, h_ready):
            for n in range(2):
                V.memset(FREEV[:], 0.0).then_inc(s.sem, 1)
                dve.wait_ge(s.sem, n + 1)
        V.memset(FREEV[:], 0.0).then_inc(ohg_ready.sem, 1)
        dve.wait_ge(ohg_ready.sem, 1)
        V.memset(FREEV[:], 0.0).then_inc(ohl_ready.sem, 1)
        V.memset(ONES[:], 1.0).then_inc(const_step.sem, 1)
        V.memset(EPST[:], EPS).then_inc(const_step.sem, 1)
        dve.wait_ge(iota_done.sem, 3)
        V.tensor_tensor(IX[:], IT[:], IS[:], ALU.bitwise_xor).then_inc(const_step.sem, 1)
        V.tensor_tensor(FIT[:], IT[:], IS[:], ALU.subtract).then_inc(const_step.sem, 1)
        dve.wait_ge(const_step.sem, 4)
        V.tensor_copy(FIX[:], IX[:]).then_inc(const_step.sem, 1)
        V.tensor_scalar(IDENT[:], FIT[:], 0.0, None, ALU.is_equal).then_inc(const_step.sem, 1)
        V.tensor_scalar(TRI[:], FIT[:], 0.0, None, ALU.is_ge).then_inc(const_step.sem, 1)
        V.tensor_scalar(USTR[:], FIT[:], 0.0, None, ALU.is_lt).then_inc(const_step.sem, 1)
        dve.wait_ge(const_step.sem, 8)
        V.scalar_tensor_tensor(TRI8[:], FIX[0:NS, 0:NS], 8.0, TRI[0:NS, 0:NS], ALU.is_lt, ALU.mult).then_inc(const_step.sem, 1)
        V.scalar_tensor_tensor(USTR8[:], FIX[0:NS, 0:NS], 8.0, USTR[0:NS, 0:NS], ALU.is_lt, ALU.mult).then_inc(const_step.sem, 1)
        V.tensor_tensor(FIT[:], FIX[:], TRI[:], ALU.mult).then_inc(const_step.sem, 1)
        dve.wait_ge(const_step.sem, 11)
        for i in range(8):
            V.tensor_scalar(FGE[:, i], FIT[:], float(1 << i), None, ALU.is_ge).then_inc(const_step.sem, 1)
        dve.wait_ge(const_step.sem, 19)
        V.tensor_copy(MASK[:, 0], IDENT[:]).then_inc(const_step.sem, 1)
        V.tensor_tensor(MASK[:, 1:8], FGE[:, 0:7], FGE[:, 1:8], ALU.subtract).then_inc(const_step.sem, 1)
        V.tensor_scalar(FB[:, 0], IBK[:], 0.0, None, ALU.is_ge).then_inc(const_step.sem, 1)
        V.tensor_scalar(FB[:, 1], IBK[:], float(SL), None, ALU.is_ge).then_inc(const_step.sem, 1)
        for h in range(HG):
            V.tensor_scalar(SEL[:, h], IS[:], 32.0 * h, None, ALU.is_equal).then_inc(const_step.sem, 1)
        dve.wait_ge(const_step.sem, 23 + HG)
        V.tensor_tensor(BLK[:], FB[:, 0], FB[:, 1], ALU.subtract).then_inc(consts_done.sem, 1)
        dve.wait_ge(params_in.sem, 16 * 12)
        dve.wait_ge(params_turned.sem, 1)
        pa = PS[:, 6, 0:2 * NROW_A].rearrange("p (l c) -> p l c", l=2)
        V.tensor_copy(PALL[:, :, 0:C_CW], pa[:, :, 0:C_CW]).then_inc(params_done.sem, 1)
        V.tensor_copy(LBW[:, 0:2], pa[:, :, C_CW:NROW_A]).then_inc(params_done.sem, 1)
        V.tensor_copy(PALL[:, :, C_CW:C_LBF], PS[:, 7, 0:96].rearrange("p (l c) -> p l c", l=2)).then_inc(params_done.sem, 1)
        dve.wait_ge(params_done.sem, 3)
        V.tensor_scalar(PALL[:, :, C_GAIN + 8:C_GAIN + 16], PALL[:, :, C_GAIN + 8:C_GAIN + 16], 0.5, None, ALU.mult).then_inc(params_done.sem, 1)
        V.tensor_scalar(PALL[:, :, C_GAIN + 40:C_GAIN + 48], PALL[:, :, C_GAIN + 40:C_GAIN + 48], 0.5, None, ALU.mult).then_inc(params_done.sem, 1)
        V.tensor_tensor(LBW[:, 2], LBW[:, 0], LBW[:, 1], ALU.max).then_inc(lb_step.sem, 1)
        dve.wait_ge(lb_step.sem, 1)
        V.tensor_tensor(LBW[:, 3], LBW[:, 0], LBW[:, 2], ALU.subtract).then_inc(lb_step.sem, 1)
        V.tensor_tensor(LBW[:, 4], LBW[:, 1], LBW[:, 2], ALU.subtract).then_inc(lb_step.sem, 1)
        dve.wait_ge(lb_exp.sem, 2)
        V.tensor_tensor(LBW[:, 5], LBW[:, 3], LBW[:, 4], ALU.add).then_inc(lb_step.sem, 1)
        dve.wait_ge(lb_step.sem, 4)
        V.reciprocal(LBW[:, 6], LBW[:, 5]).then_inc(lb_step.sem, 1)
        dve.wait_ge(lb_step.sem, 5)
        V.tensor_tensor(LBW[:, 3], LBW[:, 3], LBW[:, 6], ALU.mult).then_inc(lb_step.sem, 1)
        V.tensor_tensor(LBW[:, 4], LBW[:, 4], LBW[:, 6], ALU.mult).then_inc(lb_step.sem, 1)
        dve.wait_ge(lb_step.sem, 7)
        V.tensor_tensor(LBW[:, 5], LBW[:, 3], LBW[:, 4], ALU.add).then_inc(lb_step.sem, 1)
        V.tensor_tensor(LBW[:, 0], LBW[:, 3], LBW[:, 3], ALU.subtract).then_inc(lb_step.sem, 1)
        dve.wait_ge(lb_step.sem, 9)
        V.tensor_tensor(LBW[:, 1], LBW[:, 5], LBW[:, 3], ALU.subtract).then_inc(lb_step.sem, 1)
        dve.wait_ge(lb_step.sem, 10)
        V.tensor_scalar(PALL[:, :, C_LBF:C_LBF + 8], LBW[:, 0:2], LB_FLOOR, None, ALU.max).then_inc(lb_step.sem, 1)
        V.tensor_scalar(PALL[:, :, C_OML:C_OML + 8], LBW[:, 0:2], -1.0, 1.0, ALU.mult, ALU.add).then_inc(lb_step.sem, 1)
        V.tensor_scalar(PALL[:, :, C_A:C_A + MH], PALL[:, :, C_A:C_A + MH], -1.0, None, ALU.mult).then_inc(lb_step.sem, 1)
        dve.wait_ge(lb_step.sem, 13)
        dve.wait_ge(params_done.sem, 5)

        def low(l, i, c):
            dve.wait_ge(xh_ready.sem, xh_ready.after(l, 4 * i + c + 1))
            V.tensor_tensor(XL[:, 2 * c:2 * c + 2], XN[:, 2 * c:2 * c + 2], XH[:, 2 * c:2 * c + 2].bitcast(F32),
                            ALU.subtract).then_inc(xl_ready.sem, 1)

        def pre_norm(l):
            dve.wait_ge(root_ready.sem, root_ready.after(l, 3))
            V.reciprocal(RINV[:], ROOT[:]).then_inc(rinv_ready.sem, 1)
            dve.wait_ge(rinv_ready.sem, rinv_ready.after(l, 3))
            for k in range(DT_):
                V.scalar_tensor_tensor(XN[:, k], X[:, k], gain(2, k), RINV[:], ALU.mult, ALU.mult).then_inc(xn_ready.sem, 1)
                if k > 2 and k % 2:
                    low(l, 1, k // 2 - 1)
            low(l, 1, 3)

        def pre_gain(l, i, c):
            dve.wait_ge(x_ready.sem, x_ready.after(l, 4 * i + c - 3 if i else 0))
            for k in (2 * c, 2 * c + 1):
                V.tensor_scalar(XN[:, k], X[:, k], gain(2 * i, k), None, ALU.mult).then_inc(xn_ready.sem, 1)
            if c:
                low(l, i, c - 1)

        def pre_rinv(l, i):
            low(l, i, 3)
            if i == 0:
                split_lo(l, unit(0))
            dve.wait_ge(root_ready.sem, root_ready.after(l, 2 * i + 1))
            V.reciprocal(RINV[:], ROOT[:]).then_inc(rinv_ready.sem, 1)

        def post_norm(l, i, last_unit, then=None):
            for c in range(4):
                dve.wait_ge(ms_ready.sem, ms_ready.after(l, 4 * i + c + 1))
                V.tensor_tensor(SQ[:, 2 * c:2 * c + 2], MS[:, 2 * c:2 * c + 2], MS[:, 2 * c:2 * c + 2], ALU.mult).then_inc(postsq_ready.sem, 1)
            if i < 2:
                split_lo(l, unit(last_unit + 2))
            dve.wait_ge(root_ready.sem, root_ready.after(l, 2 * i + 2))
            V.reciprocal(RINV[:], ROOT[:]).then_inc(rinv_ready.sem, 1)
            dve.wait_ge(rinv_ready.sem, rinv_ready.after(l, 2 * i + 2))
            def add(c):
                dve.wait_ge(scaled_ready.sem, scaled_ready.after(l, 8 * i + 2 * c + 2))
                V.tensor_tensor(X[:, 2 * c:2 * c + 2], X[:, 2 * c:2 * c + 2], MS[:, 2 * c:2 * c + 2], ALU.add).then_inc(x_ready.sem, 1)
                if then and c:
                    then(l, i + 1, c - 1)

            for k in range(DT_):
                V.scalar_tensor_tensor(MS[:, k], MS[:, k], gain(2 * i + 1, k), RINV[:], ALU.mult, ALU.mult).then_inc(scaled_ready.sem, 1)
                if k > 1 and k % 2 == 0:
                    add(k // 2 - 1)
            add(3)
            if then:
                then(l, i + 1, 3)

        def ffn(l, f, up, down):
            def pair(j, par, hl, gate, up_):
                dve.wait_ge(rinv_ready.sem, rinv_ready.after(l, 4 * f + 1))
                dve.wait_ge(unit_done.sem, unit_done.after(l, gate[1]) + 1)
                dve.wait_ge(h_ready.sem, h_ready.after(l, j) + (1 - 2))
                V.tensor_tensor(SG[:, par], PS[:, 4 * par:4 * par + 2, 0:T],
                                RINV[:].rearrange("p (o t) -> p o t", o=1).broadcast_to([P, 2, T]), ALU.mult).then_inc(gr_ready.sem, 1)
                split_lo(l, ahead(gate))
                dve.wait_ge(sr_ready.sem, sr_ready.after(l, j) + 1)
                dve.wait_ge(unit_done.sem, unit_done.after(l, up_[1]) + 1)
                V.tensor_tensor(HF[:, par], SR[:, par], PS[:, 4 * par + 2:4 * par + 4, 0:T], ALU.mult).then_inc(h_ready.sem, 1)
                split_lo(l, ahead(up_))
                dve.wait_ge(hh_ready.sem, hh_ready.after(l, j) + 1)
                V.tensor_tensor(HL[:, hl, :], HF[:, par], HH[:, hl, :].bitcast(F32), ALU.subtract).then_inc(hl_ready.sem, 1)

            with dve.Fori(0, 5) as i:
                for s in range(2):
                    pair(i * 2 + (11 * f + s), s, ds(i * 4 + 2 * s, 2), unit(up + 2 * s, i, 4), unit(up + 2 * s + 1, i, 4))
            pair(11 * f + 10, 0, slice(20, 22), unit(up + 20), unit(up + 21))
            with dve.Fori(0, 4) as i:
                split_lo(l, unit(down + 2, i))
                split_lo(l, unit(down + 3, i))
            split_lo(l, unit(down + 10))
            if f == 0:
                split_lo(l, unit(down + 11))

        def halves(buf, m):
            if m <= 4:
                v = buf.rearrange("p h t -> p (h t)").rearrange("p (n two m) -> p n two m", two=2, m=m)
                return v[:, :, 0, :], v[:, :, 1, :]
            v = buf[:, :, 0:SEQ].rearrange("p h (n two m) -> p h n two m", two=2, m=m)
            return v[:, :, :, 0, :], v[:, :, :, 1, :]

        def last(half, m):
            return (half[:, :, m - 1:m] if len(half.shape) == 3 else half[:, :, :, m - 1:m]).broadcast_to(list(half.shape))

        def pick(l, g, i):
            b = 3 * (i % 2)
            for n in range(2):
                q = V.copy_predicated(APR[:, n], MASK[:, i:i + 1, :].broadcast_to([P, HG, P]),
                                      PS[:, b + n, :].rearrange("p (h t) -> p h t", t=P))
            if i < 4:
                q = V.copy_predicated(ASM[:], MASK[0:NS, i:i + 1, 0:NS].broadcast_to([NS, HG, NS]),
                                      PS[0:NS, b + 2, 0:HG * NS].rearrange("p (h t) -> p h t", t=NS))
            q.then_inc(picked.sem, 1)

        def decays(l, g):
            pre, kf = PROJ[g][0:2]
            dve.wait_ge(fsig_ready.sem, fsig_ready.after(l, g * 4 + 4))
            for h in range(HG):
                w = [col(g * 4 + (b + h)) for b in (C_OML, C_LBF)]
                V.tensor_scalar(pre[:, h], pre[:, h], w[0], w[1], ALU.mult, ALU.add).then_inc(fk_ready.sem, 1)
                V.tensor_scalar(kf[:, h], kf[:, h], w[0], None, ALU.mult).then_inc(fk_ready.sem, 1)

        def older_tap(l, q, j):
            for c in range(4):
                k = 4 * q + c
                if j == 0:
                    dve.wait_ge(acc_ready.sem, acc_ready.after(l, k + 1))
                else:
                    dve.wait_ge(tap_ready.sem, tap_ready.after(l, 12 * q + 4 * (j - 1) + c + 1))
                acc = ACC[:, q % 2, c, 0:CVW]
                V.scalar_tensor_tensor(acc, XB[:, k, j:j + CVW], col(C_CW + CT * j + k), acc, ALU.mult, ALU.add).then_inc(tap_ready.sem, 1)

        def hgrn(l, g):
            PRE, KF, QF, _, GO = PROJ[g]

            def beside(place):
                for j in BESIDE[g][place]:
                    split_lo(l, ahead(unit(U_IN + 8 + 8 * g + j)))

            dve.wait_ge(hgz_ready.sem, hgz_ready.after(l, g * 3 + 3))
            dve.wait_ge(fk_ready.sem, fk_ready.after(l, g * 8 + 8))
            dve.wait_ge(q_ready.sem, q_ready.after(l, g * 2 + 2))
            for i, m in enumerate(LEVELS, 1):
                w1, w2 = halves(W[:, i % 2], m)
                k1, _ = halves(KF[:], m)
                _, q2 = halves(QF[:], m)
                s1, _ = halves(SUF[:], m)
                p1, p2 = halves(PRE[:], m)
                if i > 1:
                    dve.wait_ge(tree_ready.sem, tree_ready.after(l, g * 14 + 2 * (i - 1)))
                V.tensor_tensor(w1, k1, s1, ALU.mult).then_inc(w_ready.sem, 1)
                V.tensor_tensor(w2, q2, p2, ALU.mult).then_inc(w_ready.sem, 1)
                if i > 2:
                    beside(i - 2)
                V.tensor_tensor(s1, s1, last(p2, m), ALU.mult).then_inc(tree_ready.sem, 1)
                dve.wait_ge(tree_ready.sem, tree_ready.after(l, g * 14 + 2 * i - 1))
                dve.wait_ge(score_ready.sem, score_ready.after(l, g * 8 + i))
                V.tensor_tensor(p2, p2, last(p1, m), ALU.mult).then_inc(tree_ready.sem, 1)
                pick(l, g, i - 1)
            dve.wait_ge(tree_ready.sem, tree_ready.after(l, g * 14 + 14))
            V.tensor_tensor(W[:, 0], QF[:], PRE[:], ALU.mult).then_inc(w_ready.sem, 1)
            beside(6)
            dve.wait_ge(picked.sem, picked.after(l, g * 8 + 7))
            dve.wait_ge(score_ready.sem, score_ready.after(l, g * 8 + 8))
            V.tensor_tensor(W[:, 1], KF[:], SUF[:], ALU.mult).then_inc(w_ready.sem, 1)
            pick(l, g, 7)
            beside(7)
            dve.wait_ge(sp2_ready.sem, sp2_ready.after(l, g + 1))
            dve.wait_ge(s1_ready.sem, s1_ready.after(l, g + 1))
            dve.wait_ge(s2_stored.sem, s2_stored.after(l, g * 16))
            for h in range(HG):
                q = V.scalar_tensor_tensor(S2[:, h], S1[:, h], PRE[:, h, SEQ - 1:SEQ], PS[:, 5, h * KD:(h + 1) * KD], ALU.mult, ALU.add)
            q.then_inc(s2_ready.sem, 1)
            for h in range(HG):
                dve.wait_ge(decayed.sem, decayed.after(l, g * 4 + h + 1))
                dve.wait_ge(upd_ready.sem, upd_ready.after(l, g * 4 + h + 1))
                s = HSIN[g][h % 3][:].rearrange("p (c b) v -> p c (b v)", c=2)
                V.tensor_tensor(s, s, PS[:, 4:6, :], ALU.add).then_inc(snew_ready.sem, 1)
                beside(8 + h)
                if g == 1 and h < 3:
                    older_tap(l, 0, h)
            if g == 0:
                decays(l, 1)
            dve.wait_ge(oroot_ready.sem, oroot_ready.after(l, g + 1))
            V.reciprocal(RTO[:], RTO[:]).then_inc(orinv_ready.sem, 1)
            dve.wait_ge(go_ready.sem, go_ready.after(l, g * 2 + 2))
            for j in range(2):
                dve.wait_ge(obc_ready.sem, obc_ready.after(l, g * 2 + j + 1))
                h = slice(2 * j, 2 * j + 2)
                V.tensor_tensor(GO[:, h], GO[:, h], PS[:, 4:6, 0:T], ALU.mult).then_inc(gor_ready.sem, 1)
            dve.wait_ge(gor_ready.sem, gor_ready.after(l, g * 2 + 2))
            for h in range(HG):
                V.scalar_tensor_tensor(SQO[:, h], PS[:, h, 0:T], col(C_HGN + 4 * g + h), GO[:, h],
                                       ALU.mult, ALU.mult).then_inc(ohg_ready.sem, 1)
            if g == 0:
                beside(12)
            else:
                split_lo(l, ahead(unit(U_IN + 22)))
            dve.wait_ge(ohh_ready.sem, ohh_ready.after(l, g + 1))
            c = slice(4 * g, 4 * g + 4)
            V.tensor_tensor(HL[:, c, :], SQO[:], HH[:, c, :].bitcast(F32), ALU.subtract).then_inc(ohl_ready.sem, 1)


        def dt_first(l):
            dve.wait_ge(dtp_ready.sem, dtp_ready.after(l, 1))
            for r, n in ROWS:
                V.tensor_tensor(DTW[r, 0, n], PS[r, 7, 0:48].rearrange("p (n h) -> p n h", h=MH)[:, n],
                                PAR[r, C_DTB:C_DTB + MH].rearrange("p (o h) -> p o h", o=1).broadcast_to([r.stop, n.stop - n.start, MH]),
                                ALU.add).then_inc(dt_step.sem, 1)
            dve.wait_ge(dt_step.sem, dt_step.after(l, 2))
            for r, n in ROWS:
                V.scalar_tensor_tensor(DTW[r, 1, n], DTW[r, 0, n], -1.0, DTW[r, 0, n], ALU.mult, ALU.min).then_inc(dt_step.sem, 1)

        def dt_rest(l):
            def step(k, f):
                dve.wait_ge(dt_step.sem, dt_step.after(l, 2 * k))
                for r, n in ROWS:
                    f(r, n).then_inc(dt_step.sem, 1)
            dve.wait_ge(dt_exp.sem, dt_exp.after(l, 4))
            step(2, lambda r, n: V.tensor_scalar(DTW[r, 1, n], DTW[r, 2, n], 1.0, -1.0, ALU.add, ALU.add))
            step(3, lambda r, n: V.tensor_scalar(DTW[r, 4, n], DTW[r, 1, n], 1e-30, None, ALU.max))
            step(4, lambda r, n: V.reciprocal(DTW[r, 4, n], DTW[r, 4, n]))
            step(5, lambda r, n: V.tensor_tensor(DTW[r, 3, n], DTW[r, 3, n], DTW[r, 4, n], ALU.mult))
            step(6, lambda r, n: V.scalar_tensor_tensor(DTW[r, 3, n], DTW[r, 1, n], 0.0, DTW[r, 3, n], ALU.is_equal, ALU.add))
            step(7, lambda r, n: V.tensor_tensor(DTW[r, 3, n], DTW[r, 3, n], DTW[r, 2, n], ALU.mult))
            step(8, lambda r, n: V.scalar_tensor_tensor(DTT[r, n], DTW[r, 0, n], 0.0, DTW[r, 3, n], ALU.max, ALU.add))
            step(9, lambda r, n: V.tensor_tensor(
                AT[r, n], DTT[r, n],
                PAR[r, C_A:C_A + MH].rearrange("p (o h) -> p o h", o=1).broadcast_to([r.stop, n.stop - n.start, MH]), ALU.mult))

        def masked_a(l, i):
            if i:
                dve.wait_ge(seg_ready.sem, seg_ready.after(l, i))
            V.tensor_tensor(L1[:], USTR[:].rearrange("p (n h s) -> p n h s", n=1, h=1).broadcast_to([P, 2, 2, P]),
                            AT[:, 0:2, 2 * i:2 * i + 2].rearrange("p n (h o) -> p n h o", o=1).broadcast_to([P, 2, 2, P]),
                            ALU.mult).then_inc(l1_ready.sem, 1)
            V.tensor_tensor(L1S[:], USTR8[:].rearrange("p (h s) -> p h s", h=1).broadcast_to([NS, 2, NS]),
                            AT[0:NS, 2, 2 * i:2 * i + 2].rearrange("p (h o) -> p h o", o=1).broadcast_to([NS, 2, NS]),
                            ALU.mult).then_inc(l1_ready.sem, 1)

        def mamba(l):
            split_lo(l, ahead(unit(U_IN + 23)))
            for q in (1, 2):
                for j in range(3):
                    older_tap(l, q, j)
                    if q == 2 and j == 0:
                        dve.wait_ge(unit_done.sem, unit_done.after(l, U_IN + 26))
                        dve.wait_ge(dt_step.sem, dt_step.after(l, 20))
                        masked_a(l, 0)
                split_lo(l, ahead(unit(U_IN + 23 + q)))
            for j, n in enumerate(TURNS):
                tn = TILES[n][1]
                dve.wait_ge(xturn_ready.sem, xturn_ready.after(l, j + 1))
                b = 3 if j == 1 else 0
                V.tensor_tensor(DTX[0:tn, n, :].rearrange("p (h d) -> p h d", d=HD),
                                PS[0:tn, b:b + 2, :].rearrange("p b (h d) -> p (b h) d", d=HD),
                                DTT[0:tn, n, :].rearrange("p (h o) -> p h o", o=1).broadcast_to([tn, MH, HD]),
                                ALU.mult).then_inc(dtx_ready.sem, 1)
                dve.wait_ge(g_ready.sem, g_ready.after(l, j + 1))
                tri = TRI if n < 2 else TRI8
                V.tensor_tensor(GM[0:tn, n, :, 0:tn], PS[0:tn, 6 + j % 2, 0:2 * P].rearrange("p (g t) -> p g t", g=2)[:, :, 0:tn],
                                tri[:].rearrange("p (o t) -> p o t", o=1).broadcast_to([tn, 2, tn]), ALU.mult).then_inc(gm_ready.sem, 1)
            dve.wait_ge(gm_ready.sem, gm_ready.after(l, 3))

            def weigh(i):
                g = i // 4
                dve.wait_ge(e_ready.sem, e_ready.after(l, 3 * i + 3))
                V.tensor_tensor(ST[:], ST[:], GM[:, 0:2, g:g + 1, :].broadcast_to([P, 2, 2, P]), ALU.mult).then_inc(st_ready.sem, 1)
                V.tensor_tensor(STS[:], STS[:], GM[0:NS, 2, g:g + 1, 0:NS].broadcast_to([NS, 2, NS]), ALU.mult).then_inc(st_ready.sem, 1)

            weigh(0)
            masked_a(l, 1)
            for i in range(PAIRS):
                dve.wait_ge(y_ready.sem, y_ready.after(l, i + 1))
                V.scalar_tensor_tensor(XC[:, i], XC[:, i], col(C_DSK + i), PS[:, 0, 0:T], ALU.mult, ALU.add).then_inc(ystep.sem, 1)
                dve.wait_ge(sp_stored[i % 2].sem, sp_stored[i % 2].after(l, i // 2 * 16))
                V.tensor_copy(SP[:, i % 2], PS[:, 0, T:T + P]).then_inc(spc_ready.sem, 1)
                if i + 2 < PAIRS:
                    masked_a(l, i + 2)
                if i + 1 < PAIRS:
                    weigh(i + 1)
                dve.wait_ge(y2_ready.sem, y2_ready.after(l, i + 1))
                if i:
                    dve.wait_ge(ydone.sem, ydone.after(l, i))
                V.tensor_tensor(Y2[:, P:T], PS[:, 1, P:T], EC[:, i % 2, P:T], ALU.mult).then_inc(ystep.sem, 1)
                dve.wait_ge(spc_ready.sem, spc_ready.after(l, i + 1))
                V.scalar_tensor_tensor(SP[:, i % 2], SP[:, i % 2], EC[:, i % 2, SEQ - 1:SEQ], PS[:, 1, 0:P],
                                       ALU.mult, ALU.add).then_inc(spn_ready.sem, 1)
                dve.wait_ge(ystep.sem, ystep.after(l, 2 * i + 2))
                V.tensor_tensor(XC[:, i, P:T], XC[:, i, P:T], Y2[:, P:T], ALU.add).then_inc(ydone.sem, 1)
                dve.wait_ge(supd_ready.sem, supd_ready.after(l, i + 1))
                s = SIN[i % 3]
                for b in range(NB):
                    e = SEQ + SL * b + SL - 1
                    q = V.scalar_tensor_tensor(s[:, b], s[:, b], EC[:, i % 2, e:e + 1], PS[:, 2 + b // 4, (b % 4) * P:(b % 4 + 1) * P],
                                               ALU.mult, ALU.add)
                q.then_inc(ssm_new.sem, 1)
            dve.wait_ge(z_ready.sem, z_ready.after(l, 4))
            dve.wait_ge(ydone.sem, ydone.after(l, PAIRS))
            for g in range(2):
                V.tensor_tensor(Z[:, 4 * g:4 * g + 4], XC[:, 4 * g:4 * g + 4], Z[:, 4 * g:4 * g + 4], ALU.mult).then_inc(yz_ready.sem, 1)
            split_lo(l, unit(U_OUT + 2))
            split_lo(l, unit(U_OUT + 3))
            dve.wait_ge(sroot_ready.sem, sroot_ready.after(l, 2))
            V.reciprocal(SQS[:, 0:2], SQS[:, 0:2]).then_inc(srinv_ready.sem, 1)
            dve.wait_ge(srinv_ready.sem, srinv_ready.after(l, 1))
            for k in range(PAIRS):
                V.scalar_tensor_tensor(Z[:, k], Z[:, k], col(C_SSN + k), SQS[:, k // 4], ALU.mult, ALU.mult).then_inc(ysn_ready.sem, 1)
            for c in range(4):
                dve.wait_ge(yh_ready.sem, yh_ready.after(l, c + 1))
                V.tensor_tensor(HL[:, 8 + 2 * c:10 + 2 * c, :], Z[:, 2 * c:2 * c + 2], HH[:, 8 + 2 * c:10 + 2 * c, :].bitcast(F32),
                                ALU.subtract).then_inc(yl_ready.sem, 1)
            with dve.Fori(0, 2) as i:
                split_lo(l, unit(U_OUT + 4, i))
                split_lo(l, unit(U_OUT + 5, i))
            split_lo(l, unit(U_OUT + 8))

        with dve.Fori(0, LAYERS) as l:
            V.tensor_copy(PAR[:].rearrange("p (o c) -> p o c", o=1), PALL[:, ds(l, 1), :]).then_inc(par_ready.sem, 1)
            dve.wait_ge(par_ready.sem, par_ready.after(l, 1))
            for c in range(4):
                pre_gain(l, 0, c)
            pre_rinv(l, 0)
            split_lo(l, unit(1))
            ffn(l, 0, U_UP1, U_DOWN1)
            post_norm(l, 0, U_DOWN1 + 10)
            pre_norm(l)
            for c in range(8):
                split_lo(l, ahead(unit(U_IN + c)))
                if c == 0:
                    dt_first(l)
                if c == 3:
                    dt_rest(l)
                if c == 5:
                    decays(l, 0)
            for g in range(2):
                hgrn(l, g)
            mamba(l)
            post_norm(l, 1, U_OUT + 7, then=pre_gain)
            pre_rinv(l, 2)
            ffn(l, 1, U_UP2, U_DOWN2)
            post_norm(l, 2, U_DOWN2 + 10)

    @block.tensor
    def _(pe):
        pe.wait_ge(consts_done.sem, 1)
        pe.wait_ge(x_rows_in.sem, 32)
        for n, (t0, tn) in enumerate(TILES):
            for k in range(DT_):
                c = (k % 4) * P
                q = pe.transpose(PS[:, 2 * n + k // 4, c:c + tn], XROW[0:tn, n, k * P:(k + 1) * P], IDENT[0:tn, 0:tn])
            q.then_inc(x_turned.sem, 1)
        pe.wait_ge(params_in.sem, 16 * 12)
        for l in range(LAYERS):
            pe.transpose(PS[:, 6, l * NROW_A:(l + 1) * NROW_A], PROWA[:, l, :], IDENT[0:NROW_A, 0:NROW_A])
            q = pe.transpose(PS[:, 7, l * 48:(l + 1) * 48], PROWB[:, l, :], IDENT[0:48, 0:48])
        q.then_inc(params_turned.sem, 1)
        pe.wait_ge(x_ready.sem, x_ready.before)
        for _ in range(2):
            pe.matmul(PS[:, 5, 0:8], ONES[:], ONES[:, 0:8], start=True, stop=True).then_inc(unit_done.sem, 1)

        def dense(out, slot, c, hi, lo, first, last_):
            wh, wl = WH[:, slot, c:c + P], WL[:, slot, c:c + P]
            pe.matmul(out, wh, hi, start=first, stop=False)
            pe.matmul(out, wh, lo, start=False, stop=False)
            return pe.matmul(out, wl, hi, start=False, stop=last_)

        def by_columns(l, u, banks, arriving=None):
            slot, n, _ = u
            pe.wait_ge(lo_ready.sem, lo_ready.after(l, n) + 1)
            for s, b in enumerate(banks):

                for k in range(DT_):
                    if arriving is not None and s == 0 and k % 2 == 0:
                        pe.wait_ge(xl_ready.sem, xl_ready.after(l, 4 * arriving + k // 2 + 1))
                    q = dense(PS[:, b, 0:T], slot, k * 256 + s * P, XH[:, k], XL[:, k], k == 0, k == DT_ - 1)
            q.then_inc(unit_done.sem, 1)

        def by_rows(l, u, k, first=False, last_=False):
            slot, n, _ = u
            pe.wait_ge(lo_ready.sem, lo_ready.after(l, n) + 1)
            for kk in range(2):
                hi, lo = ((HH[:, k + kk, :], HL[:, k + kk, :]) if isinstance(k, int) else
                          (HH[:, ds(k + kk, 1), :].rearrange("p o t -> p (o t)"), HL[:, ds(k + kk, 1), :].rearrange("p o t -> p (o t)")))
                for m in range(DT_):
                    q = dense(PS[:, m, 0:T], slot, kk * D + m * P, hi, lo, first and kk == 0, last_ and kk == 1)
            q.then_inc(unit_done.sem, 1)

        def stat(l, n, sem, per_tile, bank=0):
            for k in range(DT_):
                if k % 2 == 0:
                    pe.wait_ge(sem.sem, sem.after(l, per_tile + k // 2 + 1))
                q = pe.matmul(PS[:, bank, 0:T], ONES[:], SQ[:, k], start=(k == 0), stop=(k == DT_ - 1))
            q.then_inc(stat_ready.sem, 1)

        def ffn(l, f, up, down):
            with pe.Fori(0, 5) as i:
                pe.wait_ge(xl_ready.sem, xl_ready.after(l, 8 * f + 4))
                for s in range(2):
                    pe.wait_ge(h_ready.sem, h_ready.after(l, i * 2 + (11 * f + s)) + (1 - 2))
                    by_columns(l, unit(up + 2 * s, i, 4), (4 * s, 4 * s + 1))
                    if s:
                        pe.wait_ge(root_ready.sem, root_ready.after(l, 4 * f + 1))
                    by_columns(l, unit(up + 2 * s + 1, i, 4), (4 * s + 2, 4 * s + 3))
            pe.wait_ge(h_ready.sem, h_ready.after(l, 11 * f + 9))
            by_columns(l, unit(up + 20), (0, 1))
            by_columns(l, unit(up + 21), (2, 3))
            pe.wait_ge(h_ready.sem, h_ready.after(l, 11 * f + 11))
            pe.wait_ge(hl_ready.sem, hl_ready.after(l, 11 * f + 10))
            by_rows(l, unit(down), 0, first=True)
            with pe.Fori(0, 4) as i:
                by_rows(l, unit(down + 1, i), i * 4 + 2)
                by_rows(l, unit(down + 2, i), i * 4 + 4)
            by_rows(l, unit(down + 9), 18)
            pe.wait_ge(hl_ready.sem, hl_ready.after(l, 11 * f + 11))
            by_rows(l, unit(down + 10), 20, last_=True)
            stat(l, 2 * f, postsq_ready, 8 * f)

        def scores(l, g, i):
            b = 3 * (i % 2)
            lhs, rhs = (PROJ[g][1][:], PROJ[g][2][:]) if i == 0 else (W[:, i % 2], W[:, i % 2])
            for h in range(HG):
                for n, (t0, tn) in enumerate(TILES if i < 4 else TILES[:2]):
                    q = pe.matmul(PS[0:tn, b + n, h * tn:(h + 1) * tn], lhs[:, h, t0:t0 + tn], rhs[:, h, t0:t0 + tn],
                                  start=True, stop=True)
            q.then_inc(score_ready.sem, 1)

        def turn(src, n, bank, sem):
            t0, tn = TILES[n]
            for h in range(HG):
                q = pe.transpose(PS[0:tn, bank, h * KD:(h + 1) * KD], src[:, h, t0:t0 + tn], IDENT[:])
            q.then_inc(sem.sem, 1)

        def first_heads(l):
            for c in range(8):
                if c == 3:
                    pe.wait_ge(dt_step.sem, dt_step.after(l, 2))
                if c in (4, 5):
                    pe.wait_ge(fsig_ready.sem, fsig_ready.after(l, 2 * (c - 3)))
                if c in (6, 7):
                    pe.wait_ge(q_ready.sem, q_ready.after(l, c - 5))
                by_columns(l, unit(U_IN + c), (2 * (c % 4), 2 * (c % 4) + 1), arriving=1 if c == 0 else None)
                if c == 0:
                    pe.wait_ge(wdt_in.sem, wdt_in.after(l, 16))
                    for n, (t0, tn) in enumerate(TILES):
                        for k in range(DT_):
                            q = pe.matmul(PS[0:tn, 7, n * MH:(n + 1) * MH], XN[:, k, t0:t0 + tn], WDT[:, k],
                                          start=(k == 0), stop=(k == DT_ - 1))
                    q.then_inc(dtp_ready.sem, 1)

        def evacuated(l, u):
            return ((fsig_ready, 6), (fsig_ready, 8), (q_ready, 3), (q_ready, 4), (v_ready, 3), (v_ready, 4), (go_ready, 3),
                    (go_ready, 4), *((xb_ready, 2 * j + 2) for j in range(6)))[u]

        def hgrn(l, g):
            def beside(place):
                for j in BESIDE[g][place]:
                    u = 8 * g + j
                    if u:
                        s, n = evacuated(l, u - 1)
                        pe.wait_ge(s.sem, s.after(l, n))

                    by_columns(l, unit(U_IN + 8 + u), (6, 7))

            pe.wait_ge(v_ready.sem, v_ready.after(l, g * 2 + 2))
            if g == 0:
                pe.wait_ge(go_ready.sem, go_ready.after(l, 2))
            if g:
                pe.wait_ge(gor_ready.sem, gor_ready.after(l, 2 * g))
            for j, n in enumerate(TURNS):
                if j == 2:
                    pe.wait_ge(vtok_ready.sem, vtok_ready.after(l, g * 3 + 1))
                turn(PROJ[g][3][:], n, 4 + j % 2, vturn_ready)
            pe.wait_ge(fk_ready.sem, fk_ready.after(l, g * 8 + 8))
            pe.wait_ge(q_ready.sem, q_ready.after(l, g * 2 + 2))
            pe.wait_ge(ohg_ready.sem, ohg_ready.after(l, g * 4))
            scores(l, g, 0)
            for i in range(1, 8):
                pe.wait_ge(w_ready.sem, w_ready.after(l, g * 16 + 2 * i))
                if i == 1:
                    pe.wait_ge(vtok_ready.sem, vtok_ready.after(l, g * 3 + 3))
                else:
                    pe.wait_ge(picked.sem, picked.after(l, g * 8 + i - 1))
                if g == 1 and i == 7:
                    pe.wait_ge(crow_in.sem, crow_in.after(l, 16))
                scores(l, g, i)
                if i < 7:
                    beside(i)
            if g == 1:
                for c in range(3):
                    q = pe.transpose(PS[:, 5, c * 96:(c + 1) * 96], CROW[:, c * P:(c + 1) * P], IDENT[0:96, 0:96])
                q.then_inc(cturn_ready.sem, 1)
            beside(7)
            pe.wait_ge(w_ready.sem, w_ready.after(l, g * 16 + 16))
            for j, n in enumerate(TURNS):
                if j == 2:
                    pe.wait_ge(ktok_ready.sem, ktok_ready.after(l, g * 3 + 1))
                turn(W[:, 1], n, j % 2, kturn_ready)
            pe.wait_ge(picked.sem, picked.after(l, g * 8 + 8))
            for n, s in enumerate((sp1_ready, sp2_ready)):
                pe.wait_ge(ktok_ready.sem, ktok_ready.after(l, g * 3 + 2 * n + 1))
                if g == 1:
                    pe.wait_ge(pads_ready.sem, pads_ready.after(l, 3))
                for h in range(HG):
                    c = slice(h * KD, (h + 1) * KD)
                    q = pe.matmul(PS[:, 4 + n, c], KTOK[:, n, c], VTOK[:, n, c], start=True, stop=True)
                q.then_inc(s.sem, 1)
            pe.wait_ge(s1_ready.sem, s1_ready.after(l, g + 1))
            for h in range(HG):
                c = slice(h * KD, (h + 1) * KD)
                s = h % 3
                pe.wait_ge(hs_in[s].sem, hs_in[s].after(l, 16 * (g * SLOT_HEADS[s] + h // 3 + 1)))
                pe.matmul(PS[:, h, 0:P], VTOK[:, 0, c], APR[:, 0, h], start=True, stop=True)
                pe.matmul(PS[:, h, P:SEQ], VTOK[:, 1, c], APR[:, 1, h], start=True, stop=False, skip_group_check=True)
                pe.matmul(PS[:, h, P:SEQ], S1[:, h], W[:, 0, h, P:SEQ], start=False, stop=True, skip_group_check=True)
                pe.matmul(PS[:, h, SEQ:T], VTOK[0:NS, 2, c], ASM[:, h], start=True, stop=False, skip_group_check=True)
                for b in range(NB):
                    t = SEQ + SL * b
                    q = pe.matmul(PS[:, h, t:t + SL], HSIN[g][s][:, b], W[:, 0, h, t:t + SL], start=False, stop=(b == NB - 1),
                                  skip_group_check=True)
                q.then_inc(o_ready.sem, 1)
                pe.wait_ge(vm_ready.sem, vm_ready.after(l, g * 4 + h + 1))
                if h:
                    pe.wait_ge(snew_ready.sem, snew_ready.after(l, g * 4 + h))
                else:
                    pe.wait_ge(s2_ready.sem, s2_ready.after(l, g + 1))
                for b in range(2):
                    q = pe.matmul(PS[:, 4 + b, :], KTOK[0:NS, 2, c], VM[:, 4 * b:4 * b + 4, :].rearrange("p b v -> p (b v)"),
                                  start=True, stop=True)
                q.then_inc(upd_ready.sem, 1)
                beside(8 + h)
            pe.wait_ge(snew_ready.sem, snew_ready.after(l, g * 4 + 4))

            pe.wait_ge(sqo_ready.sem, sqo_ready.after(l, g * 4 + 4))
            for h in range(HG):
                q = pe.matmul(PS[32 * h:32 * h + 32, 4, 0:T], ONES[:, 0:32], SQO[:, h], start=True, stop=True)
            q.then_inc(ostat_ready.sem, 1)
            beside(12)
            if g == 1:
                pe.wait_ge(xb_ready.sem, xb_ready.after(l, 12))
                by_columns(l, unit(U_IN + 22), (6, 7))
            pe.wait_ge(orinv_ready.sem, orinv_ready.after(l, g + 1))
            for j in range(2):
                if j:
                    pe.wait_ge(gor_ready.sem, gor_ready.after(l, g * 2 + 1))
                for s in range(2):
                    q = pe.matmul(PS[:, 4 + s, 0:T], SEL[:, 2 * j + s], RTO[:], start=True, stop=True)
                q.then_inc(obc_ready.sem, 1)

        def mamba(l):
            for j in range(1, 4):
                b = 6 - 2 * (j % 2)
                if j == 1:
                    pe.wait_ge(gor_ready.sem, gor_ready.after(l, 4))
                else:
                    pe.wait_ge(z_ready.sem, z_ready.after(l, j - 1))
                by_columns(l, unit(U_IN + 22 + j), (b, b + 1))
            pe.wait_ge(ohg_ready.sem, ohg_ready.after(l, 8))
            pe.wait_ge(dt_step.sem, dt_step.after(l, 20))
            for n, (t0, tn) in enumerate(TILES):
                u = USTR if n < 2 else USTR8
                q = pe.matmul(PS[0:tn, 1, n * MH:(n + 1) * MH], u[:], AT[0:tn, n, :], start=True, stop=True)
            q.then_inc(remp_ready.sem, 1)

            def segment_sums(i):
                pe.wait_ge(l1_ready.sem, l1_ready.after(l, 2 * i + 2))
                if i:
                    pe.wait_ge(e_ready.sem, e_ready.after(l, 3 * i))
                for h in range(2):
                    for n in range(2):
                        pe.matmul(PS[:, 4, (2 * n + h) * P:(2 * n + h + 1) * P], L1[:, n, h], TRI[:], start=True, stop=True)
                    pe.matmul(PS[0:NS, 5, h * NS:(h + 1) * NS], L1S[:, h], TRI8[:], start=True, stop=True)
                for n, (t0, tn) in enumerate(TILES):
                    tri = TRI if n < 2 else TRI8
                    for h in range(2):
                        q = pe.matmul(PS[HD * h:HD * h + HD, 5, P + t0:P + t0 + tn],
                                      AT[0:tn, n, 2 * i + h:2 * i + h + 1].broadcast_to([tn, HD]), tri[:], start=True, stop=True)
                q.then_inc(seg_ready.sem, 1)

            pe.wait_ge(z_ready.sem, z_ready.after(l, 4))
            segment_sums(0)
            pe.wait_ge(xc_ready.sem, xc_ready.after(l, 6))
            pe.wait_ge(z_ready.sem, z_ready.after(l, 4))
            pe.wait_ge(rem_ready.sem, rem_ready.after(l, 2))
            for j, n in enumerate(TURNS):
                t0, tn = TILES[n]
                b, bb = (3, 5) if j == 1 else (0, 2)
                if j == 0:
                    pe.wait_ge(e_ready.sem, e_ready.after(l, 3))
                if j == 2:
                    pe.wait_ge(dtx_ready.sem, dtx_ready.after(l, 1))
                    pe.wait_ge(btok_ready.sem, btok_ready.after(l, 1))
                    pe.wait_ge(gm_ready.sem, gm_ready.after(l, 1))
                for k in range(10):
                    c = (k % 4) * P
                    q = pe.transpose(PS[0:tn, (b + k // 4) if k < 8 else bb, c:c + P], XC[:, k, t0:t0 + tn], IDENT[:])
                q.then_inc(xturn_ready.sem, 1)
                for g in range(2):
                    q = pe.matmul(PS[0:tn, 6 + j % 2, g * P:g * P + tn], XC[:, 8 + g, t0:t0 + tn], XC[:, 10 + g, t0:t0 + tn],
                                  start=True, stop=True)
                q.then_inc(g_ready.sem, 1)
            pe.wait_ge(wx_ready.sem, wx_ready.after(l, 1))
            pe.wait_ge(dtx_ready.sem, dtx_ready.after(l, 3))
            for g in range(2):
                q = pe.matmul(PS[:, g, :], BTOK[:, 0, g * P:(g + 1) * P], WX[:, 0, g * 512:(g + 1) * 512], start=True, stop=True)
            q.then_inc(ht1p_ready.sem, 1)
            pe.wait_ge(gm_ready.sem, gm_ready.after(l, 3))
            pe.wait_ge(btok_ready.sem, btok_ready.after(l, 3))
            pe.wait_ge(cs_ready.sem, cs_ready.after(l, 2))
            for c in range(CT):
                q = pe.transpose(PS[0:27, 5 + c // 4, (c % 4) * P:(c % 4 + 1) * P], CS[:, c, :], IDENT[:])
            q.then_inc(csturn_ready.sem, 1)
            pe.wait_ge(co_ready.sem, co_ready.after(l, 1))
            pe.wait_ge(wx_ready.sem, wx_ready.after(l, 3))

            for i in range(PAIRS):
                g = i // 4
                cc = slice(i * P, (i + 1) * P)
                pe.wait_ge(st_ready.sem, st_ready.after(l, 2 * i + 2))
                if i:
                    pe.wait_ge(spc_ready.sem, spc_ready.after(l, i))
                else:
                    pe.wait_ge(ht1_ready.sem, ht1_ready.after(l, 1))
                for h in range(2):
                    for n, (t0, tn) in enumerate(TILES):
                        c = (2 * i + h) * HD
                        pe.matmul(PS[HD * h:HD * h + HD, 0, t0:t0 + tn], DTX[0:tn, n, c:c + HD],
                                  ST[:, n, h] if n < 2 else STS[:, h], start=True, stop=True)
                pe.matmul(PS[:, 0, T:T + P], WX[:, 0, cc], BTOK[:, 0, g * P:(g + 1) * P], start=True, stop=True
                          ).then_inc(y_ready.sem, 1)
                pe.wait_ge(ms_in[i % 3].sem, ms_in[i % 3].after(l, (i // 3 + 1) * 16))
                if i:
                    pe.wait_ge(hts_ready.sem, hts_ready.after(l, i))
                for b in range(NB):
                    q = pe.transpose(PS[:, 6 + b // 4, (b % 4) * P:(b % 4 + 1) * P], SIN[i % 3][:, b], IDENT[:])
                q.then_inc(hts_turned.sem, 1)
                if i + 1 < PAIRS:
                    segment_sums(i + 1)
                pe.wait_ge(hts_ready.sem, hts_ready.after(l, i + 1))
                if i:
                    pe.wait_ge(spn_ready.sem, spn_ready.after(l, i))
                pe.matmul(PS[:, 1, P:SEQ], HT1[:, cc], XC[:, 10 + g, P:SEQ], start=True, stop=True)
                for b in range(NB):
                    t = SEQ + SL * b
                    pe.matmul(PS[:, 1, t:t + SL], HTS[:, b], XC[:, 10 + g, t:t + SL], start=True, stop=True)
                pe.matmul(PS[:, 1, 0:P], WX[:, 1, cc], BTOK[:, 1, g * P:(g + 1) * P], start=True, stop=True
                          ).then_inc(y2_ready.sem, 1)
                pe.wait_ge(bmk_ready.sem, bmk_ready.after(l, g + 1))
                if i:
                    pe.wait_ge(ssm_new.sem, ssm_new.after(l, i))
                for b in range(2):
                    q = pe.matmul(PS[:, 2 + b, :], WX[0:NS, 2, cc], BMK[:, 4 * b:4 * b + 4, :].rearrange("p b n -> p (b n)"),
                                  start=True, stop=True)
                q.then_inc(supd_ready.sem, 1)
            pe.wait_ge(ohl_ready.sem, ohl_ready.after(l, 2))
            pe.wait_ge(ssm_new.sem, ssm_new.after(l, PAIRS))
            by_rows(l, unit(U_OUT), 0, first=True)
            by_rows(l, unit(U_OUT + 1), 2)
            pe.wait_ge(sqs_ready.sem, sqs_ready.after(l, 2))
            for g in range(2):
                for b, t, n in SPARE:
                    for k in range(4):
                        q = pe.matmul(PS[:, b + 4 * g, T:T + n], ONES[:], SQS[:, 4 * g + k, t:t + n], start=False, stop=(k == 3),
                                      skip_group_check=True)
            q.then_inc(sstat_ready.sem, 1)
            pe.wait_ge(sroot_ready.sem, sroot_ready.after(l, 2))
            by_rows(l, unit(U_OUT + 2), 4)
            by_rows(l, unit(U_OUT + 3), 6)
            for j in range(4):
                pe.wait_ge(yl_ready.sem, yl_ready.after(l, j + 1))
                by_rows(l, unit(U_OUT + 4 + j), 8 + 2 * j, last_=(j == 3))
            stat(l, 1, postsq_ready, 4)

        with pe.Fori(0, LAYERS) as l:
            pe.wait_ge(par_ready.sem, par_ready.after(l, 1))
            stat(l, 0, presq_ready, 0, bank=7)
            ffn(l, 0, U_UP1, U_DOWN1)
            stat(l, 1, presq_ready, 4)
            first_heads(l)
            for g in range(2):
                hgrn(l, g)
            mamba(l)
            stat(l, 2, presq_ready, 8, bank=7)
            ffn(l, 1, U_UP2, U_DOWN2)
        for k in range(DT_):
            if k % 2 == 0:
                pe.wait_ge(x_ready.sem, x_ready.after(LAYERS, 0) - 3 + k // 2)
            for n, (t0, tn) in enumerate(TILES):
                q = pe.transpose(PS[0:tn, 2 * n + k // 4, (k % 4) * P:(k % 4 + 1) * P], X[:, k, t0:t0 + tn], IDENT[:])
                if k == DT_ - 1:
                    q.then_inc(yout_turned.sem, 1)


_INS = ("x_prompt", "x_sample", "state_hgrn", "state_ssm", "state_conv", "w_in", "hg_lb_logits", "conv_w", "conv_b",
        "dt_bias", "a_log", "d_skip", "hg_norm_w", "ssm_norm_w", "w_out", "ffn1_w_gate", "ffn1_w_up", "ffn1_w_down",
        "ffn2_w_gate", "ffn2_w_up", "ffn2_w_down", "norm_gain")
_OUTS = (("y_prompt", (1, SEQ, D)), ("y_sample", (NB, SL, D)),
         ("hgrn_prompt", (LAYERS, 1, HH_, KD, KD)), ("ssm_prompt", (LAYERS, 1, MH, HD, P)),
         ("conv_prompt", (LAYERS, 1, CW - 1, CT * P)), ("hgrn_sample", (LAYERS, NB, HH_, KD, KD)),
         ("ssm_sample", (LAYERS, NB, MH, HD, P)), ("conv_sample", (LAYERS, NB, CW - 1, CT * P)))


def kernel(**inputs):
    import numpy as np
    import concourse.bacc as bacc
    from concourse.bass_utils import run_bass_kernel_spmd

    nc = bacc.Bacc("TRN2", target_bir_lowering=False, num_devices=1)
    arrays = {name: np.ascontiguousarray(inputs[name]) for name in _INS}
    a = {name: nc.dram_tensor(name, v.shape, F32, kind="ExternalInput").ap() for name, v in arrays.items()}
    o = {name: nc.dram_tensor(name, shape, F32, kind="ExternalOutput").ap() for name, shape in _OUTS}
    trunk(nc, a, o)
    r = run_bass_kernel_spmd(nc, [arrays], core_ids=[0])
    return tuple(r.results[0][name] for name, _ in _OUTS)
```
